# Optimizing a Trainium2 kernel written in Bass

```python
import math
import jax, jax.numpy as jnp
from jax import lax
import numpy as np

D_MODEL = 1024
BATCH = 1
SEQ = 1024
DEPTH = 1

CHUNK = 64
Q_BLOCK = 128
EPS = 1e-6
CONV_CH = D_MODEL
CONV_WIDTH = 31
MLA_HEADS = 8
QK_NOPE = 128
QK_ROPE = 64
V_DIM = 128
Q_LORA = D_MODEL // 4
KV_LORA = D_MODEL // 4
ROPE_THETA = 10000.0
PEER_HEADS = 8
PEER_KEYS = 128
PEER_EXPERTS = PEER_KEYS * PEER_KEYS
PEER_QDIM = 256
PEER_TOPK = 16
TOKEN_BLOCK = 128
IN_SIZES = (CONV_CH, CONV_CH, Q_LORA, KV_LORA, QK_ROPE, D_MODEL, D_MODEL)
IN_COLS = sum(IN_SIZES)
IN_SPLITS = [int(i) for i in np.cumsum(IN_SIZES)[:-1]]

kernel_name = "hybrid_conformer_mla_peer_block"

def rms_norm(x, g):
    xf = x.astype(jnp.float32)
    y = xf * lax.rsqrt(jnp.mean(xf * xf, axis=-1, keepdims=True) + EPS)
    return (y * g.astype(jnp.float32)).astype(x.dtype)

def layer_norm(x, g, b):
    xf = x.astype(jnp.float32)
    mu = jnp.mean(xf, axis=-1, keepdims=True)
    var = jnp.mean(jnp.square(xf - mu), axis=-1, keepdims=True)
    y = (xf - mu) * lax.rsqrt(var + EPS)
    return (y * g.astype(jnp.float32) + b.astype(jnp.float32)).astype(x.dtype)

def rope_tables(seq, dim):
    pos = jnp.arange(seq, dtype=jnp.float32)
    inv_freq = ROPE_THETA ** (-jnp.arange(0, dim, 2, dtype=jnp.float32) / dim)
    ang = pos[:, None] * inv_freq[None, :]
    return jnp.cos(ang), jnp.sin(ang)

def apply_rope(x, cos, sin):
    half = x.shape[-1] // 2
    xf = x.astype(jnp.float32)
    x1, x2 = xf[..., :half], xf[..., half:]
    c = cos[None, :, None, :]
    s = sin[None, :, None, :]
    return jnp.concatenate([x1 * c - x2 * s, x1 * s + x2 * c], axis=-1).astype(x.dtype)

def conformer_conv_branch(a, b, dw, dw_b, ln_g, ln_b, w_pw):
    u = a * jax.nn.sigmoid(b)
    y = lax.conv_general_dilated(
        u, dw[:, None, :], window_strides=(1,), padding=[(CONV_WIDTH - 1, 0)],
        dimension_numbers=("NWC", "WIO", "NWC"), feature_group_count=CONV_CH) + dw_b
    y = jax.nn.silu(layer_norm(y, ln_g, ln_b))
    return y @ w_pw

def mla_branch(q_c, c_kv, k_rope, q_norm_g, w_q_up, kv_norm_g, w_kv_up, w_o):
    B, S, _ = q_c.shape
    q = (rms_norm(q_c, q_norm_g) @ w_q_up).reshape(B, S, MLA_HEADS, QK_NOPE + QK_ROPE)
    kv = (rms_norm(c_kv, kv_norm_g) @ w_kv_up).reshape(B, S, MLA_HEADS, QK_NOPE + V_DIM)
    cos, sin = rope_tables(S, QK_ROPE)
    q = jnp.concatenate([q[..., :QK_NOPE], apply_rope(q[..., QK_NOPE:], cos, sin)], axis=-1)
    kr = apply_rope(k_rope[:, :, None, :], cos, sin)
    k = jnp.concatenate([kv[..., :QK_NOPE], jnp.broadcast_to(kr, (B, S, MLA_HEADS, QK_ROPE))], axis=-1)
    v = kv[..., QK_NOPE:]
    scale = 1.0 / math.sqrt(QK_NOPE + QK_ROPE)
    chunk_id = jnp.arange(S) // CHUNK
    outs = []
    for i in range(S // Q_BLOCK):
        q0, q1 = i * Q_BLOCK, (i + 1) * Q_BLOCK
        s = jnp.einsum("bqhd,bkhd->bhqk", q[:, q0:q1], k[:, :q1]).astype(jnp.float32) * scale
        mask = chunk_id[q0:q1, None] >= chunk_id[None, :q1]
        p = jax.nn.softmax(jnp.where(mask, s, -jnp.inf), axis=-1).astype(v.dtype)
        outs.append(jnp.einsum("bhqk,bkhd->bqhd", p, v[:, :q1]))
    o = jnp.concatenate(outs, axis=1).reshape(B, S, MLA_HEADS * V_DIM)
    return o @ w_o

def peer_ffn(xn, w_q, sub_keys, u_tab, v_tab):
    B, S, D = xn.shape
    blocks = xn.reshape(B * S // TOKEN_BLOCK, TOKEN_BLOCK, D)
    n_cand = PEER_TOPK * PEER_TOPK

    def block_fn(xb):
        q = (xb @ w_q).reshape(TOKEN_BLOCK, PEER_HEADS, 2, PEER_QDIM // 2)
        sc = jnp.einsum("thcd,hckd->thck", q, sub_keys).astype(jnp.float32)
        s1, i1 = lax.top_k(sc[:, :, 0], PEER_TOPK)
        s2, i2 = lax.top_k(sc[:, :, 1], PEER_TOPK)
        cand = (s1[..., :, None] + s2[..., None, :]).reshape(TOKEN_BLOCK, PEER_HEADS, n_cand)
        cand_idx = (i1[..., :, None] * PEER_KEYS + i2[..., None, :]).reshape(TOKEN_BLOCK, PEER_HEADS, n_cand)
        top_s, pos = lax.top_k(cand, PEER_TOPK)
        idx = jnp.take_along_axis(cand_idx, pos, axis=-1)
        g = jax.nn.softmax(top_s, axis=-1).astype(xb.dtype)
        u_sel = jnp.take(u_tab, idx, axis=0)
        act = jax.nn.gelu(jnp.einsum("thkd,td->thk", u_sel, xb)) * g
        v_sel = jnp.take(v_tab, idx, axis=0)
        return jnp.einsum("thk,thkd->td", act, v_sel)

    return lax.map(block_fn, blocks).reshape(B, S, D)

def hybrid_layer(x, norm_mix_g, w_in, b_gate, conv_dw, conv_dw_b, conv_ln_g, conv_ln_b,
                 conv_w_pw, q_norm_g, w_q_up, kv_norm_g, w_kv_up, mla_w_o, w_out,
                 norm_ffn_g, peer_w_q, peer_sub_keys, peer_u, peer_v):
    n = rms_norm(x, norm_mix_g)
    z = n @ w_in
    glu_a, glu_b, q_c, c_kv, k_rope, gate_c, gate_m = jnp.split(z, IN_SPLITS, axis=-1)
    y_conv = conformer_conv_branch(glu_a, glu_b, conv_dw, conv_dw_b, conv_ln_g, conv_ln_b, conv_w_pw)
    y_mla = mla_branch(q_c, c_kv, k_rope, q_norm_g, w_q_up, kv_norm_g, w_kv_up, mla_w_o)
    merged = jax.nn.sigmoid(gate_c + b_gate[0]) * y_conv + jax.nn.sigmoid(gate_m + b_gate[1]) * y_mla
    h = x + merged @ w_out
    return h + peer_ffn(rms_norm(h, norm_ffn_g), peer_w_q, peer_sub_keys, peer_u, peer_v)

def setup_inputs(seed: int = 0) -> dict:
    key = jax.random.key(seed)
    ks = jax.random.split(key, 24)

    def nrm(k, shape, scale):
        return jax.random.normal(k, shape, dtype=jnp.float32) * scale

    def gain(k, shape):
        return 1.0 + nrm(k, shape, 0.02)

    L = DEPTH
    return {
        "x": nrm(ks[0], (BATCH, SEQ, D_MODEL), 1.0),
        "norm_mix_g": gain(ks[1], (L, D_MODEL)),
        "w_in": nrm(ks[2], (L, D_MODEL, IN_COLS), D_MODEL ** -0.5),
        "b_gate": nrm(ks[3], (L, 2, D_MODEL), 0.02),
        "conv_dw": nrm(ks[4], (L, CONV_WIDTH, CONV_CH), CONV_WIDTH ** -0.5),
        "conv_dw_b": nrm(ks[5], (L, CONV_CH), 0.02),
        "conv_ln_g": gain(ks[6], (L, CONV_CH)),
        "conv_ln_b": nrm(ks[7], (L, CONV_CH), 0.02),
        "conv_w_pw": nrm(ks[8], (L, CONV_CH, D_MODEL), CONV_CH ** -0.5),
        "q_norm_g": gain(ks[9], (L, Q_LORA)),
        "w_q_up": nrm(ks[10], (L, Q_LORA, MLA_HEADS * (QK_NOPE + QK_ROPE)), Q_LORA ** -0.5),
        "kv_norm_g": gain(ks[11], (L, KV_LORA)),
        "w_kv_up": nrm(ks[12], (L, KV_LORA, MLA_HEADS * (QK_NOPE + V_DIM)), KV_LORA ** -0.5),
        "mla_w_o": nrm(ks[13], (L, MLA_HEADS * V_DIM, D_MODEL), (MLA_HEADS * V_DIM) ** -0.5),
        "w_out": nrm(ks[14], (L, D_MODEL, D_MODEL), D_MODEL ** -0.5),
        "norm_ffn_g": gain(ks[15], (L, D_MODEL)),
        "peer_w_q": nrm(ks[16], (L, D_MODEL, PEER_HEADS * PEER_QDIM), D_MODEL ** -0.5),
        "peer_sub_keys": nrm(ks[17], (L, PEER_HEADS, 2, PEER_KEYS, PEER_QDIM // 2), (PEER_QDIM // 2) ** -0.5),
        "peer_u": nrm(ks[18], (L, PEER_EXPERTS, D_MODEL), D_MODEL ** -0.5),
        "peer_v": nrm(ks[19], (L, PEER_EXPERTS, D_MODEL), D_MODEL ** -0.5),
        "norm_final_g": gain(ks[20], (D_MODEL,)),
    }

def reference(x, norm_mix_g, w_in, b_gate, conv_dw, conv_dw_b, conv_ln_g, conv_ln_b,
              conv_w_pw, q_norm_g, w_q_up, kv_norm_g, w_kv_up, mla_w_o, w_out,
              norm_ffn_g, peer_w_q, peer_sub_keys, peer_u, peer_v, norm_final_g):
    h = x
    for l in range(DEPTH):
        h = hybrid_layer(h, norm_mix_g[l], w_in[l], b_gate[l], conv_dw[l], conv_dw_b[l],
                         conv_ln_g[l], conv_ln_b[l], conv_w_pw[l], q_norm_g[l], w_q_up[l],
                         kv_norm_g[l], w_kv_up[l], mla_w_o[l], w_out[l], norm_ffn_g[l],
                         peer_w_q[l], peer_sub_keys[l], peer_u[l], peer_v[l])
    return rms_norm(h, norm_final_g)


_drawn_inputs = setup_inputs


def setup_inputs(seed=0):
    import zlib

    import numpy as np

    out = dict(_drawn_inputs(seed))
    spreads = {}
    factors = {'norm_mix_g': 6.937,
     'b_gate': 8.0,
     'conv_dw_b': 4.627,
     'conv_ln_g': 7.296,
     'conv_ln_b': 8.0,
     'q_norm_g': 8.0,
     'kv_norm_g': 8.0,
     'norm_ffn_g': 8.0,
     'peer_w_q': 3.954,
     'peer_sub_keys': 3.959,
     'peer_u': 4.358,
     'peer_v': 3.944,
     'norm_final_g': 2.951}
    for name, (base, spread) in spreads.items():
        noise = np.random.default_rng([zlib.crc32(name.encode()), seed]).standard_normal(out[name].shape)
        drawn = base * np.exp(spread * noise) if base else spread * noise
        out[name] = __import__('jax').numpy.asarray(drawn.astype(out[name].dtype))
    for name, factor in factors.items():
        out[name] = (out[name] * factor).astype(out[name].dtype)
    return out
```

```python
import math

import numpy as np

P = 128
D = 1024
T = 1024
KC = D // P
HALF = 512
TAPS = 31
HEADS = 8
NOPE, ROPE, VDIM = 128, 64, 128
LORA = 256
LC = LORA // P
QT = T // P
CHUNK = 64
KEYS = 128
TOPK = 16
EXPERT_TILES = 128
EPS = 1e-6
SCALE = 1.0 / math.sqrt(NOPE + ROPE)
THETA = 10000.0

W_LATENT = 0
W_GLU = 5
W_CONVOUT = W_GLU + 16
W_MLAOUT = W_CONVOUT + 16
W_OUT = W_MLAOUT + 16
W_ROUTER = W_OUT + 8
W_JOBS = W_ROUTER + 16

J_NORM_X = 0
J_LATENT = 1
J_NORM_Q = 6
J_NORM_KV = 7
J_GLU = 8
J_HEAD = J_GLU + 16
J_LN_MEAN = J_HEAD + 32
J_LN_VAR = J_LN_MEAN + 1
J_CONVOUT = J_LN_VAR + 1
J_MLAOUT = J_CONVOUT + 16
J_OUT = J_MLAOUT + 16
J_NORM_H = J_OUT + 8
J_ROUTER = J_NORM_H + 1
J_SEL = J_ROUTER + 32
J_G = J_SEL + 3
G_TOK = 8
G_BATCH = 64
G_BLOCKS = T // G_BATCH
J_EXP = J_G + T // G_TOK
GROUP = 2
GROUPS = EXPERT_TILES // GROUP
STEP_JOBS = GROUP + KC
J_NORM_OUT = J_EXP + GROUPS * STEP_JOBS

V_GMIX, V_BC, V_BM, V_DWB, V_LNG, V_LNB, V_QG, V_KG, V_GFFN, V_GFIN = 0, 8, 16, 24, 32, 40, 48, 50, 52, 60
V_DW = 68
V_COLS = V_DW + KC * TAPS


def build(nc, xT, wproj, whead, keysT, uT, vtab, vecs, tables, rotary, outT):
    import concourse.bass as bass
    from concourse import mybir

    f32, f32r, u32 = mybir.dt.float32, mybir.dt.float32r, mybir.dt.uint32
    ALU, ACT, AX = mybir.AluOpType, mybir.ActivationFunctionType, mybir.AxisListType
    mm = nc.tensor.matmul

    base = (nc.sbuf_base + 31) // 32 * 32

    def at(name, shape, kib, dt=f32):
        return nc.alloc_sbuf_tensor_at(name, shape, dt, offset=base + int(kib * 1024))

    act = at("act", [P, KC, T], 0)
    region_a = at("region_a", [P, KC, T], 32)
    region_b = at("region_b", [P, KC, T], 64)
    merged = at("merged", [P, KC, T], 96)
    q_nope = at("q_nope", [P, T], 96)
    q_rope = at("q_rope", [ROPE, T], 100)
    k_nope = at("k_nope", [P, T], 104)
    v_head = at("v_head", [P, QT, VDIM], 108)
    probs = at("probs", [P, 2, T], 112)
    probsT = at("probsT", [P, 2, QT, P], 120)
    wring = at("wring", [P, 4, KC, P], 128)
    latent = at("latent", [P, 4, T], 144)
    k_rope = at("k_rope", [ROPE, T], 160)
    rot = at("rot", [P, T], 164)
    rstd = at("rstd", [P, T], 168)
    squares = at("squares", [P, 2, T], 172)
    gate = at("gate", [P, 2, T], 180)
    glu = at("glu", [P, 2, TAPS - 1 + T], 188)
    hwring = at("hwring", [P, LC, 512], 196.5)
    tabs = at("tabs", [P, 3, P], 200.5)
    vec = at("vec", [P, V_COLS], 202)
    negmax = at("negmax", [P, 2], 203.5)
    expsum = at("expsum", [P, 2], 203.625)
    spare = at("spare", [P, 32], 203.75)
    ones, ident, iota = tabs[:, 0, :], tabs[:, 1, :], tabs[:, 2, :]
    x_hi = at("x_hi", [P, KC, T], 32, f32r)
    x_lo = at("x_lo", [P, KC, T], 64, f32r)
    wq_hi = at("wq_hi", [P, 2, KC, P], 96, f32r)
    wq_lo = at("wq_lo", [P, 2, KC, P], 104, f32r)
    query = at("query", [P, 2, T], 112)
    keys = at("keys", [P, 16, KEYS], 120)
    best = at("best", [P, 2, QT, TOPK], 144)
    best_key = at("best_key", [P, 2, QT, TOPK], 145, u32)
    best_keyf = at("best_keyf", [P, 2, QT, TOPK], 146)
    rest = at("rest", [P, QT, KEYS], 148)
    cand = at("cand", [P, QT, TOPK, TOPK], 152)
    cand_rest = at("cand_rest", [P, QT, TOPK, TOPK], 160)
    pick = at("pick", [P, QT, TOPK, TOPK], 172)
    top = at("top", [P, QT, TOPK], 180)
    top_pos = at("top_pos", [P, QT, TOPK], 180.5, u32)
    pos_a = at("pos_a", [P, QT, TOPK], 181, u32)
    pos_b = at("pos_b", [P, QT, TOPK], 181.5, u32)
    pos_af = at("pos_af", [P, QT, TOPK], 182)
    pos_bf = at("pos_bf", [P, QT, TOPK], 182.5)
    shifted = at("shifted", [P, QT, TOPK], 183)
    weight = at("weight", [P, QT, TOPK], 183.5)
    wsum = at("wsum", [P, 2, QT], 184)
    sel = at("sel", [P, 3, QT, P], 188)
    selT = at("selT", [P, 3, T], 96)
    hot2 = at("hot2", [P, 2, G_TOK, P], 108)
    hot1 = at("hot1", [P, 2, G_TOK, P], 116)
    gblock = at("gblock", [P, 2, P, G_BATCH], 124)
    a_hi = at("a_hi", [P, 2, GROUP, T], 96, f32r)
    a_lo = at("a_lo", [P, 2, GROUP, T], 112, f32r)
    v_hi = at("v_hi", [P, GROUP, D], 128, f32r)
    v_lo = at("v_lo", [P, GROUP, D], 136, f32r)
    v_raw = at("v_raw", [P, 2, D], 144)
    u_raw = at("u_raw", [P, 2, KC, P], 152)
    u_hi = at("u_hi", [P, 2, KC, P], 160, f32r)
    u_lo = at("u_lo", [P, 2, KC, P], 168, f32r)
    g_raw = at("g_raw", [P, 2, G_BLOCKS, GROUP * G_BATCH], 176)
    hidden = at("hidden", [P, 2, T], 192)

    g_dram = nc.dram_tensor("g_dram", [G_BLOCKS, P, P * G_BATCH], f32).ap()
    ps = nc.alloc_psum_tensor("ps", [P, 4, T], f32)

    names = dict(
        consts_in=1, x_in=4, x_again=1, w_in=4, hw_in=1, keys_in=1, u_in=2, v_in=2, g_in=2, g_out=2, y_out=1,
        job_done=1, slot_free=4,
        sq_ready=1, sq_used=1, var_ready=1, rstd_ready=1, act_ready=1,
        lat_normed=1, krope_ready=1,
        gate_used=1, conv_ready=1,
        s_ready=1, max_ready=1, exp_ready=1, p_ready=1, pt_ready=1, pt_copied=1, pv_done=1, o_ready=1, o_copied=1,
        centred=1, ln_ready=1, silu_ready=1, merged_ready=1, h_ready=1,
        xn_ready=1, xhi_ready=1, xlo_ready=1, wq_hi_ready=1, wq_split=1,
        shifted_ready=1, weight_exp=1, sel_ready=1, selT_ready=1, hot_ready=1, 
        a_ready=1, a_hi_ready=1, a_split=1, u_hi_ready=1, u_split=1, v_hi_ready=1, v_split=1,
        final_ready=1, dve_step=1)
    S = {}
    for name, n in names.items():
        made = [nc.alloc_semaphore(f"{name}{k}" if n > 1 else name) for k in range(n)]
        S[name] = made if n > 1 else made[0]
    job_done, slot_free = S["job_done"], S["slot_free"]

    def wait_job(eng, j):
        eng.wait_ge(job_done, j + 1)

    def wait_slot(eng, j, rounds=0):
        eng.wait_ge(slot_free[j % 4], rounds + j // 4)

    def wait_read(eng, j, rounds=0):
        eng.wait_ge(slot_free[j % 4], rounds + (j // 4 + 1))

    def flat(ap):
        return ap.rearrange("p a b -> p (a b)")

    block_cm = nc.Block()
    block = block_cm.__enter__()

    @block.sync
    def _(sp):
        sp.dma_start(vec[:], vecs).then_inc(S["consts_in"], 16)
        sp.dma_start(tabs[:], tables).then_inc(S["consts_in"], 16)
        sp.dma_start(rot[:], rotary).then_inc(S["consts_in"], 16)
        for k in range(4):
            sp.dma_start(region_a[:, 2 * k:2 * k + 2, :], xT[:, 2 * k:2 * k + 2, :]).then_inc(S["x_in"][k], 16)
            sp.dma_start(flat(wring[:, k]), wproj[k]).then_inc(S["w_in"][k], 16)

        def load_w(w, i=0):
            sp.dma_start(flat(wring[:, w % 4]), wproj[i * 4 + w]).then_inc(S["w_in"][w % 4], 16)

        for w in range(4, 9):
            wait_job(sp, J_LATENT + w - 4)
            load_w(w)
        with sp.Fori(0, 3) as i:
            for w in range(W_GLU + 4, W_GLU + 8):
                wait_job(sp, i * 4 + (J_GLU + w - 4 - W_GLU))
                load_w(w, i)
        sp.dma_start(flat(hwring[:]), whead[0]).then_inc(S["hw_in"], 16)
        for w in range(W_CONVOUT, W_CONVOUT + 4):
            wait_job(sp, J_GLU + w - 4 - W_GLU)
            load_w(w)
        with sp.Fori(1, HEADS) as h:
            wait_job(sp, h * 4 + (J_HEAD - 1))
            sp.dma_start(flat(hwring[:]), whead[h]).then_inc(S["hw_in"], 16)
        later = J_CONVOUT - W_CONVOUT
        with sp.Fori(0, 4) as i:
            for w in range(W_CONVOUT + 4, W_CONVOUT + 8):
                wait_job(sp, i * 4 + (w - 4 + later))
                load_w(w, i)
        sp.dma_start(region_b[:], xT).then_inc(S["x_again"], 16)
        with sp.Fori(0, 6) as i:
            for w in range(W_CONVOUT + 20, W_CONVOUT + 24):
                wait_job(sp, i * 4 + (w - 4 + later))
                load_w(w, i)
        wait_job(sp, J_NORM_H - 1)
        sp.dma_start(keys[:], keysT).then_inc(S["keys_in"], 16)
        with sp.Fori(0, 3) as i:
            for k in range(4):
                sp.wait_ge(S["wq_split"], i * 4 + k + 1)
                load_w(W_ROUTER + 4 + k, i)

        with sp.Fori(0, G_BLOCKS // 2) as i:
            for k in range(2):
                wait_read(sp, J_G + 8 * k + 7, i * 4)
                sp.dma_start(g_dram[i * 2 + k], gblock[:, k].rearrange("p a t -> p (a t)")).then_inc(S["g_out"][k], 16)
        for k in range(2):
            sp.wait_ge(S["g_out"][k], 16 * G_BLOCKS // 2)

        def load_u(e, k):
            sp.dma_start(flat(u_raw[:, k]), uT[e]).then_inc(S["u_in"][k], 16)

        def load_v(e, k):
            sp.dma_start(v_raw[:, k], vtab[e]).then_inc(S["v_in"][k], 16)

        def load_g(g, k):
            cols = g_dram.rearrange("b p (g c) -> g p b c", c=GROUP * G_BATCH)
            sp.dma_start(g_raw[:, k], cols[g]).then_inc(S["g_in"][k], 16)

        def expert_loads(s, k, more_u=True, more_g=True):
            for n in range(GROUP):
                if not (isinstance(s, int) and s == 0 and k == 0):
                    sp.wait_ge(S["v_split"], s * 4 + 2 * k - 1 + n)
                load_v(s * 4 + (2 * k + n), n)
            if more_g:
                if not (isinstance(s, int) and s == 0 and k == 0):
                    sp.wait_ge(S["a_ready"], s * 4 + 2 * k)
                load_g(s * 2 + (k + 1), (k + 1) % 2)
            if more_u:
                for n in range(GROUP):
                    sp.wait_ge(S["u_split"], s * 4 + 2 * k + 3 + n)
                    load_u(s * 4 + (2 * k + 4 + n), n)

        load_u(0, 0)
        load_u(1, 1)
        load_g(0, 0)
        for n in range(GROUP):
            sp.wait_ge(S["u_split"], n + 1)
            load_u(2 + n, n)
        expert_loads(0, 0)
        expert_loads(0, 1)
        with sp.Fori(1, GROUPS // 2 - 1) as s:
            expert_loads(s, 0)
            expert_loads(s, 1)
        expert_loads(GROUPS // 2 - 1, 0, more_u=False)
        expert_loads(GROUPS // 2 - 1, 1, more_u=False, more_g=False)

        for c in range(KC):
            sp.wait_ge(S["final_ready"], c + 1)
            sp.dma_start(outT[:, c, :], act[:, c, :]).then_inc(S["y_out"], 16)
        sp.wait_ge(S["y_out"], 16 * KC)

    @block.tensor
    def _(pe):
        used = {"sq": 0}

        def project(j, w, acts, i):
            wait_slot(pe, j, i)
            pe.wait_ge(S["w_in"][w % 4], i * 16 + (w // 4 + 1) * 16)
            for half in range(2):
                cols = slice(half * HALF, (half + 1) * HALF)
                for c in range(KC):
                    last = mm(ps[:, j % 4, cols], wring[:, w % 4, c, :], acts[:, c, cols],
                              start=c == 0, stop=c == KC - 1)
            last.then_inc(job_done, 1)

        def ones_sum(j, tiles):
            if j >= 4:
                wait_slot(pe, j)
            for n, (sem, value, tile, after) in enumerate(tiles):
                pe.wait_ge(sem, value)
                for half in range(2):
                    cols = slice(half * HALF, (half + 1) * HALF)
                    last = mm(ps[:, j % 4, cols], ones, tile[:, cols], start=n == 0, stop=n == len(tiles) - 1,
                              skip_group_check=True)
                if after is not None:
                    last.then_inc(after, 1)
            if tiles[-1][3] is None:
                last.then_inc(job_done, 1)
            else:
                pe.wait_ge(tiles[-1][3], used["sq"])
                pe.nop().then_inc(job_done, 1)

        def square_tiles(n):
            first = used["sq"]
            used["sq"] += n
            return [(S["sq_ready"], k + 1, squares[:, k % 2, :], S["sq_used"]) for k in range(first, first + n)]

        pe.wait_ge(S["consts_in"], 48)
        ones_sum(J_NORM_X, square_tiles(KC))
        for k in range(5):
            j, w = J_LATENT + k, W_LATENT + k
            if j >= 4:
                wait_slot(pe, j)
            pe.wait_ge(S["w_in"][w % 4], (w // 4 + 1) * 16)
            for half in range(2):
                cols = slice(half * HALF, (half + 1) * HALF)
                for c in range(KC):
                    if k == 0 and half == 0:
                        pe.wait_ge(S["act_ready"], c + 1)
                    last = mm(ps[:, j % 4, cols], wring[:, w % 4, c, :], act[:, c, cols],
                              start=c == 0, stop=c == KC - 1)
            last.then_inc(job_done, 1)
        ones_sum(J_NORM_Q, square_tiles(LC))
        ones_sum(J_NORM_KV, square_tiles(LC))

        with pe.Fori(0, 4) as i:
            for k in range(4):
                project(J_GLU + k, W_GLU + k, act, i)

        pe.wait_ge(S["lat_normed"], 4)
        pe.wait_ge(S["krope_ready"], 1)
        with pe.Fori(0, HEADS) as h:
            pe.wait_ge(S["hw_in"], h * 16 + 16)
            for k, (first, tile) in enumerate(((0, 0), (128, 0), (256, 2))):
                j = J_HEAD + k
                wait_slot(pe, j, h)
                for half in range(2):
                    cols = slice(half * HALF, (half + 1) * HALF)
                    for c in range(LC):
                        last = mm(ps[:, j % 4, cols], hwring[:, c, first:first + P], latent[:, tile + c, cols],
                                  start=c == 0, stop=c == LC - 1)
                last.then_inc(job_done, 1)
            j = J_HEAD + 3
            wait_slot(pe, j, h)
            pe.wait_ge(S["o_copied"], h + 1)
            for t in range(QT):
                for c in range(LC):
                    last = mm(ps[:, j % 4, t * P:(t + 1) * P], latent[:, 2 + c, t * P:(t + 1) * P],
                              hwring[:, c, 384:512], start=c == 0, stop=c == LC - 1)
            last.then_inc(job_done, 1)
            for k in range(3):
                wait_read(pe, J_HEAD + k, h)

            def scores(i):
                rows = slice(i * P, (i + 1) * P)
                width = (i + 1) * P
                for c0 in range(0, width, HALF):
                    cols = slice(c0, min(width, c0 + HALF))
                    mm(ps[:, i % 2, cols], q_nope[:, rows], k_nope[:, cols], start=True, stop=False)
                    last = mm(ps[:, i % 2, cols], q_rope[:, rows], k_rope[:, cols], start=False, stop=True)
                last.then_inc(S["s_ready"], 1)

            def transposes(i):
                pe.wait_ge(S["p_ready"], h * QT + i + 1)
                pe.wait_ge(S["pt_copied"], h * QT + i + 1)
                for b in range(i + 1):
                    last = nc.tensor.transpose(ps[:, 2, b * P:(b + 1) * P], probs[:, i % 2, b * P:(b + 1) * P], ident)
                last.then_inc(S["pt_ready"], 1)

            def values(i):
                pe.wait_ge(S["pt_copied"], h * QT + i + 2)
                for b in range(i + 1):
                    last = mm(ps[:, 3, i * P:(i + 1) * P], v_head[:, b, :], probsT[:, i % 2, b, :],
                              start=b == 0, stop=b == i)
                last.then_inc(S["pv_done"], 1)

            scores(0)
            scores(1)
            transposes(0)
            scores(2)
            wait_read(pe, J_HEAD + 3, h)
            values(0)
            for i in range(1, QT):
                transposes(i)
                if i + 2 < QT:
                    scores(i + 2)
                values(i)

        ones_sum(J_LN_MEAN, [(S["conv_ready"], c + 1, region_b[:, c, :], None) for c in range(KC)])
        ones_sum(J_LN_VAR, square_tiles(KC))

        def gated_branch(j0, w0, branch, ready, n):
            with pe.Fori(0, 4) as i:
                for k in range(4):
                    if k == 1:
                        pe.wait_ge(ready, n)
                    project(j0 + k, w0 + k, branch if k % 2 else act, i)

        gated_branch(J_CONVOUT, W_CONVOUT, region_b, S["silu_ready"], KC)
        gated_branch(J_MLAOUT, W_MLAOUT, region_a, S["o_copied"], HEADS + 1)
        pe.wait_ge(S["merged_ready"], KC)
        with pe.Fori(0, 2) as i:
            for k in range(4):
                project(J_OUT + k, W_OUT + k, merged, i)
        ones_sum(J_NORM_H, square_tiles(KC))

        def three_passes(out, hi, lo, m_hi, m_lo, first, last_one):
            mm(out, hi, m_hi, start=first, stop=False)
            mm(out, hi, m_lo, start=False, stop=False)
            return mm(out, lo, m_hi, start=False, stop=last_one)

        pe.wait_ge(S["xlo_ready"], KC)
        pe.wait_ge(S["keys_in"], 16)
        with pe.Fori(0, HEADS) as i:
            for k in range(2):
                j = J_ROUTER + 2 * k
                wait_slot(pe, j, i)
                pe.wait_ge(S["wq_split"], i * 2 + k + 1)
                for half in range(2):
                    cols = slice(half * HALF, (half + 1) * HALF)
                    for c in range(KC):
                        last = three_passes(ps[:, j % 4, cols], wq_hi[:, k, c, :], wq_lo[:, k, c, :],
                                            x_hi[:, c, cols], x_lo[:, c, cols], c == 0, c == KC - 1)
                last.then_inc(job_done, 1)
                j += 1
                wait_slot(pe, j, i)
                wait_read(pe, j - 1, i)
                for t in range(QT):
                    last = mm(ps[:, j % 4, t * P:(t + 1) * P], query[:, k, t * P:(t + 1) * P],
                              keys[:, bass.ds(i * 2 + k, 1), :].rearrange("p a k -> p (a k)"), start=True, stop=True)
                last.then_inc(job_done, 1)
        pe.wait_ge(S["sel_ready"], HEADS)
        for n in range(3):
            j = J_SEL + n
            wait_slot(pe, j)
            for t in range(QT):
                last = nc.tensor.transpose(ps[:, j % 4, t * P:(t + 1) * P], sel[:, n, t, :], ident)
            last.then_inc(job_done, 1)

        with pe.Fori(0, T // G_TOK // 4) as i:
            for k in range(4):
                j = J_G + k
                wait_slot(pe, j, i)
                pe.wait_ge(S["hot_ready"], i * 4 + k + 1)
                for t in range(G_TOK):
                    last = mm(ps[:, j % 4, t * P:(t + 1) * P], hot2[:, k % 2, t, :], hot1[:, k % 2, t, :],
                              start=True, stop=True)
                last.then_inc(job_done, 1)

        def hidden_job(j, s, e):
            wait_slot(pe, j, s * 5)
            for half in range(2):
                cols = slice(half * HALF, (half + 1) * HALF)
                for c in range(KC):
                    last = three_passes(ps[:, j % 4, cols], u_hi[:, e, c, :], u_lo[:, e, c, :],
                                        x_hi[:, c, cols], x_lo[:, c, cols], c == 0, c == KC - 1)
            last.then_inc(job_done, 1)

        def value_job(j, s, slot, c):
            wait_slot(pe, j, s * 5)
            for half in range(2):
                cols = slice(half * HALF, (half + 1) * HALF)
                for n in range(GROUP):
                    feats = slice(c * P, (c + 1) * P)
                    last = three_passes(ps[:, j % 4, cols], v_hi[:, n, feats], v_lo[:, n, feats],
                                        a_hi[:, slot, n, cols], a_lo[:, slot, n, cols], n == 0, n == GROUP - 1)
            last.then_inc(job_done, 1)

        def expert_step(s, k, has_next=True):
            j = J_EXP + GROUP + STEP_JOBS * k
            if has_next:
                for n in range(GROUP):
                    pe.wait_ge(S["u_split"], s * 4 + 2 * k + 3 + n)
                    hidden_job(j + n, s, n)
                j += GROUP
            pe.wait_ge(S["v_split"], s * 4 + 2 * k + 2)
            pe.wait_ge(S["a_split"], s * 4 + 2 * k + 2)
            for c in range(KC):
                value_job(j + c, s, k, c)

        for n in range(GROUP):
            pe.wait_ge(S["u_split"], n + 1)
            hidden_job(J_EXP + n, 0, n)
        with pe.Fori(0, GROUPS // 2 - 1) as s:
            expert_step(s, 0)
            expert_step(s, 1)
        expert_step(GROUPS // 2 - 1, 0)
        expert_step(GROUPS // 2 - 1, 1, has_next=False)
        ones_sum(J_NORM_OUT, square_tiles(KC))

    @block.scalar
    def _(sc):
        fn = nc.scalar.activation
        count = {"sq": 0, "rstd": 0}

        def square(tile):
            n = count["sq"]
            count["sq"] += 1
            if n >= 2:
                sc.wait_ge(S["sq_used"], n - 1)
            fn(squares[:, n % 2, :], tile, ACT.Square).then_inc(S["sq_ready"], 1)

        def root():
            count["rstd"] += 1
            sc.wait_ge(S["var_ready"], count["rstd"])
            fn(rstd[:], rstd[:], ACT.Sqrt).then_inc(S["rstd_ready"], 1)

        for c in range(KC):
            if c % 2 == 0:
                sc.wait_ge(S["x_in"][c // 2], 16)
            square(region_a[:, c, :])
        root()
        sc.wait_ge(S["consts_in"], 48)
        for k in range(4):
            j = J_LATENT + k
            wait_job(sc, j)
            square(ps[:, j % 4, :])
            fn(latent[:, k, :], ps[:, j % 4, :], ACT.Copy).then_inc(slot_free[j % 4], 1)
        root()
        root()
        with sc.Fori(0, 4) as i:
            for n in range(2):
                j = J_GLU + 2 * n
                wait_job(sc, i * 4 + j)
                sc.wait_ge(S["gate_used"], i * 2 + n + 1)
                fn(gate[:, n, :], ps[:, j % 4, :], ACT.Sigmoid).then_inc(slot_free[j % 4], 1)

        sc.nop().then_inc(S["o_copied"], 1)
        sc.nop().then_inc(S["pt_copied"], 1)
        with sc.Fori(0, HEADS) as h:
            wait_job(sc, h * 4 + J_HEAD)
            fn(q_nope[:], ps[:, 0, :], ACT.Copy, scale=SCALE).then_inc(slot_free[0], 1)
            wait_job(sc, h * 4 + (J_HEAD + 2))
            fn(k_nope[:], ps[:, 2, :], ACT.Copy).then_inc(slot_free[2], 1)
            wait_job(sc, h * 4 + (J_HEAD + 3))
            fn(v_head[:].rearrange("p t v -> p (t v)"), ps[:, 3, :], ACT.Copy).then_inc(slot_free[3], 1)

            def exps(i):
                sc.wait_ge(S["max_ready"], h * QT + i + 1)
                if i >= 2:
                    sc.wait_ge(S["pt_ready"], h * QT + i - 1)
                width = (i + 1) * P
                fn(probs[:, i % 2, 0:width], ps[:, i % 2, 0:width], ACT.Exp, bias=negmax[:, i % 2:i % 2 + 1],
                   accum_out=expsum[:, i % 2:i % 2 + 1]).then_inc(S["exp_ready"], 1)

            def copy_probsT(i):
                sc.wait_ge(S["pt_ready"], h * QT + i + 1)
                if i >= 2:
                    sc.wait_ge(S["pv_done"], h * QT + i - 1)
                width = (i + 1) * P
                fn(probsT[:, i % 2, 0:i + 1, :].rearrange("p b k -> p (b k)"), ps[:, 2, 0:width],
                   ACT.Copy).then_inc(S["pt_copied"], 1)

            exps(0)
            for i in range(QT):
                if i + 1 < QT:
                    exps(i + 1)
                copy_probsT(i)
            sc.wait_ge(S["pv_done"], h * QT + QT)
            fn(region_a[:, bass.ds(h, 1), :].rearrange("p a t -> p (a t)"), ps[:, 3, :],
               ACT.Copy).then_inc(S["o_copied"], 1)

        for c in range(KC):
            sc.wait_ge(S["centred"], c + 1)
            square(region_b[:, c, :])
        root()
        for c in range(KC):
            sc.wait_ge(S["ln_ready"], c + 1)
            fn(region_b[:, c, :], region_b[:, c, :], ACT.Silu, scale=vec[:, V_LNG + c:V_LNG + c + 1],
               bias=vec[:, V_LNB + c:V_LNB + c + 1]).then_inc(S["silu_ready"], 1)
        for phase, (j0, bias) in enumerate(((J_CONVOUT, V_BC), (J_MLAOUT, V_BM))):
            with sc.Fori(0, 4) as i:
                for n in range(2):
                    j = j0 + 2 * n
                    wait_job(sc, i * 4 + j)
                    sc.wait_ge(S["gate_used"], i * 2 + (8 * (phase + 1) + n + 1))
                    fn(gate[:, n, :], ps[:, j % 4, :], ACT.Sigmoid,
                       bias=vec[:, bass.ds(i * 2 + (bias + n), 1)]).then_inc(slot_free[j % 4], 1)
        for c in range(KC):
            sc.wait_ge(S["h_ready"], c + 1)
            square(act[:, c, :])
        root()

        for c in range(KC):
            sc.wait_ge(S["xn_ready"], c + 1)
            fn(x_hi[:, c, :], gate[:, c % 2, :], ACT.Copy).then_inc(S["xhi_ready"], 1)

        def split_wq(n, i=0):
            w = W_ROUTER + n
            sc.wait_ge(S["w_in"][w % 4], i * 16 + (w // 4 + 1) * 16)
            fn(flat(wq_hi[:, n % 2]), flat(wring[:, w % 4]), ACT.Copy).then_inc(S["wq_hi_ready"], 1)

        def copy_query(n, i=0):
            j = J_ROUTER + 2 * n
            wait_job(sc, i * 8 + j)
            fn(query[:, n % 2, :], ps[:, j % 4, :], ACT.Copy).then_inc(slot_free[j % 4], 1)

        def head_weights(h):
            sc.wait_ge(S["shifted_ready"], h + 1)
            fn(weight[:], shifted[:], ACT.Exp).then_inc(S["weight_exp"], 1)

        split_wq(0)
        split_wq(1)
        with sc.Fori(0, 3) as i:
            for n in range(4):
                copy_query(n, i)
                split_wq(n + 2, i)
                if n % 2:
                    head_weights(i * 2 + n // 2)
        for n in range(4):
            copy_query(12 + n)
            if n < 2:
                split_wq(14 + n)
            if n % 2:
                head_weights(6 + n // 2)
        for n in range(3):
            j = J_SEL + n
            wait_job(sc, j)
            fn(selT[:, n, :], ps[:, j % 4, :], ACT.Copy).then_inc(slot_free[j % 4], 1)
        def g_block(b, i=0, first=False):
            if not first:
                sc.wait_ge(S["g_out"][b], i * 16)
            for k in range(8):
                j = J_G + 8 * b + k
                wait_job(sc, i * 16 + j)
                tok = slice(G_TOK * k, G_TOK * (k + 1))
                fn(gblock[:, b, :, tok].rearrange("p a t -> p t a"),
                   ps[:, j % 4, :].rearrange("p (t a) -> p t a", a=P), ACT.Copy).then_inc(slot_free[j % 4], 1)

        for b in range(2):
            g_block(b, first=True)
        with sc.Fori(1, G_BLOCKS // 2) as i:
            for b in range(2):
                g_block(b, i)

        def u_hi_copy(e, k, s=0):
            sc.wait_ge(S["u_in"][k], s * 32 + (e // 2 + 1) * 16)
            fn(flat(u_hi[:, k]), flat(u_raw[:, k]), ACT.Copy).then_inc(S["u_hi_ready"], 1)

        def gelu(j, s, e, first=False):
            wait_job(sc, s * 20 + j)
            if not first:
                sc.wait_ge(S["a_split"], s * 4 + e - 1)
            fn(hidden[:, e % 2, :], ps[:, j % 4, :], ACT.Gelu_apprx_tanh).then_inc(slot_free[j % 4], 1)

        def a_hi_copy(s, e, slot):
            sc.wait_ge(S["a_ready"], s * 4 + e + 1)
            fn(a_hi[:, slot, e % 2, :], hidden[:, e % 2, :], ACT.Copy).then_inc(S["a_hi_ready"], 1)

        def v_hi_copy(s, e):
            sc.wait_ge(S["v_in"][e % 2], s * 32 + (e // 2 + 1) * 16)
            fn(v_hi[:, e % 2, :], v_raw[:, e % 2, :], ACT.Copy).then_inc(S["v_hi_ready"], 1)

        def expert_step(s, k, has_next=True, more_u=True):
            if not (isinstance(s, int) and s == 0 and k == 0):
                wait_job(sc, s * 20 + (J_EXP + GROUP + STEP_JOBS * k - 1))
            for n in range(GROUP):
                v_hi_copy(s, 2 * k + n)
            if has_next:
                j = J_EXP + GROUP + STEP_JOBS * k
                for n in range(GROUP):
                    gelu(j + n, s, 2 * k + 2 + n)
                    if more_u:
                        u_hi_copy(2 * k + 4 + n, n, s)
                for n in range(GROUP):
                    a_hi_copy(s, 2 * k + 2 + n, (k + 1) % 2)

        u_hi_copy(0, 0)
        u_hi_copy(1, 1)
        for n in range(GROUP):
            gelu(J_EXP + n, 0, n, first=True)
            u_hi_copy(2 + n, n)
        for n in range(GROUP):
            a_hi_copy(0, n, 0)
        expert_step(0, 0)
        expert_step(0, 1)
        with sc.Fori(1, GROUPS // 2 - 1) as s:
            expert_step(s, 0)
            expert_step(s, 1)
        expert_step(GROUPS // 2 - 1, 0, more_u=False)
        expert_step(GROUPS // 2 - 1, 1, has_next=False)
        for c in range(KC):
            wait_read(sc, J_NORM_OUT - KC + c)
            square(act[:, c, :])
        root()

    @block.gpsimd
    def _(pool):
        with pool.Fori(0, 4) as i:
            for k in range(4):
                pool.wait_ge(S["wq_hi_ready"], i * 4 + k + 1)
                w = W_ROUTER + k
                nc.gpsimd.tensor_tensor(flat(wq_lo[:, k % 2]), flat(wring[:, w % 4]), flat(wq_hi[:, k % 2]),
                                        ALU.subtract).then_inc(S["wq_split"], 1)

    @block.vector
    def _(v):
        dv = nc.vector
        step = S["dve_step"]
        chain = {"base": 0, "n": 0}

        def link(ins):
            ins.then_inc(step, 1)
            chain["n"] += 1
            v.wait_ge(step, chain["base"] + chain["n"])

        def enter_loop(i, per):
            chain["base"] = i * per
            return chain["n"] + per

        def leave_loop(end, per, rounds):
            assert chain["n"] == end, (chain["n"], end)
            chain["base"] = 0
            chain["n"] += per * (rounds - 1)

        count = {"norm": 0}

        def rstd_of(j, width):
            wait_job(v, j)
            dv.tensor_scalar(rstd[:], ps[:, j % 4, :], 1.0 / width, EPS, ALU.mult, ALU.add).then_inc(slot_free[j % 4], 1)
            wait_read(v, j)
            dv.reciprocal(rstd[:], rstd[:]).then_inc(S["var_ready"], 1)
            count["norm"] += 1
            v.wait_ge(S["rstd_ready"], count["norm"])

        v.wait_ge(S["consts_in"], 48)
        link(dv.memset(glu[:, :, 0:TAPS - 1], 0.0))
        for k in range(4):
            v.wait_ge(S["x_in"][k], 16)
        rstd_of(J_NORM_X, D)
        for c in range(KC):
            dv.scalar_tensor_tensor(act[:, c, :], region_a[:, c, :], vec[:, V_GMIX + c:V_GMIX + c + 1], rstd[:],
                                    ALU.mult, ALU.mult).then_inc(S["act_ready"], 1)
        j = J_LATENT + 4
        wait_job(v, j)
        dv.tensor_tensor(gate[0:ROPE, 0, :], ps[0:ROPE, j % 4, :], rot[0:ROPE, :], ALU.mult)
        dv.tensor_tensor(gate[0:ROPE, 1, :], ps[ROPE:P, j % 4, :], rot[ROPE:P, :], ALU.mult).then_inc(slot_free[j % 4], 1)
        wait_read(v, j)
        dv.tensor_tensor(k_rope[:], gate[0:ROPE, 0, :], gate[0:ROPE, 1, :], ALU.add).then_inc(S["krope_ready"], 1)
        v.wait_ge(S["krope_ready"], 1)
        v.nop().then_inc(S["gate_used"], 1)
        v.nop().then_inc(S["gate_used"], 1)
        for lat, (j, g) in enumerate(((J_NORM_Q, V_QG), (J_NORM_KV, V_KG))):
            rstd_of(j, LORA)
            for c in range(LC):
                dv.scalar_tensor_tensor(latent[:, 2 * lat + c, :], latent[:, 2 * lat + c, :], vec[:, g + c:g + c + 1],
                                        rstd[:], ALU.mult, ALU.mult).then_inc(S["lat_normed"], 1)
            v.wait_ge(S["lat_normed"], 2 * lat + 2)

        with v.Fori(0, 4) as i:
            end = enter_loop(i, 2 * TAPS)
            for n in range(2):
                j = J_GLU + 2 * n + 1
                wait_job(v, i * 4 + j)
                wait_read(v, j - 1, i)
                dv.tensor_tensor(glu[:, n, TAPS - 1:], ps[:, j % 4, :], gate[:, n, :],
                                 ALU.mult).then_inc(slot_free[j % 4], 1)
                wait_read(v, j, i)
                out = region_b[:, bass.ds(i * 2 + n, 1), :].rearrange("p a t -> p (a t)")

                def tap(k):
                    return vec[:, bass.ds(i * (2 * TAPS) + (V_DW + n * TAPS + k), 1)]

                link(dv.tensor_scalar(out, glu[:, n, 0:T], tap(0), vec[:, bass.ds(i * 2 + (V_DWB + n), 1)],
                                      ALU.mult, ALU.add))
                for k in range(1, TAPS):
                    link(dv.scalar_tensor_tensor(out, glu[:, n, k:k + T], tap(k), out, ALU.mult, ALU.add))
                v.nop().then_inc(S["conv_ready"], 1)
                v.nop().then_inc(S["gate_used"], 1)

        leave_loop(end, 2 * TAPS, 4)

        with v.Fori(0, HEADS) as h:
            end = enter_loop(h, 2 + QT * 2)
            wait_job(v, h * 4 + (J_HEAD + 1))
            dv.scalar_tensor_tensor(gate[0:ROPE, 0, :], ps[0:ROPE, 1, :], SCALE, rot[0:ROPE, :], ALU.mult, ALU.mult)
            link(dv.scalar_tensor_tensor(gate[0:ROPE, 1, :], ps[ROPE:P, 1, :], SCALE, rot[ROPE:P, :],
                                         ALU.mult, ALU.mult))
            link(dv.tensor_tensor(q_rope[:], gate[0:ROPE, 0, :], gate[0:ROPE, 1, :], ALU.add))
            v.nop().then_inc(slot_free[1], 1)

            def row_max(i):
                width = (i + 1) * P
                v.wait_ge(S["s_ready"], h * QT + i + 1)
                link(dv.memset(ps[0:CHUNK, i % 2, width - CHUNK:width], -1e30))
                dv.tensor_reduce(negmax[:, i % 2:i % 2 + 1], ps[:, i % 2, 0:width], AX.X, ALU.max,
                                 negate=True).then_inc(S["max_ready"], 1)

            def normalise(i):
                width = (i + 1) * P
                v.wait_ge(S["exp_ready"], h * QT + i + 1)
                link(dv.reciprocal(expsum[:, i % 2:i % 2 + 1], expsum[:, i % 2:i % 2 + 1]))
                dv.tensor_scalar(probs[:, i % 2, 0:width], probs[:, i % 2, 0:width], expsum[:, i % 2:i % 2 + 1],
                                 None, ALU.mult).then_inc(S["p_ready"], 1)

            row_max(0)
            for i in range(QT):
                if i + 1 < QT:
                    row_max(i + 1)
                normalise(i)

        leave_loop(end, 2 + QT * 2, HEADS)

        wait_job(v, J_LN_MEAN)
        dv.tensor_scalar(gate[:, 0, :], ps[:, J_LN_MEAN % 4, :], 1.0 / D, None,
                         ALU.mult).then_inc(slot_free[J_LN_MEAN % 4], 1)
        wait_read(v, J_LN_MEAN)
        for c in range(KC):
            dv.tensor_tensor(region_b[:, c, :], region_b[:, c, :], gate[:, 0, :], ALU.subtract).then_inc(S["centred"], 1)
        rstd_of(J_LN_VAR, D)
        for c in range(KC):
            dv.tensor_tensor(region_b[:, c, :], region_b[:, c, :], rstd[:], ALU.mult).then_inc(S["ln_ready"], 1)

        with v.Fori(0, 4) as i:
            for n in range(2):
                j = J_CONVOUT + 2 * n + 1
                wait_job(v, i * 4 + j)
                wait_read(v, j - 1, i)
                out = merged[:, bass.ds(i * 2 + n, 1), :].rearrange("p a t -> p (a t)")
                dv.tensor_tensor(out, ps[:, j % 4, :], gate[:, n, :], ALU.mult).then_inc(slot_free[j % 4], 1)
                wait_read(v, j, i)
                v.nop().then_inc(S["gate_used"], 1)
        with v.Fori(0, 4) as i:
            for n in range(2):
                j = J_MLAOUT + 2 * n + 1
                wait_job(v, i * 4 + j)
                wait_read(v, j - 1, i)
                out = merged[:, bass.ds(i * 2 + n, 1), :].rearrange("p a t -> p (a t)")
                dv.tensor_tensor(gate[:, n, :], ps[:, j % 4, :], gate[:, n, :], ALU.mult).then_inc(slot_free[j % 4], 1)
                wait_read(v, j, i)
                dv.tensor_tensor(out, out, gate[:, n, :], ALU.add).then_inc(S["merged_ready"], 1)
                v.wait_ge(S["merged_ready"], i * 2 + n + 1)
                v.nop().then_inc(S["gate_used"], 1)
        v.wait_ge(S["x_again"], 16)
        for c in range(KC):
            j = J_OUT + c
            wait_job(v, j)
            dv.tensor_tensor(act[:, c, :], ps[:, j % 4, :], region_b[:, c, :], ALU.add).then_inc(slot_free[j % 4], 1)
            wait_read(v, j)
            v.nop().then_inc(S["h_ready"], 1)
        rstd_of(J_NORM_H, D)
        for c in range(KC):
            if c >= 2:
                v.wait_ge(S["xhi_ready"], c - 1)
                v.wait_ge(S["xlo_ready"], c - 1)
            dv.scalar_tensor_tensor(gate[:, c % 2, :], act[:, c, :], vec[:, V_GFFN + c:V_GFFN + c + 1], rstd[:],
                                    ALU.mult, ALU.mult).then_inc(S["xn_ready"], 1)
            v.wait_ge(S["xn_ready"], c + 1)
            v.wait_ge(S["xhi_ready"], c + 1)
            dv.tensor_tensor(x_lo[:, c, :], gate[:, c % 2, :], x_hi[:, c, :], ALU.subtract).then_inc(S["xlo_ready"], 1)
        v.wait_ge(S["xlo_ready"], KC)

        def carry_wait():
            carried[0] += 1
            dv.memset(spare[:, carried[0] - 1:carried[0]], 0.0)

        carried = [0]

        def wide(ap, n):
            return ap.unsqueeze(3).to_broadcast([P, QT, TOPK, n])

        def tall(ap, n):
            return ap.unsqueeze(2).to_broadcast([P, QT, n, TOPK])

        iota16 = iota[:, 0:TOPK].unsqueeze(1).unsqueeze(1).to_broadcast([P, QT, TOPK, TOPK])
        with v.Fori(0, HEADS) as h:
            end = enter_loop(h, 25)
            for k in range(2):
                j = J_ROUTER + 2 * k + 1
                wait_job(v, h * 4 + j)
                scores = [ps[:, j % 4, t * P:(t + 1) * P] for t in range(QT)]
                carry_wait()
                for t in range(QT):
                    last = dv.max(best[:, k, t, 0:8], scores[t])
                link(last)
                carry_wait()
                for t in range(QT):
                    dv.max_index(best_key[:, k, t, 0:8], best[:, k, t, 0:8], scores[t])
                for t in range(QT):
                    last = dv.match_replace(rest[:, t, :], best[:, k, t, 0:8], scores[t], -3e38)
                link(last)
                v.nop().then_inc(slot_free[j % 4], 1)
                carry_wait()
                for t in range(QT):
                    last = dv.max(best[:, k, t, 8:16], rest[:, t, :])
                link(last)
                carry_wait()
                for t in range(QT):
                    last = dv.max_index(best_key[:, k, t, 8:16], best[:, k, t, 8:16], rest[:, t, :])
                link(last)
                link(dv.tensor_copy(best_keyf[:, k], best_key[:, k]))
            link(dv.tensor_tensor(cand[:], wide(best[:, 0], TOPK), tall(best[:, 1], TOPK), ALU.add))
            sums = [cand[:, t].rearrange("p a b -> p (a b)") for t in range(QT)]
            sums_rest = [cand_rest[:, t].rearrange("p a b -> p (a b)") for t in range(QT)]
            carry_wait()
            for t in range(QT):
                last = dv.max(top[:, t, 0:8], sums[t])
            link(last)
            carry_wait()
            for t in range(QT):
                dv.max_index(top_pos[:, t, 0:8], top[:, t, 0:8], sums[t])
            for t in range(QT):
                last = dv.match_replace(sums_rest[t], top[:, t, 0:8], sums[t], -3e38)
            link(last)
            carry_wait()
            for t in range(QT):
                last = dv.max(top[:, t, 8:16], sums_rest[t])
            link(last)
            dv.tensor_tensor(shifted[:], top[:], top[:, :, 0:1].to_broadcast([P, QT, TOPK]),
                             ALU.subtract).then_inc(S["shifted_ready"], 1)
            carry_wait()
            for t in range(QT):
                last = dv.max_index(top_pos[:, t, 8:16], top[:, t, 8:16], sums_rest[t])
            link(last)
            dv.tensor_scalar(pos_a[:], top_pos[:], 4, None, ALU.logical_shift_right)
            link(dv.tensor_scalar(pos_b[:], top_pos[:], 15, None, ALU.bitwise_and))
            dv.tensor_copy(pos_af[:], pos_a[:])
            link(dv.tensor_copy(pos_bf[:], pos_b[:]))
            for n, pos in enumerate((pos_af, pos_bf)):
                link(dv.tensor_tensor(pick[:], iota16, wide(pos[:], TOPK), ALU.is_equal))
                link(dv.tensor_tensor(pick[:], pick[:], tall(best_keyf[:, n], TOPK), ALU.mult))
                link(dv.tensor_reduce(sel[:, n, :, bass.ds(h * TOPK, TOPK)], pick[:], AX.X, ALU.add))
            v.wait_ge(S["weight_exp"], h + 1)
            link(dv.tensor_reduce(wsum[:, 0, :], weight[:], AX.X, ALU.add))
            link(dv.reciprocal(wsum[:, 1, :], wsum[:, 0, :]))
            dv.tensor_tensor(sel[:, 2, :, bass.ds(h * TOPK, TOPK)], weight[:],
                             wsum[:, 1, :].unsqueeze(2).to_broadcast([P, QT, TOPK]),
                             ALU.mult).then_inc(S["sel_ready"], 1)
            v.wait_ge(S["sel_ready"], h + 1)

        leave_loop(end, 25, HEADS)

        for n in range(3):
            wait_read(v, J_SEL + n)

        def hot(i, k, first=False):
            if not first:
                wait_job(v, i * 2 + k + (J_G - 2))
            for t in range(G_TOK):
                tok = bass.ds(i * (2 * G_TOK) + (k * G_TOK + t), 1)
                dv.tensor_scalar(hot2[:, k, t, :], iota, selT[:, 1, tok], None, ALU.is_equal)
                last = dv.tensor_scalar(hot1[:, k, t, :], iota, selT[:, 0, tok], selT[:, 2, tok], ALU.is_equal, ALU.mult)
            last.then_inc(S["hot_ready"], 1)

        hot(0, 0, True)
        hot(0, 1, True)
        with v.Fori(1, T // G_TOK // 2) as i:
            for k in range(2):
                hot(i, k)

        def u_lo_sub(s, e):
            v.wait_ge(S["u_hi_ready"], s * 4 + e + 1)
            k = e % 2
            dv.tensor_tensor(flat(u_lo[:, k]), flat(u_raw[:, k]), flat(u_hi[:, k]), ALU.subtract).then_inc(S["u_split"], 1)

        def v_lo_sub(s, e):
            v.wait_ge(S["v_hi_ready"], s * 4 + e + 1)
            dv.tensor_tensor(v_lo[:, e % 2, :], v_raw[:, e % 2, :], v_hi[:, e % 2, :],
                             ALU.subtract).then_inc(S["v_split"], 1)

        def weigh(j, s, e):
            if e % 2 == 0:
                v.wait_ge(S["g_in"][(e // 2) % 2], s * 16 + (e // 4 + 1) * 16)
            wait_read(v, j, s * 5)
            h3 = hidden[:, e % 2, :].rearrange("p (b t) -> p b t", t=G_BATCH)
            g3 = g_raw[:, (e // 2) % 2, :, (e % 2) * G_BATCH:(e % 2 + 1) * G_BATCH]
            dv.tensor_tensor(h3, h3, g3, ALU.mult).then_inc(S["a_ready"], 1)

        def a_lo_sub(s, e, slot):
            v.wait_ge(S["a_hi_ready"], s * 4 + e + 1)
            dv.tensor_tensor(a_lo[:, slot, e % 2, :], hidden[:, e % 2, :], a_hi[:, slot, e % 2, :],
                             ALU.subtract).then_inc(S["a_split"], 1)

        def expert_step(s, k, has_next=True, more_u=True, before=STEP_JOBS):
            for n in range(GROUP):
                v_lo_sub(s, 2 * k + n)
            j = J_EXP + GROUP + STEP_JOBS * k
            if has_next:
                for n in range(GROUP):
                    weigh(j + n, s, 2 * k + 2 + n)
                    if more_u:
                        u_lo_sub(s, 2 * k + 4 + n)
                for n in range(GROUP):
                    a_lo_sub(s, 2 * k + 2 + n, (k + 1) % 2)
                j += GROUP
            for c in range(KC):
                wait_job(v, s * 20 + (j + c))
                if before:
                    wait_read(v, j + c - before, s * 5)
                dv.tensor_tensor(act[:, c, :], ps[:, (j + c) % 4, :], act[:, c, :],
                                 ALU.add).then_inc(slot_free[(j + c) % 4], 1)

        u_lo_sub(0, 0)
        u_lo_sub(0, 1)
        for n in range(GROUP):
            weigh(J_EXP + n, 0, n)
            u_lo_sub(0, 2 + n)
        for n in range(GROUP):
            a_lo_sub(0, n, 0)
        expert_step(0, 0, before=0)
        expert_step(0, 1)
        with v.Fori(1, GROUPS // 2 - 1) as s:
            expert_step(s, 0)
            expert_step(s, 1)
        expert_step(GROUPS // 2 - 1, 0, more_u=False)
        expert_step(GROUPS // 2 - 1, 1, has_next=False, before=KC)
        rstd_of(J_NORM_OUT, D)
        for c in range(KC):
            dv.scalar_tensor_tensor(act[:, c, :], act[:, c, :], vec[:, V_GFIN + c:V_GFIN + c + 1], rstd[:],
                                    ALU.mult, ALU.mult).then_inc(S["final_ready"], 1)

    block_cm.__exit__(None, None, None)


def kernel(**inputs):
    import concourse.bacc as bacc
    from concourse import mybir
    from concourse.bass_utils import run_bass_kernel_spmd

    a = {k: np.asarray(x) for k, x in inputs.items()}

    def column_tiles(w):
        k, n = w.shape
        return w.reshape(k // P, P, n // P, P).transpose(2, 1, 0, 3).reshape(n // P, P, k)

    w_in = a["w_in"][0]
    glu_a, glu_b = w_in[:, 0:D], w_in[:, D:2 * D]
    at = 2 * D
    q_lat, kv_lat = w_in[:, at:at + LORA], w_in[:, at + LORA:at + 2 * LORA]
    at += 2 * LORA
    rope = w_in[:, at:at + ROPE]
    at += ROPE
    gate_c, gate_m = w_in[:, at:at + D], w_in[:, at + D:at + 2 * D]

    def swapped(w):
        return np.concatenate([w[:, ROPE // 2:], w[:, :ROPE // 2]], axis=1)

    def in_pairs(first, second):
        return np.stack([column_tiles(first), column_tiles(second)], axis=1).reshape(16, P, D)

    wproj = np.concatenate([
        column_tiles(q_lat), column_tiles(kv_lat), column_tiles(np.concatenate([rope, swapped(rope)], axis=1)),
        in_pairs(glu_b, glu_a), in_pairs(gate_c, a["conv_w_pw"][0]), in_pairs(gate_m, a["mla_w_o"][0]),
        column_tiles(a["w_out"][0]), column_tiles(a["peer_w_q"][0])])
    heads = []
    for h in range(HEADS):
        q = a["w_q_up"][0][:, h * (NOPE + ROPE):(h + 1) * (NOPE + ROPE)]
        kv = a["w_kv_up"][0][:, h * (NOPE + VDIM):(h + 1) * (NOPE + VDIM)]
        w = np.concatenate([q[:, :NOPE], q[:, NOPE:], swapped(q[:, NOPE:]), kv], axis=1)
        heads.append(w.reshape(LC, P, 512).transpose(1, 0, 2).reshape(P, LC * 512))
    keysT = a["peer_sub_keys"][0].transpose(3, 0, 1, 2).reshape(P, 16, KEYS)
    uT = a["peer_u"][0].reshape(EXPERT_TILES, P, KC, P).transpose(0, 3, 2, 1).reshape(EXPERT_TILES, P, D)
    vtab = a["peer_v"][0].reshape(EXPERT_TILES, P, D)

    def cols(x):
        return x.reshape(-1, P).T

    dw = a["conv_dw"][0].reshape(TAPS, KC, P).transpose(2, 1, 0).reshape(P, KC * TAPS)
    vecs = np.concatenate([cols(a["norm_mix_g"][0]), cols(a["b_gate"][0, 0]), cols(a["b_gate"][0, 1]),
                           cols(a["conv_dw_b"][0]), cols(a["conv_ln_g"][0]), cols(a["conv_ln_b"][0]),
                           cols(a["q_norm_g"][0]), cols(a["kv_norm_g"][0]), cols(a["norm_ffn_g"][0]),
                           cols(a["norm_final_g"]), dw], axis=1)
    tables = np.stack([np.ones((P, P)), np.eye(P), np.broadcast_to(np.arange(P), (P, P))], axis=1).astype(np.float32)
    freq = np.float32(THETA) ** (-np.arange(0, ROPE, 2, dtype=np.float32) / np.float32(ROPE))
    angle = freq[:, None] * np.arange(T, dtype=np.float32)[None, :]
    rotary = np.concatenate([np.cos(angle), np.cos(angle), -np.sin(angle), np.sin(angle)]).astype(np.float32)

    arrays = dict(xT=a["x"][0].T.reshape(KC, P, T).transpose(1, 0, 2), wproj=wproj, whead=np.stack(heads),
                  keysT=keysT, uT=uT, vtab=vtab, vecs=vecs, tables=tables, rotary=rotary)
    arrays = {k: np.ascontiguousarray(x) for k, x in arrays.items()}
    nc = bacc.Bacc("TRN2", target_bir_lowering=False, num_devices=1)
    args = [nc.dram_tensor(k, x.shape, mybir.dt.float32, kind="ExternalInput").ap() for k, x in arrays.items()]
    args.append(nc.dram_tensor("outT", (P, KC, T), mybir.dt.float32, kind="ExternalOutput").ap())
    build(nc, *args)
    got = run_bass_kernel_spmd(nc, [arrays], core_ids=[0]).results[0]["outT"]
    return np.ascontiguousarray(got.transpose(2, 1, 0).reshape(1, T, D))
```

```python
import math

import numpy as np

P = 128
D = 1024
T = 1024
KC = D // P
HALF = 512
TAPS = 31
HEADS = 8
NOPE, ROPE, VDIM = 128, 64, 128
LORA = 256
LC = LORA // P
QT = T // P
CHUNK = 64
KEYS = 128
TOPK = 16
EXPERT_TILES = 128
EPS = 1e-6
SCALE = 1.0 / math.sqrt(NOPE + ROPE)
THETA = 10000.0

W_LATENT = 0
W_GLU = 5
W_CONVOUT = W_GLU + 16
W_MLAOUT = W_CONVOUT + 16
W_OUT = W_MLAOUT + 16
W_ROUTER = W_OUT + 8
W_JOBS = W_ROUTER + 16

J_NORM_X = 0
J_LATENT = 1
J_NORM_Q = 6
J_NORM_KV = 7
J_GLU = 8
J_HEAD = J_GLU + 16
J_LN_MEAN = J_HEAD + 32
J_LN_VAR = J_LN_MEAN + 1
J_CONVOUT = J_LN_VAR + 1
J_MLAOUT = J_CONVOUT + 16
J_OUT = J_MLAOUT + 16
J_NORM_H = J_OUT + 8
J_ROUTER = J_NORM_H + 1
R_JOBS = 8
R_QUERY, R_SCORE, R_HIDDEN = 0, 3, (2, 5, 6, 7)
J_SEL = J_ROUTER + 8 * R_JOBS
J_G = J_SEL + 3
G_TOK = 8
G_BATCH = 64
G_BLOCKS = T // G_BATCH
G_JOBS = 20
GROUP = 2
GROUPS = EXPERT_TILES // GROUP
AHEAD = 64
GROUPS_AHEAD = AHEAD // GROUP
J_AHEAD = J_G + G_BLOCKS // 2 * G_JOBS
STEP_JOBS = GROUP + KC
J_EXP = J_AHEAD + GROUPS_AHEAD * KC
J_STEP = J_EXP + GROUP - STEP_JOBS * GROUPS_AHEAD
J_NORM_OUT = J_EXP + (GROUPS - GROUPS_AHEAD) * STEP_JOBS

V_GMIX, V_BC, V_BM, V_DWB, V_LNG, V_LNB, V_QG, V_KG, V_GFFN, V_GFIN = 0, 8, 16, 24, 32, 40, 48, 50, 52, 60
V_DW = 68
V_COLS = V_DW + KC * TAPS


def build(nc, xT, wproj, whead, keysT, uT, vtab, vecs, tables, rotary, outT):
    import concourse.bass as bass
    from concourse import mybir

    f32, f32r, u32 = mybir.dt.float32, mybir.dt.float32r, mybir.dt.uint32
    ALU, ACT, AX = mybir.AluOpType, mybir.ActivationFunctionType, mybir.AxisListType
    mm = nc.tensor.matmul

    base = (nc.sbuf_base + 31) // 32 * 32

    def at(name, shape, kib, dt=f32):
        return nc.alloc_sbuf_tensor_at(name, shape, dt, offset=base + int(kib * 1024))

    act = at("act", [P, KC, T], 0)
    region_a = at("region_a", [P, KC, T], 32)
    region_b = at("region_b", [P, KC, T], 64)
    merged = at("merged", [P, KC, T], 96)
    q_nope = at("q_nope", [P, T], 96)
    q_rope = at("q_rope", [ROPE, T], 100)
    k_nope = at("k_nope", [P, T], 104)
    v_head = at("v_head", [P, QT, VDIM], 108)
    probs = at("probs", [P, 2, T], 112)
    probsT = at("probsT", [P, 2, QT, P], 120)
    wring = at("wring", [P, 4, KC, P], 128)
    latent = at("latent", [P, 4, T], 144)
    k_rope = at("k_rope", [ROPE, T], 160)
    rot = at("rot", [P, T], 164)
    rstd = at("rstd", [P, T], 168)
    squares = at("squares", [P, 2, T], 172)
    gate = at("gate", [P, 2, T], 180)
    glu = at("glu", [P, 2, TAPS - 1 + T], 188)
    hwring = at("hwring", [P, LC, 512], 196.5)
    tabs = at("tabs", [P, 3, P], 200.5)
    vec = at("vec", [P, V_COLS], 202)
    negmax = at("negmax", [P, 2], 203.5)
    expsum = at("expsum", [P, 2], 203.625)
    spare = at("spare", [P, 32], 203.75)
    ones, ident, iota = tabs[:, 0, :], tabs[:, 1, :], tabs[:, 2, :]
    x_hi = at("x_hi", [P, KC, T], 32, f32r)
    x_lo = at("x_lo", [P, KC, T], 64, f32r)
    wq_hi = at("wq_hi", [P, 2, KC, P], 96, f32r)
    wq_lo = at("wq_lo", [P, 2, KC, P], 104, f32r)
    query = at("query", [P, 2, T], 112)
    keys = at("keys", [P, 16, KEYS], 120)
    best = at("best", [P, 2, QT, TOPK], 144)
    best_key = at("best_key", [P, 2, QT, TOPK], 145, u32)
    best_keyf = at("best_keyf", [P, 2, QT, TOPK], 146)
    rest = at("rest", [P, QT, KEYS], 148)
    cand = at("cand", [P, QT, TOPK, TOPK], 152)
    cand_rest = at("cand_rest", [P, QT, TOPK, TOPK], 160)
    pick = at("pick", [P, QT, TOPK, TOPK], 172)
    top = at("top", [P, QT, TOPK], 180)
    top_pos = at("top_pos", [P, QT, TOPK], 180.5, u32)
    pos_a = at("pos_a", [P, QT, TOPK], 181, u32)
    pos_b = at("pos_b", [P, QT, TOPK], 181.5, u32)
    pos_af = at("pos_af", [P, QT, TOPK], 182)
    pos_bf = at("pos_bf", [P, QT, TOPK], 182.5)
    shifted = at("shifted", [P, QT, TOPK], 183)
    weight = at("weight", [P, QT, TOPK], 183.5)
    wsum = at("wsum", [P, 2, QT], 184)
    sel = at("sel", [P, 3, QT, P], 188)
    selT = at("selT", [P, 3, T], 96)
    hot2 = at("hot2", [P, 2, G_TOK, P], 108)
    hot1 = at("hot1", [P, 2, G_TOK, P], 116)
    gblock = at("gblock", [P, 2, P, G_BATCH], 124)
    a_hi = at("a_hi", [P, 2, GROUP, T], 96, f32r)
    a_lo = at("a_lo", [P, 2, GROUP, T], 112, f32r)
    v_hi = at("v_hi", [P, GROUP, D], 128, f32r)
    v_lo = at("v_lo", [P, GROUP, D], 136, f32r)
    v_raw = at("v_raw", [P, 2, D], 144)
    u_raw = at("u_raw", [P, 2, KC, P], 152)
    u_hi = at("u_hi", [P, 2, KC, P], 160, f32r)
    u_lo = at("u_lo", [P, 2, KC, P], 168, f32r)
    g_raw = at("g_raw", [P, 2, G_BLOCKS, GROUP * G_BATCH], 176)
    hidden = at("hidden", [P, 2, T], 192)
    v_hi_odd = at("v_hi_odd", [P, GROUP, D], 160, f32r)
    v_lo_odd = at("v_lo_odd", [P, GROUP, D], 168, f32r)
    ahead_raw = at("ahead_raw", [P, 2, KC, P], 0)
    ahead_hi = at("ahead_hi", [P, 2, KC, P], 8, f32r)
    ahead_lo = at("ahead_lo", [P, 2, KC, P], 16, f32r)
    ahead_out = at("ahead_out", [P, 2, T], 24)

    g_dram = nc.dram_tensor("g_dram", [G_BLOCKS, P, P * G_BATCH], f32).ap()
    h_dram = nc.dram_tensor("h_dram", [P, KC, T], f32).ap()
    ahead_dram = nc.dram_tensor("ahead_dram", [AHEAD, P, T], f32).ap()
    ps = nc.alloc_psum_tensor("ps", [P, 4, T], f32)

    names = dict(
        consts_in=1, x_in=4, x_again=1, w_in=4, hw_in=1, keys_in=1, u_in=2, v_in=2, g_in=2, g_out=2, y_out=1, h_out=1, h_in=1, ahead_out=2, hid_in=2,
        job_done=1, slot_free=4,
        sq_ready=1, sq_used=1, var_ready=1, rstd_ready=1, act_ready=1,
        lat_normed=1, krope_ready=1,
        gate_used=1, conv_ready=1,
        s_ready=1, max_ready=1, exp_ready=1, p_ready=1, pt_ready=1, pt_copied=1, pv_done=1, o_ready=1, o_copied=1,
        centred=1, ln_ready=1, silu_ready=1, merged_ready=1, h_ready=1,
        xn_ready=1, xhi_ready=1, xlo_ready=1, wq_hi_ready=1, wq_split=1,
        shifted_ready=1, weight_exp=1, sel_ready=1, selT_ready=1, hot_ready=1, 
        a_ready=1, a_hi_ready=1, a_split=1, u_hi_ready=1, u_split=1, v_hi_ready=1, v_split=1,
        final_ready=1, dve_step=1)
    S = {}
    for name, n in names.items():
        made = [nc.alloc_semaphore(f"{name}{k}" if n > 1 else name) for k in range(n)]
        S[name] = made if n > 1 else made[0]
    job_done, slot_free = S["job_done"], S["slot_free"]

    def wait_job(eng, j):
        eng.wait_ge(job_done, j + 1)

    def wait_slot(eng, j, rounds=0):
        eng.wait_ge(slot_free[j % 4], rounds + j // 4)

    def wait_read(eng, j, rounds=0):
        eng.wait_ge(slot_free[j % 4], rounds + (j // 4 + 1))

    def flat(ap):
        return ap.rearrange("p a b -> p (a b)")

    block_cm = nc.Block()
    block = block_cm.__enter__()

    @block.sync
    def _(sp):
        sp.dma_start(vec[:], vecs).then_inc(S["consts_in"], 16)
        sp.dma_start(tabs[:], tables).then_inc(S["consts_in"], 16)
        sp.dma_start(rot[:], rotary).then_inc(S["consts_in"], 16)
        for k in range(4):
            sp.dma_start(region_a[:, 2 * k:2 * k + 2, :], xT[:, 2 * k:2 * k + 2, :]).then_inc(S["x_in"][k], 16)
            sp.dma_start(flat(wring[:, k]), wproj[k]).then_inc(S["w_in"][k], 16)

        def load_w(w, i=0):
            sp.dma_start(flat(wring[:, w % 4]), wproj[i * 4 + w]).then_inc(S["w_in"][w % 4], 16)

        for w in range(4, 9):
            wait_job(sp, J_LATENT + w - 4)
            load_w(w)
        with sp.Fori(0, 3) as i:
            for w in range(W_GLU + 4, W_GLU + 8):
                wait_job(sp, i * 4 + (J_GLU + w - 4 - W_GLU))
                load_w(w, i)
        sp.dma_start(flat(hwring[:]), whead[0]).then_inc(S["hw_in"], 16)
        for w in range(W_CONVOUT, W_CONVOUT + 4):
            wait_job(sp, J_GLU + w - 4 - W_GLU)
            load_w(w)
        with sp.Fori(1, HEADS) as h:
            wait_job(sp, h * 4 + (J_HEAD - 1))
            sp.dma_start(flat(hwring[:]), whead[h]).then_inc(S["hw_in"], 16)
        later = J_CONVOUT - W_CONVOUT
        with sp.Fori(0, 4) as i:
            for w in range(W_CONVOUT + 4, W_CONVOUT + 8):
                wait_job(sp, i * 4 + (w - 4 + later))
                load_w(w, i)
        sp.dma_start(region_b[:], xT).then_inc(S["x_again"], 16)
        with sp.Fori(0, 6) as i:
            for w in range(W_CONVOUT + 20, W_CONVOUT + 24):
                wait_job(sp, i * 4 + (w - 4 + later))
                load_w(w, i)
        wait_job(sp, J_NORM_H - 1)
        sp.dma_start(keys[:], keysT).then_inc(S["keys_in"], 16)
        sp.wait_ge(S["xn_ready"], KC)
        sp.dma_start(h_dram, act[:]).then_inc(S["h_out"], 16)
        sp.wait_ge(S["h_out"], 16)

        def load_ahead(n, i=0, step=0):
            sp.dma_start(flat(ahead_raw[:, n % 2]), uT[i * step + n]).then_inc(S["u_in"][n % 2], 16)

        def tile_ahead(n, j, i=0, step=0, jstep=0, more=True, between=None):
            if more:
                sp.wait_ge(S["u_split"], i * step + (n + 1))
                load_ahead(n + 2, i, step)
            if between:
                between()
            wait_read(sp, j, i * (jstep // 4))
            sp.dma_start(ahead_dram[i * step + n], ahead_out[:, n % 2]).then_inc(S["ahead_out"][n % 2], 16)

        load_ahead(0)
        load_ahead(1)

        def router_loads(i, h, more_w=True):
            if more_w:
                for k in range(2):
                    sp.wait_ge(S["wq_split"], i * 4 + (2 * h + k + 1))
                    load_w(W_ROUTER + 4 + 2 * h + k, i)
            for m in range(4):
                tile_ahead(4 * h + m, J_ROUTER + R_JOBS * h + R_HIDDEN[m], i, 8, 2 * R_JOBS)

        with sp.Fori(0, 3) as i:
            router_loads(i, 0)
            router_loads(i, 1)
        router_loads(3, 0, more_w=False)
        router_loads(3, 1, more_w=False)

        def g_loads(i, last=False):
            for q in range(4):
                def g_store():
                    wait_read(sp, J_G + 5 * q + 3, i * (G_JOBS // 4))
                    sp.dma_start(g_dram[i * 2 + q // 2],
                                 gblock[:, q // 2].rearrange("p a t -> p (a t)")).then_inc(S["g_out"][q // 2], 16)
                tile_ahead(AHEAD // 2 + q, J_G + 5 * q + 4, i, 4, G_JOBS, more=not (last and q >= 2),
                           between=g_store if q % 2 else None)

        with sp.Fori(0, G_BLOCKS // 2 - 1) as i:
            g_loads(i)
        g_loads(G_BLOCKS // 2 - 1, last=True)
        for k in range(2):
            sp.wait_ge(S["g_out"][k], 16 * G_BLOCKS // 2)
            sp.wait_ge(S["ahead_out"][k], 16 * AHEAD // 2)

        def load_u(e, k):
            sp.dma_start(flat(u_raw[:, k]), uT[e]).then_inc(S["u_in"][k], 16)

        def load_v(e, k):
            sp.dma_start(v_raw[:, k], vtab[e]).then_inc(S["v_in"][k], 16)

        def load_g(g, k):
            cols = g_dram.rearrange("b p (g c) -> g p b c", c=GROUP * G_BATCH)
            sp.dma_start(g_raw[:, k], cols[g]).then_inc(S["g_in"][k], 16)

        def ahead_loads(s, k, first=False):
            for n in range(GROUP):
                if not first:
                    sp.wait_ge(S["v_split"], s * 4 + 2 * k - 1 + n)
                load_v(s * 4 + (2 * k + n), n)
            if not isinstance(s, int):
                sp.wait_ge(S["a_ready"], s * 4 + 2 * k - 2)
            load_g(s * 2 + k, k)
            for n in range(GROUP):
                if not first:
                    sp.wait_ge(S["a_split"], s * 4 + 2 * k - 1 + n)
                sp.dma_start(hidden[:, n], ahead_dram[s * 4 + (2 * k + n)]).then_inc(S["hid_in"][n], 16)

        ahead_loads(0, 0, first=True)
        sp.dma_start(act[:], h_dram).then_inc(S["h_in"], 16)
        ahead_loads(0, 1)
        with sp.Fori(1, GROUPS_AHEAD // 2) as s:
            ahead_loads(s, 0)
            ahead_loads(s, 1)

        def expert_loads(s, k, more_u=True, more_g=True):
            for n in range(GROUP):
                sp.wait_ge(S["v_split"], s * 4 + 2 * k - 1 + n)
                load_v(s * 4 + (2 * k + n), n)
            if more_g:
                sp.wait_ge(S["a_ready"], s * 4 + 2 * k)
                load_g(s * 2 + (k + 1), (k + 1) % 2)
            if more_u:
                for n in range(GROUP):
                    sp.wait_ge(S["u_split"], s * 4 + 2 * k + 3 + n)
                    load_u(s * 4 + (2 * k + 4 + n), n)

        load_u(AHEAD, 0)
        load_u(AHEAD + 1, 1)
        sp.wait_ge(S["a_ready"], AHEAD - GROUP)
        load_g(GROUPS_AHEAD, 0)
        for n in range(GROUP):
            sp.wait_ge(S["u_split"], AHEAD + n + 1)
            load_u(AHEAD + 2 + n, n)
        with sp.Fori(GROUPS_AHEAD // 2, GROUPS // 2 - 1) as s:
            expert_loads(s, 0)
            expert_loads(s, 1)
        expert_loads(GROUPS // 2 - 1, 0, more_u=False)
        expert_loads(GROUPS // 2 - 1, 1, more_u=False, more_g=False)

        for c in range(KC):
            sp.wait_ge(S["final_ready"], c + 1)
            sp.dma_start(outT[:, c, :], act[:, c, :]).then_inc(S["y_out"], 16)
        sp.wait_ge(S["y_out"], 16 * KC)

    @block.tensor
    def _(pe):
        used = {"sq": 0}

        def project(j, w, acts, i):
            wait_slot(pe, j, i)
            pe.wait_ge(S["w_in"][w % 4], i * 16 + (w // 4 + 1) * 16)
            for half in range(2):
                cols = slice(half * HALF, (half + 1) * HALF)
                for c in range(KC):
                    last = mm(ps[:, j % 4, cols], wring[:, w % 4, c, :], acts[:, c, cols],
                              start=c == 0, stop=c == KC - 1)
            last.then_inc(job_done, 1)

        def ones_sum(j, tiles):
            if j >= 4:
                wait_slot(pe, j)
            for n, (sem, value, tile, after) in enumerate(tiles):
                pe.wait_ge(sem, value)
                for half in range(2):
                    cols = slice(half * HALF, (half + 1) * HALF)
                    last = mm(ps[:, j % 4, cols], ones, tile[:, cols], start=n == 0, stop=n == len(tiles) - 1,
                              skip_group_check=True)
                if after is not None:
                    last.then_inc(after, 1)
            if tiles[-1][3] is None:
                last.then_inc(job_done, 1)
            else:
                pe.wait_ge(tiles[-1][3], used["sq"])
                pe.nop().then_inc(job_done, 1)

        def square_tiles(n):
            first = used["sq"]
            used["sq"] += n
            return [(S["sq_ready"], k + 1, squares[:, k % 2, :], S["sq_used"]) for k in range(first, first + n)]

        pe.wait_ge(S["consts_in"], 48)
        ones_sum(J_NORM_X, square_tiles(KC))
        for k in range(5):
            j, w = J_LATENT + k, W_LATENT + k
            if j >= 4:
                wait_slot(pe, j)
            pe.wait_ge(S["w_in"][w % 4], (w // 4 + 1) * 16)
            for half in range(2):
                cols = slice(half * HALF, (half + 1) * HALF)
                for c in range(KC):
                    if k == 0 and half == 0:
                        pe.wait_ge(S["act_ready"], c + 1)
                    last = mm(ps[:, j % 4, cols], wring[:, w % 4, c, :], act[:, c, cols],
                              start=c == 0, stop=c == KC - 1)
            last.then_inc(job_done, 1)
        ones_sum(J_NORM_Q, square_tiles(LC))
        ones_sum(J_NORM_KV, square_tiles(LC))

        with pe.Fori(0, 4) as i:
            for k in range(4):
                project(J_GLU + k, W_GLU + k, act, i)

        pe.wait_ge(S["lat_normed"], 4)
        pe.wait_ge(S["krope_ready"], 1)
        with pe.Fori(0, HEADS) as h:
            pe.wait_ge(S["hw_in"], h * 16 + 16)
            for k, (first, tile) in enumerate(((0, 0), (128, 0), (256, 2))):
                j = J_HEAD + k
                wait_slot(pe, j, h)
                for half in range(2):
                    cols = slice(half * HALF, (half + 1) * HALF)
                    for c in range(LC):
                        last = mm(ps[:, j % 4, cols], hwring[:, c, first:first + P], latent[:, tile + c, cols],
                                  start=c == 0, stop=c == LC - 1)
                last.then_inc(job_done, 1)
            j = J_HEAD + 3
            wait_slot(pe, j, h)
            pe.wait_ge(S["o_copied"], h + 1)
            for t in range(QT):
                for c in range(LC):
                    last = mm(ps[:, j % 4, t * P:(t + 1) * P], latent[:, 2 + c, t * P:(t + 1) * P],
                              hwring[:, c, 384:512], start=c == 0, stop=c == LC - 1)
            last.then_inc(job_done, 1)
            for k in range(3):
                wait_read(pe, J_HEAD + k, h)

            def scores(i):
                rows = slice(i * P, (i + 1) * P)
                width = (i + 1) * P
                for c0 in range(0, width, HALF):
                    cols = slice(c0, min(width, c0 + HALF))
                    mm(ps[:, i % 2, cols], q_nope[:, rows], k_nope[:, cols], start=True, stop=False)
                    last = mm(ps[:, i % 2, cols], q_rope[:, rows], k_rope[:, cols], start=False, stop=True)
                last.then_inc(S["s_ready"], 1)

            def transposes(i):
                pe.wait_ge(S["p_ready"], h * QT + i + 1)
                pe.wait_ge(S["pt_copied"], h * QT + i + 1)
                for b in range(i + 1):
                    last = nc.tensor.transpose(ps[:, 2, b * P:(b + 1) * P], probs[:, i % 2, b * P:(b + 1) * P], ident)
                last.then_inc(S["pt_ready"], 1)

            def values(i):
                pe.wait_ge(S["pt_copied"], h * QT + i + 2)
                for b in range(i + 1):
                    last = mm(ps[:, 3, i * P:(i + 1) * P], v_head[:, b, :], probsT[:, i % 2, b, :],
                              start=b == 0, stop=b == i)
                last.then_inc(S["pv_done"], 1)

            scores(0)
            scores(1)
            transposes(0)
            scores(2)
            wait_read(pe, J_HEAD + 3, h)
            values(0)
            for i in range(1, QT):
                transposes(i)
                if i + 2 < QT:
                    scores(i + 2)
                values(i)

        ones_sum(J_LN_MEAN, [(S["conv_ready"], c + 1, region_b[:, c, :], None) for c in range(KC)])
        ones_sum(J_LN_VAR, square_tiles(KC))

        def gated_branch(j0, w0, branch, ready, n):
            with pe.Fori(0, 4) as i:
                for k in range(4):
                    if k == 1:
                        pe.wait_ge(ready, n)
                    project(j0 + k, w0 + k, branch if k % 2 else act, i)

        gated_branch(J_CONVOUT, W_CONVOUT, region_b, S["silu_ready"], KC)
        gated_branch(J_MLAOUT, W_MLAOUT, region_a, S["o_copied"], HEADS + 1)
        pe.wait_ge(S["merged_ready"], KC)
        with pe.Fori(0, 2) as i:
            for k in range(4):
                project(J_OUT + k, W_OUT + k, merged, i)
        ones_sum(J_NORM_H, square_tiles(KC))

        def three_passes(out, hi, lo, m_hi, m_lo, first, last_one):
            mm(out, hi, m_hi, start=first, stop=False)
            mm(out, hi, m_lo, start=False, stop=False)
            return mm(out, lo, m_hi, start=False, stop=last_one)

        def hidden_half(j, hi, lo, half):
            cols = slice(half * HALF, (half + 1) * HALF)
            for c in range(KC):
                last = three_passes(ps[:, j % 4, cols], hi[:, c, :], lo[:, c, :],
                                    x_hi[:, c, cols], x_lo[:, c, cols], c == 0, c == KC - 1)
            return last

        pe.wait_ge(S["xlo_ready"], KC)
        pe.wait_ge(S["keys_in"], 16)
        with pe.Fori(0, HEADS) as h:
            def queries(k):
                j = J_ROUTER + R_QUERY + k
                wait_slot(pe, j, h * 2)
                pe.wait_ge(S["wq_split"], h * 2 + k + 1)
                for half in range(2):
                    last = hidden_half(j, wq_hi[:, k], wq_lo[:, k], half)
                last.then_inc(job_done, 1)

            def key_scores(k):
                j = J_ROUTER + R_SCORE + k
                wait_slot(pe, j, h * 2)
                wait_read(pe, J_ROUTER + R_QUERY + k, h * 2)
                for t in range(QT):
                    last = mm(ps[:, j % 4, t * P:(t + 1) * P], query[:, k, t * P:(t + 1) * P],
                              keys[:, bass.ds(h * 2 + k, 1), :].rearrange("p a k -> p (a k)"), start=True, stop=True)
                last.then_inc(job_done, 1)

            def hidden_ahead(m):
                j = J_ROUTER + R_HIDDEN[m]
                wait_slot(pe, j, h * 2)
                pe.wait_ge(S["u_split"], h * 4 + m + 1)
                for half in range(2):
                    last = hidden_half(j, ahead_hi[:, m % 2], ahead_lo[:, m % 2], half)
                last.then_inc(job_done, 1)

            queries(0)
            queries(1)
            hidden_ahead(0)
            key_scores(0)
            key_scores(1)
            hidden_ahead(1)
            hidden_ahead(2)
            hidden_ahead(3)
        pe.wait_ge(S["sel_ready"], HEADS)
        for n in range(3):
            j = J_SEL + n
            wait_slot(pe, j)
            for t in range(QT):
                last = nc.tensor.transpose(ps[:, j % 4, t * P:(t + 1) * P], sel[:, n, t, :], ident)
            last.then_inc(job_done, 1)

        with pe.Fori(0, G_BLOCKS // 2) as i:
            for q in range(4):
                def g_job(r):
                    j = J_G + 5 * q + r
                    wait_slot(pe, j, i * (G_JOBS // 4))
                    pe.wait_ge(S["hot_ready"], i * 16 + (4 * q + r + 1))
                    for t in range(G_TOK):
                        last = mm(ps[:, j % 4, t * P:(t + 1) * P], hot2[:, r % 2, t, :], hot1[:, r % 2, t, :],
                                  start=True, stop=True)
                    last.then_inc(job_done, 1)

                j = J_G + 5 * q + 4
                g_job(0)
                g_job(1)
                wait_slot(pe, j, i * (G_JOBS // 4))
                pe.wait_ge(S["u_split"], i * 4 + (AHEAD // 2 + q + 1))
                hidden_half(j, ahead_hi[:, q % 2], ahead_lo[:, q % 2], 0)
                g_job(2)
                g_job(3)
                hidden_half(j, ahead_hi[:, q % 2], ahead_lo[:, q % 2], 1).then_inc(job_done, 1)

        def hidden_job(j, s, e):
            wait_slot(pe, j, s * 5)
            hidden_half(j, u_hi[:, e], u_lo[:, e], 0)
            hidden_half(j, u_hi[:, e], u_lo[:, e], 1).then_inc(job_done, 1)

        def value_job(j, rounds, hi, lo, place, c):
            wait_slot(pe, j, rounds)
            for half in range(2):
                cols = slice(half * HALF, (half + 1) * HALF)
                for n in range(GROUP):
                    feats = slice(c * P, (c + 1) * P)
                    last = three_passes(ps[:, j % 4, cols], hi[:, n, feats], lo[:, n, feats],
                                        a_hi[:, place, n, cols], a_lo[:, place, n, cols], n == 0, n == GROUP - 1)
            last.then_inc(job_done, 1)

        def expert_step(s, k, has_next=True):
            j = J_STEP + STEP_JOBS * k
            if has_next:
                for n in range(GROUP):
                    pe.wait_ge(S["u_split"], s * 4 + 2 * k + 3 + n)
                    hidden_job(j + n, s, n)
                j += GROUP
            pe.wait_ge(S["v_split"], s * 4 + 2 * k + 2)
            pe.wait_ge(S["a_split"], s * 4 + 2 * k + 2)
            for c in range(KC):
                value_job(j + c, s * 5, v_hi, v_lo, k, c)

        with pe.Fori(0, GROUPS_AHEAD // 2) as s:
            for k, (hi, lo) in enumerate(((v_hi, v_lo), (v_hi_odd, v_lo_odd))):
                pe.wait_ge(S["v_split"], s * 4 + 2 * k + 2)
                pe.wait_ge(S["a_split"], s * 4 + 2 * k + 2)
                for c in range(KC):
                    value_job(J_AHEAD + KC * k + c, s * 4, hi, lo, k, c)
        for n in range(GROUP):
            pe.wait_ge(S["u_split"], AHEAD + n + 1)
            hidden_job(J_EXP + n, 0, n)
        with pe.Fori(GROUPS_AHEAD // 2, GROUPS // 2 - 1) as s:
            expert_step(s, 0)
            expert_step(s, 1)
        expert_step(GROUPS // 2 - 1, 0)
        expert_step(GROUPS // 2 - 1, 1, has_next=False)
        ones_sum(J_NORM_OUT, square_tiles(KC))

    @block.scalar
    def _(sc):
        fn = nc.scalar.activation
        count = {"sq": 0, "rstd": 0}

        def square(tile):
            n = count["sq"]
            count["sq"] += 1
            if n >= 2:
                sc.wait_ge(S["sq_used"], n - 1)
            fn(squares[:, n % 2, :], tile, ACT.Square).then_inc(S["sq_ready"], 1)

        def root():
            count["rstd"] += 1
            sc.wait_ge(S["var_ready"], count["rstd"])
            fn(rstd[:], rstd[:], ACT.Sqrt).then_inc(S["rstd_ready"], 1)

        for c in range(KC):
            if c % 2 == 0:
                sc.wait_ge(S["x_in"][c // 2], 16)
            square(region_a[:, c, :])
        root()
        sc.wait_ge(S["consts_in"], 48)
        for k in range(4):
            j = J_LATENT + k
            wait_job(sc, j)
            square(ps[:, j % 4, :])
            fn(latent[:, k, :], ps[:, j % 4, :], ACT.Copy).then_inc(slot_free[j % 4], 1)
        root()
        root()
        with sc.Fori(0, 4) as i:
            for n in range(2):
                j = J_GLU + 2 * n
                wait_job(sc, i * 4 + j)
                sc.wait_ge(S["gate_used"], i * 2 + n + 1)
                fn(gate[:, n, :], ps[:, j % 4, :], ACT.Sigmoid).then_inc(slot_free[j % 4], 1)

        sc.nop().then_inc(S["o_copied"], 1)
        sc.nop().then_inc(S["pt_copied"], 1)
        with sc.Fori(0, HEADS) as h:
            wait_job(sc, h * 4 + J_HEAD)
            fn(q_nope[:], ps[:, 0, :], ACT.Copy, scale=SCALE).then_inc(slot_free[0], 1)
            wait_job(sc, h * 4 + (J_HEAD + 2))
            fn(k_nope[:], ps[:, 2, :], ACT.Copy).then_inc(slot_free[2], 1)
            wait_job(sc, h * 4 + (J_HEAD + 3))
            fn(v_head[:].rearrange("p t v -> p (t v)"), ps[:, 3, :], ACT.Copy).then_inc(slot_free[3], 1)

            def exps(i):
                sc.wait_ge(S["max_ready"], h * QT + i + 1)
                if i >= 2:
                    sc.wait_ge(S["pt_ready"], h * QT + i - 1)
                width = (i + 1) * P
                fn(probs[:, i % 2, 0:width], ps[:, i % 2, 0:width], ACT.Exp, bias=negmax[:, i % 2:i % 2 + 1],
                   accum_out=expsum[:, i % 2:i % 2 + 1]).then_inc(S["exp_ready"], 1)

            def copy_probsT(i):
                sc.wait_ge(S["pt_ready"], h * QT + i + 1)
                if i >= 2:
                    sc.wait_ge(S["pv_done"], h * QT + i - 1)
                width = (i + 1) * P
                fn(probsT[:, i % 2, 0:i + 1, :].rearrange("p b k -> p (b k)"), ps[:, 2, 0:width],
                   ACT.Copy).then_inc(S["pt_copied"], 1)

            exps(0)
            for i in range(QT):
                if i + 1 < QT:
                    exps(i + 1)
                copy_probsT(i)
            sc.wait_ge(S["pv_done"], h * QT + QT)
            fn(region_a[:, bass.ds(h, 1), :].rearrange("p a t -> p (a t)"), ps[:, 3, :],
               ACT.Copy).then_inc(S["o_copied"], 1)

        for c in range(KC):
            sc.wait_ge(S["centred"], c + 1)
            square(region_b[:, c, :])
        root()
        for c in range(KC):
            sc.wait_ge(S["ln_ready"], c + 1)
            fn(region_b[:, c, :], region_b[:, c, :], ACT.Silu, scale=vec[:, V_LNG + c:V_LNG + c + 1],
               bias=vec[:, V_LNB + c:V_LNB + c + 1]).then_inc(S["silu_ready"], 1)
        for phase, (j0, bias) in enumerate(((J_CONVOUT, V_BC), (J_MLAOUT, V_BM))):
            with sc.Fori(0, 4) as i:
                for n in range(2):
                    j = j0 + 2 * n
                    wait_job(sc, i * 4 + j)
                    sc.wait_ge(S["gate_used"], i * 2 + (8 * (phase + 1) + n + 1))
                    fn(gate[:, n, :], ps[:, j % 4, :], ACT.Sigmoid,
                       bias=vec[:, bass.ds(i * 2 + (bias + n), 1)]).then_inc(slot_free[j % 4], 1)
        for c in range(KC):
            sc.wait_ge(S["h_ready"], c + 1)
            square(act[:, c, :])
        root()

        for c in range(KC):
            sc.wait_ge(S["xn_ready"], c + 1)
            fn(x_hi[:, c, :], gate[:, c % 2, :], ACT.Copy).then_inc(S["xhi_ready"], 1)

        def split_wq(n, i=0):
            w = W_ROUTER + n
            sc.wait_ge(S["w_in"][w % 4], i * 16 + (w // 4 + 1) * 16)
            fn(flat(wq_hi[:, n % 2]), flat(wring[:, w % 4]), ACT.Copy).then_inc(S["wq_hi_ready"], 1)

        def ahead_hi_copy(e, i=0, step=0):
            sc.wait_ge(S["u_in"][e % 2], i * (8 * step) + (e // 2 + 1) * 16)
            fn(flat(ahead_hi[:, e % 2]), flat(ahead_raw[:, e % 2]), ACT.Copy).then_inc(S["u_hi_ready"], 1)

        def ahead_gelu(e, j, i=0, step=0, jstep=0, more=True):
            wait_job(sc, i * jstep + j)
            if e >= 2 or not isinstance(i, int):
                sc.wait_ge(S["ahead_out"][e % 2], i * (8 * step) + e // 2 * 16)
            fn(ahead_out[:, e % 2, :], ps[:, j % 4, :], ACT.Gelu_apprx_tanh).then_inc(slot_free[j % 4], 1)
            if more:
                ahead_hi_copy(e + 2, i, step)

        def router_head(i, h, more_w=True):
            for k in range(2):
                j = J_ROUTER + R_JOBS * h + R_QUERY + k
                wait_job(sc, i * (2 * R_JOBS) + j)
                fn(query[:, k, :], ps[:, j % 4, :], ACT.Copy).then_inc(slot_free[j % 4], 1)
                if more_w:
                    split_wq(2 * h + k + 2, i)
            for m in range(4):
                ahead_gelu(4 * h + m, J_ROUTER + R_JOBS * h + R_HIDDEN[m], i, 8, 2 * R_JOBS)
            sc.wait_ge(S["shifted_ready"], i * 2 + h + 1)
            fn(weight[:], shifted[:], ACT.Exp).then_inc(S["weight_exp"], 1)

        split_wq(0)
        split_wq(1)
        ahead_hi_copy(0)
        ahead_hi_copy(1)
        router_head(0, 0)
        router_head(0, 1)
        with sc.Fori(1, 3) as i:
            router_head(i, 0)
            router_head(i, 1)
        router_head(3, 0)
        router_head(3, 1, more_w=False)
        for n in range(3):
            j = J_SEL + n
            wait_job(sc, j)
            fn(selT[:, n, :], ps[:, j % 4, :], ACT.Copy).then_inc(slot_free[j % 4], 1)
        def g_blocks(i, first=False, last=False):
            for q in range(4):
                b = q // 2
                if q % 2 == 0 and not first:
                    sc.wait_ge(S["g_out"][b], i * 16)
                for r in range(4):
                    j = J_G + 5 * q + r
                    wait_job(sc, i * G_JOBS + j)
                    tok = slice(G_TOK * (4 * (q % 2) + r), G_TOK * (4 * (q % 2) + r + 1))
                    fn(gblock[:, b, :, tok].rearrange("p a t -> p t a"),
                       ps[:, j % 4, :].rearrange("p (t a) -> p t a", a=P), ACT.Copy).then_inc(slot_free[j % 4], 1)
                ahead_gelu(AHEAD // 2 + q, J_G + 5 * q + 4, i, 4, G_JOBS, more=not (last and q >= 2))

        g_blocks(0, first=True)
        with sc.Fori(1, G_BLOCKS // 2 - 1) as i:
            g_blocks(i)
        g_blocks(G_BLOCKS // 2 - 1, last=True)

        def u_hi_copy(e, k, s=0):
            sc.wait_ge(S["u_in"][k], s * 32 + (e // 2 + 1) * 16)
            fn(flat(u_hi[:, k]), flat(u_raw[:, k]), ACT.Copy).then_inc(S["u_hi_ready"], 1)

        def gelu(j, s, e):
            wait_job(sc, s * 20 + j)
            sc.wait_ge(S["a_split"], s * 4 + e - 1)
            fn(hidden[:, e % 2, :], ps[:, j % 4, :], ACT.Gelu_apprx_tanh).then_inc(slot_free[j % 4], 1)

        def a_hi_copy(s, e, place):
            sc.wait_ge(S["a_ready"], s * 4 + e + 1)
            fn(a_hi[:, place, e % 2, :], hidden[:, e % 2, :], ACT.Copy).then_inc(S["a_hi_ready"], 1)

        def v_hi_copy(s, e, place=v_hi):
            sc.wait_ge(S["v_in"][e % 2], s * 32 + (e // 2 + 1) * 16)
            fn(place[:, e % 2, :], v_raw[:, e % 2, :], ACT.Copy).then_inc(S["v_hi_ready"], 1)

        def ahead_group(s, k):
            for n in range(GROUP):
                v_hi_copy(s, 2 * k + n, v_hi_odd if k else v_hi)
            for n in range(GROUP):
                a_hi_copy(s, 2 * k + n, k)

        ahead_group(0, 0)
        ahead_group(0, 1)
        with sc.Fori(1, GROUPS_AHEAD // 2) as s:
            for k in range(2):
                wait_job(sc, s * (2 * KC) + (J_AHEAD + KC * k - KC - 1))
                ahead_group(s, k)

        def expert_step(s, k, has_next=True, more_u=True):
            wait_job(sc, s * 20 + (J_STEP + STEP_JOBS * k - 1))
            for n in range(GROUP):
                v_hi_copy(s, 2 * k + n)
            if has_next:
                j = J_STEP + STEP_JOBS * k
                for n in range(GROUP):
                    gelu(j + n, s, 2 * k + 2 + n)
                    if more_u:
                        u_hi_copy(2 * k + 4 + n, n, s)
                for n in range(GROUP):
                    a_hi_copy(s, 2 * k + 2 + n, (k + 1) % 2)

        wait_job(sc, J_EXP - 1)
        u_hi_copy(AHEAD, 0)
        u_hi_copy(AHEAD + 1, 1)
        for n in range(GROUP):
            gelu(J_EXP + n, 0, AHEAD + n)
            u_hi_copy(AHEAD + 2 + n, n)
        for n in range(GROUP):
            a_hi_copy(0, AHEAD + n, 0)
        with sc.Fori(GROUPS_AHEAD // 2, GROUPS // 2 - 1) as s:
            expert_step(s, 0)
            expert_step(s, 1)
        expert_step(GROUPS // 2 - 1, 0, more_u=False)
        expert_step(GROUPS // 2 - 1, 1, has_next=False)
        for c in range(KC):
            wait_read(sc, J_NORM_OUT - KC + c)
            square(act[:, c, :])
        root()

    @block.gpsimd
    def _(pool):
        def wq_lo_sub(n, i=0):
            pool.wait_ge(S["wq_hi_ready"], i * 4 + n + 1)
            nc.gpsimd.tensor_tensor(flat(wq_lo[:, n % 2]), flat(wring[:, (W_ROUTER + n) % 4]), flat(wq_hi[:, n % 2]),
                                    ALU.subtract).then_inc(S["wq_split"], 1)

        def ahead_lo_sub(e, i=0, step=0):
            pool.wait_ge(S["u_hi_ready"], i * step + e + 1)
            nc.gpsimd.tensor_tensor(flat(ahead_lo[:, e % 2]), flat(ahead_raw[:, e % 2]), flat(ahead_hi[:, e % 2]),
                                    ALU.subtract).then_inc(S["u_split"], 1)

        def router_head(i, h, more_w=True):
            if more_w:
                wq_lo_sub(2 * h + 2, i)
                wq_lo_sub(2 * h + 3, i)
            for m in range(4):
                ahead_lo_sub(4 * h + m + 2, i, 8)

        wq_lo_sub(0)
        wq_lo_sub(1)
        ahead_lo_sub(0)
        ahead_lo_sub(1)
        with pool.Fori(0, 3) as i:
            router_head(i, 0)
            router_head(i, 1)
        router_head(3, 0)
        router_head(3, 1, more_w=False)
        with pool.Fori(0, (AHEAD - 34) // 2) as i:
            for k in range(2):
                ahead_lo_sub(34 + k, i, 2)

    @block.vector
    def _(v):
        dv = nc.vector
        step = S["dve_step"]
        chain = {"base": 0, "n": 0}

        def link(ins):
            ins.then_inc(step, 1)
            chain["n"] += 1
            v.wait_ge(step, chain["base"] + chain["n"])

        def enter_loop(i, per):
            chain["base"] = i * per
            return chain["n"] + per

        def leave_loop(end, per, rounds):
            assert chain["n"] == end, (chain["n"], end)
            chain["base"] = 0
            chain["n"] += per * (rounds - 1)

        count = {"norm": 0}

        def rstd_of(j, width):
            wait_job(v, j)
            dv.tensor_scalar(rstd[:], ps[:, j % 4, :], 1.0 / width, EPS, ALU.mult, ALU.add).then_inc(slot_free[j % 4], 1)
            wait_read(v, j)
            dv.reciprocal(rstd[:], rstd[:]).then_inc(S["var_ready"], 1)
            count["norm"] += 1
            v.wait_ge(S["rstd_ready"], count["norm"])

        v.wait_ge(S["consts_in"], 48)
        link(dv.memset(glu[:, :, 0:TAPS - 1], 0.0))
        for k in range(4):
            v.wait_ge(S["x_in"][k], 16)
        rstd_of(J_NORM_X, D)
        for c in range(KC):
            dv.scalar_tensor_tensor(act[:, c, :], region_a[:, c, :], vec[:, V_GMIX + c:V_GMIX + c + 1], rstd[:],
                                    ALU.mult, ALU.mult).then_inc(S["act_ready"], 1)
        j = J_LATENT + 4
        wait_job(v, j)
        dv.tensor_tensor(gate[0:ROPE, 0, :], ps[0:ROPE, j % 4, :], rot[0:ROPE, :], ALU.mult)
        dv.tensor_tensor(gate[0:ROPE, 1, :], ps[ROPE:P, j % 4, :], rot[ROPE:P, :], ALU.mult).then_inc(slot_free[j % 4], 1)
        wait_read(v, j)
        dv.tensor_tensor(k_rope[:], gate[0:ROPE, 0, :], gate[0:ROPE, 1, :], ALU.add).then_inc(S["krope_ready"], 1)
        v.wait_ge(S["krope_ready"], 1)
        v.nop().then_inc(S["gate_used"], 1)
        v.nop().then_inc(S["gate_used"], 1)
        for lat, (j, g) in enumerate(((J_NORM_Q, V_QG), (J_NORM_KV, V_KG))):
            rstd_of(j, LORA)
            for c in range(LC):
                dv.scalar_tensor_tensor(latent[:, 2 * lat + c, :], latent[:, 2 * lat + c, :], vec[:, g + c:g + c + 1],
                                        rstd[:], ALU.mult, ALU.mult).then_inc(S["lat_normed"], 1)
            v.wait_ge(S["lat_normed"], 2 * lat + 2)

        with v.Fori(0, 4) as i:
            end = enter_loop(i, 2 * TAPS)
            for n in range(2):
                j = J_GLU + 2 * n + 1
                wait_job(v, i * 4 + j)
                wait_read(v, j - 1, i)
                dv.tensor_tensor(glu[:, n, TAPS - 1:], ps[:, j % 4, :], gate[:, n, :],
                                 ALU.mult).then_inc(slot_free[j % 4], 1)
                wait_read(v, j, i)
                out = region_b[:, bass.ds(i * 2 + n, 1), :].rearrange("p a t -> p (a t)")

                def tap(k):
                    return vec[:, bass.ds(i * (2 * TAPS) + (V_DW + n * TAPS + k), 1)]

                link(dv.tensor_scalar(out, glu[:, n, 0:T], tap(0), vec[:, bass.ds(i * 2 + (V_DWB + n), 1)],
                                      ALU.mult, ALU.add))
                for k in range(1, TAPS):
                    link(dv.scalar_tensor_tensor(out, glu[:, n, k:k + T], tap(k), out, ALU.mult, ALU.add))
                v.nop().then_inc(S["conv_ready"], 1)
                v.nop().then_inc(S["gate_used"], 1)

        leave_loop(end, 2 * TAPS, 4)

        with v.Fori(0, HEADS) as h:
            end = enter_loop(h, 2 + QT * 2)
            wait_job(v, h * 4 + (J_HEAD + 1))
            dv.scalar_tensor_tensor(gate[0:ROPE, 0, :], ps[0:ROPE, 1, :], SCALE, rot[0:ROPE, :], ALU.mult, ALU.mult)
            link(dv.scalar_tensor_tensor(gate[0:ROPE, 1, :], ps[ROPE:P, 1, :], SCALE, rot[ROPE:P, :],
                                         ALU.mult, ALU.mult))
            link(dv.tensor_tensor(q_rope[:], gate[0:ROPE, 0, :], gate[0:ROPE, 1, :], ALU.add))
            v.nop().then_inc(slot_free[1], 1)

            def row_max(i):
                width = (i + 1) * P
                v.wait_ge(S["s_ready"], h * QT + i + 1)
                link(dv.memset(ps[0:CHUNK, i % 2, width - CHUNK:width], -1e30))
                dv.tensor_reduce(negmax[:, i % 2:i % 2 + 1], ps[:, i % 2, 0:width], AX.X, ALU.max,
                                 negate=True).then_inc(S["max_ready"], 1)

            def normalise(i):
                width = (i + 1) * P
                v.wait_ge(S["exp_ready"], h * QT + i + 1)
                link(dv.reciprocal(expsum[:, i % 2:i % 2 + 1], expsum[:, i % 2:i % 2 + 1]))
                dv.tensor_scalar(probs[:, i % 2, 0:width], probs[:, i % 2, 0:width], expsum[:, i % 2:i % 2 + 1],
                                 None, ALU.mult).then_inc(S["p_ready"], 1)

            row_max(0)
            for i in range(QT):
                if i + 1 < QT:
                    row_max(i + 1)
                normalise(i)

        leave_loop(end, 2 + QT * 2, HEADS)

        wait_job(v, J_LN_MEAN)
        dv.tensor_scalar(gate[:, 0, :], ps[:, J_LN_MEAN % 4, :], 1.0 / D, None,
                         ALU.mult).then_inc(slot_free[J_LN_MEAN % 4], 1)
        wait_read(v, J_LN_MEAN)
        for c in range(KC):
            dv.tensor_tensor(region_b[:, c, :], region_b[:, c, :], gate[:, 0, :], ALU.subtract).then_inc(S["centred"], 1)
        rstd_of(J_LN_VAR, D)
        for c in range(KC):
            dv.tensor_tensor(region_b[:, c, :], region_b[:, c, :], rstd[:], ALU.mult).then_inc(S["ln_ready"], 1)

        with v.Fori(0, 4) as i:
            for n in range(2):
                j = J_CONVOUT + 2 * n + 1
                wait_job(v, i * 4 + j)
                wait_read(v, j - 1, i)
                out = merged[:, bass.ds(i * 2 + n, 1), :].rearrange("p a t -> p (a t)")
                dv.tensor_tensor(out, ps[:, j % 4, :], gate[:, n, :], ALU.mult).then_inc(slot_free[j % 4], 1)
                wait_read(v, j, i)
                v.nop().then_inc(S["gate_used"], 1)
        with v.Fori(0, 4) as i:
            for n in range(2):
                j = J_MLAOUT + 2 * n + 1
                wait_job(v, i * 4 + j)
                wait_read(v, j - 1, i)
                out = merged[:, bass.ds(i * 2 + n, 1), :].rearrange("p a t -> p (a t)")
                dv.tensor_tensor(gate[:, n, :], ps[:, j % 4, :], gate[:, n, :], ALU.mult).then_inc(slot_free[j % 4], 1)
                wait_read(v, j, i)
                dv.tensor_tensor(out, out, gate[:, n, :], ALU.add).then_inc(S["merged_ready"], 1)
                v.wait_ge(S["merged_ready"], i * 2 + n + 1)
                v.nop().then_inc(S["gate_used"], 1)
        v.wait_ge(S["x_again"], 16)
        for c in range(KC):
            j = J_OUT + c
            wait_job(v, j)
            dv.tensor_tensor(act[:, c, :], ps[:, j % 4, :], region_b[:, c, :], ALU.add).then_inc(slot_free[j % 4], 1)
            wait_read(v, j)
            v.nop().then_inc(S["h_ready"], 1)
        rstd_of(J_NORM_H, D)
        for c in range(KC):
            if c >= 2:
                v.wait_ge(S["xhi_ready"], c - 1)
                v.wait_ge(S["xlo_ready"], c - 1)
            dv.scalar_tensor_tensor(gate[:, c % 2, :], act[:, c, :], vec[:, V_GFFN + c:V_GFFN + c + 1], rstd[:],
                                    ALU.mult, ALU.mult).then_inc(S["xn_ready"], 1)
            v.wait_ge(S["xn_ready"], c + 1)
            v.wait_ge(S["xhi_ready"], c + 1)
            dv.tensor_tensor(x_lo[:, c, :], gate[:, c % 2, :], x_hi[:, c, :], ALU.subtract).then_inc(S["xlo_ready"], 1)
        v.wait_ge(S["xlo_ready"], KC)

        def carry_wait():
            carried[0] += 1
            dv.memset(spare[:, carried[0] - 1:carried[0]], 0.0)

        carried = [0]

        def wide(ap, n):
            return ap.unsqueeze(3).to_broadcast([P, QT, TOPK, n])

        def tall(ap, n):
            return ap.unsqueeze(2).to_broadcast([P, QT, n, TOPK])

        iota16 = iota[:, 0:TOPK].unsqueeze(1).unsqueeze(1).to_broadcast([P, QT, TOPK, TOPK])
        with v.Fori(0, HEADS) as h:
            end = enter_loop(h, 25)
            for k in range(2):
                j = J_ROUTER + R_SCORE + k
                wait_job(v, h * R_JOBS + j)
                scores = [ps[:, j % 4, t * P:(t + 1) * P] for t in range(QT)]
                carry_wait()
                for t in range(QT):
                    last = dv.max(best[:, k, t, 0:8], scores[t])
                link(last)
                carry_wait()
                for t in range(QT):
                    dv.max_index(best_key[:, k, t, 0:8], best[:, k, t, 0:8], scores[t])
                for t in range(QT):
                    last = dv.match_replace(rest[:, t, :], best[:, k, t, 0:8], scores[t], -3e38)
                link(last)
                v.nop().then_inc(slot_free[j % 4], 1)
                carry_wait()
                for t in range(QT):
                    last = dv.max(best[:, k, t, 8:16], rest[:, t, :])
                link(last)
                carry_wait()
                for t in range(QT):
                    last = dv.max_index(best_key[:, k, t, 8:16], best[:, k, t, 8:16], rest[:, t, :])
                link(last)
                link(dv.tensor_copy(best_keyf[:, k], best_key[:, k]))
            link(dv.tensor_tensor(cand[:], wide(best[:, 0], TOPK), tall(best[:, 1], TOPK), ALU.add))
            sums = [cand[:, t].rearrange("p a b -> p (a b)") for t in range(QT)]
            sums_rest = [cand_rest[:, t].rearrange("p a b -> p (a b)") for t in range(QT)]
            carry_wait()
            for t in range(QT):
                last = dv.max(top[:, t, 0:8], sums[t])
            link(last)
            carry_wait()
            for t in range(QT):
                dv.max_index(top_pos[:, t, 0:8], top[:, t, 0:8], sums[t])
            for t in range(QT):
                last = dv.match_replace(sums_rest[t], top[:, t, 0:8], sums[t], -3e38)
            link(last)
            carry_wait()
            for t in range(QT):
                last = dv.max(top[:, t, 8:16], sums_rest[t])
            link(last)
            dv.tensor_tensor(shifted[:], top[:], top[:, :, 0:1].to_broadcast([P, QT, TOPK]),
                             ALU.subtract).then_inc(S["shifted_ready"], 1)
            carry_wait()
            for t in range(QT):
                last = dv.max_index(top_pos[:, t, 8:16], top[:, t, 8:16], sums_rest[t])
            link(last)
            dv.tensor_scalar(pos_a[:], top_pos[:], 4, None, ALU.logical_shift_right)
            link(dv.tensor_scalar(pos_b[:], top_pos[:], 15, None, ALU.bitwise_and))
            dv.tensor_copy(pos_af[:], pos_a[:])
            link(dv.tensor_copy(pos_bf[:], pos_b[:]))
            for n, pos in enumerate((pos_af, pos_bf)):
                link(dv.tensor_tensor(pick[:], iota16, wide(pos[:], TOPK), ALU.is_equal))
                link(dv.tensor_tensor(pick[:], pick[:], tall(best_keyf[:, n], TOPK), ALU.mult))
                link(dv.tensor_reduce(sel[:, n, :, bass.ds(h * TOPK, TOPK)], pick[:], AX.X, ALU.add))
            v.wait_ge(S["weight_exp"], h + 1)
            link(dv.tensor_reduce(wsum[:, 0, :], weight[:], AX.X, ALU.add))
            link(dv.reciprocal(wsum[:, 1, :], wsum[:, 0, :]))
            dv.tensor_tensor(sel[:, 2, :, bass.ds(h * TOPK, TOPK)], weight[:],
                             wsum[:, 1, :].unsqueeze(2).to_broadcast([P, QT, TOPK]),
                             ALU.mult).then_inc(S["sel_ready"], 1)
            v.wait_ge(S["sel_ready"], h + 1)

        leave_loop(end, 25, HEADS)

        for n in range(3):
            wait_read(v, J_SEL + n)

        with v.Fori(0, G_BLOCKS // 2) as i:
            for q in range(4):
                for r in range(4):
                    wait_job(v, i * G_JOBS + (J_G + 5 * q + r - (2 if r >= 2 else 3)))
                    for t in range(G_TOK):
                        tok = bass.ds(i * (2 * G_BATCH) + ((4 * q + r) * G_TOK + t), 1)
                        dv.tensor_scalar(hot2[:, r % 2, t, :], iota, selT[:, 1, tok], None, ALU.is_equal)
                        last = dv.tensor_scalar(hot1[:, r % 2, t, :], iota, selT[:, 0, tok], selT[:, 2, tok],
                                                ALU.is_equal, ALU.mult)
                    last.then_inc(S["hot_ready"], 1)

        def u_lo_sub(s, e):
            v.wait_ge(S["u_hi_ready"], s * 4 + e + 1)
            k = e % 2
            dv.tensor_tensor(flat(u_lo[:, k]), flat(u_raw[:, k]), flat(u_hi[:, k]), ALU.subtract).then_inc(S["u_split"], 1)

        def v_lo_sub(s, e, hi=v_hi, lo=v_lo):
            v.wait_ge(S["v_hi_ready"], s * 4 + e + 1)
            dv.tensor_tensor(lo[:, e % 2, :], v_raw[:, e % 2, :], hi[:, e % 2, :],
                             ALU.subtract).then_inc(S["v_split"], 1)

        def weigh(j, s, e):
            if e % 2 == 0:
                v.wait_ge(S["g_in"][(e // 2) % 2], s * 16 + (e // 4 + 1) * 16)
            if j is None:
                v.wait_ge(S["hid_in"][e % 2], s * 32 + (e // 2 + 1) * 16)
            else:
                wait_read(v, j, s * 5)
            h3 = hidden[:, e % 2, :].rearrange("p (b t) -> p b t", t=G_BATCH)
            g3 = g_raw[:, (e // 2) % 2, :, (e % 2) * G_BATCH:(e % 2 + 1) * G_BATCH]
            dv.tensor_tensor(h3, h3, g3, ALU.mult).then_inc(S["a_ready"], 1)

        def a_lo_sub(s, e, slot):
            v.wait_ge(S["a_hi_ready"], s * 4 + e + 1)
            dv.tensor_tensor(a_lo[:, slot, e % 2, :], hidden[:, e % 2, :], a_hi[:, slot, e % 2, :],
                             ALU.subtract).then_inc(S["a_split"], 1)

        def expert_step(s, k, has_next=True, more_u=True, before=STEP_JOBS):
            for n in range(GROUP):
                v_lo_sub(s, 2 * k + n)
            j = J_STEP + STEP_JOBS * k
            if has_next:
                for n in range(GROUP):
                    weigh(j + n, s, 2 * k + 2 + n)
                    if more_u:
                        u_lo_sub(s, 2 * k + 4 + n)
                for n in range(GROUP):
                    a_lo_sub(s, 2 * k + 2 + n, (k + 1) % 2)
                j += GROUP
            accumulate(s, j, STEP_JOBS // 2, before)

        def accumulate(s, j, rounds, before):
            for c in range(KC):
                wait_job(v, s * (rounds * 4) + (j + c))
                if before:
                    wait_read(v, j + c - before, s * rounds)
                dv.tensor_tensor(act[:, c, :], ps[:, (j + c) % 4, :], act[:, c, :],
                                 ALU.add).then_inc(slot_free[(j + c) % 4], 1)

        def ahead_group(s, k):
            for n in range(GROUP):
                v_lo_sub(s, 2 * k + n, v_hi_odd if k else v_hi, v_lo_odd if k else v_lo)
            for n in range(GROUP):
                weigh(None, s, 2 * k + n)
            for n in range(GROUP):
                a_lo_sub(s, 2 * k + n, k)

        ahead_group(0, 0)
        ahead_group(0, 1)
        v.wait_ge(S["h_in"], 16)
        accumulate(0, J_AHEAD, 4, 0)
        with v.Fori(1, GROUPS_AHEAD // 2) as s:
            ahead_group(s, 0)
            accumulate(s, J_AHEAD - KC, 4, KC)
            ahead_group(s, 1)
            accumulate(s, J_AHEAD, 4, KC)
        accumulate(0, J_EXP - KC, 4, KC)
        u_lo_sub(0, AHEAD)
        u_lo_sub(0, AHEAD + 1)
        for n in range(GROUP):
            weigh(J_EXP + n, 0, AHEAD + n)
            u_lo_sub(0, AHEAD + 2 + n)
        for n in range(GROUP):
            a_lo_sub(0, AHEAD + n, 0)
        expert_step(GROUPS_AHEAD // 2, 0, before=STEP_JOBS + GROUP)
        expert_step(GROUPS_AHEAD // 2, 1)
        with v.Fori(GROUPS_AHEAD // 2 + 1, GROUPS // 2 - 1) as s:
            expert_step(s, 0)
            expert_step(s, 1)
        expert_step(GROUPS // 2 - 1, 0, more_u=False)
        expert_step(GROUPS // 2 - 1, 1, has_next=False, before=KC)
        rstd_of(J_NORM_OUT, D)
        for c in range(KC):
            dv.scalar_tensor_tensor(act[:, c, :], act[:, c, :], vec[:, V_GFIN + c:V_GFIN + c + 1], rstd[:],
                                    ALU.mult, ALU.mult).then_inc(S["final_ready"], 1)

    block_cm.__exit__(None, None, None)


def kernel(**inputs):
    import concourse.bacc as bacc
    from concourse import mybir
    from concourse.bass_utils import run_bass_kernel_spmd

    a = {k: np.asarray(x) for k, x in inputs.items()}

    def column_tiles(w):
        k, n = w.shape
        return w.reshape(k // P, P, n // P, P).transpose(2, 1, 0, 3).reshape(n // P, P, k)

    w_in = a["w_in"][0]
    glu_a, glu_b = w_in[:, 0:D], w_in[:, D:2 * D]
    at = 2 * D
    q_lat, kv_lat = w_in[:, at:at + LORA], w_in[:, at + LORA:at + 2 * LORA]
    at += 2 * LORA
    rope = w_in[:, at:at + ROPE]
    at += ROPE
    gate_c, gate_m = w_in[:, at:at + D], w_in[:, at + D:at + 2 * D]

    def swapped(w):
        return np.concatenate([w[:, ROPE // 2:], w[:, :ROPE // 2]], axis=1)

    def in_pairs(first, second):
        return np.stack([column_tiles(first), column_tiles(second)], axis=1).reshape(16, P, D)

    wproj = np.concatenate([
        column_tiles(q_lat), column_tiles(kv_lat), column_tiles(np.concatenate([rope, swapped(rope)], axis=1)),
        in_pairs(glu_b, glu_a), in_pairs(gate_c, a["conv_w_pw"][0]), in_pairs(gate_m, a["mla_w_o"][0]),
        column_tiles(a["w_out"][0]), column_tiles(a["peer_w_q"][0])])
    heads = []
    for h in range(HEADS):
        q = a["w_q_up"][0][:, h * (NOPE + ROPE):(h + 1) * (NOPE + ROPE)]
        kv = a["w_kv_up"][0][:, h * (NOPE + VDIM):(h + 1) * (NOPE + VDIM)]
        w = np.concatenate([q[:, :NOPE], q[:, NOPE:], swapped(q[:, NOPE:]), kv], axis=1)
        heads.append(w.reshape(LC, P, 512).transpose(1, 0, 2).reshape(P, LC * 512))
    keysT = a["peer_sub_keys"][0].transpose(3, 0, 1, 2).reshape(P, 16, KEYS)
    uT = a["peer_u"][0].reshape(EXPERT_TILES, P, KC, P).transpose(0, 3, 2, 1).reshape(EXPERT_TILES, P, D)
    vtab = a["peer_v"][0].reshape(EXPERT_TILES, P, D)

    def cols(x):
        return x.reshape(-1, P).T

    dw = a["conv_dw"][0].reshape(TAPS, KC, P).transpose(2, 1, 0).reshape(P, KC * TAPS)
    vecs = np.concatenate([cols(a["norm_mix_g"][0]), cols(a["b_gate"][0, 0]), cols(a["b_gate"][0, 1]),
                           cols(a["conv_dw_b"][0]), cols(a["conv_ln_g"][0]), cols(a["conv_ln_b"][0]),
                           cols(a["q_norm_g"][0]), cols(a["kv_norm_g"][0]), cols(a["norm_ffn_g"][0]),
                           cols(a["norm_final_g"]), dw], axis=1)
    tables = np.stack([np.ones((P, P)), np.eye(P), np.broadcast_to(np.arange(P), (P, P))], axis=1).astype(np.float32)
    freq = np.float32(THETA) ** (-np.arange(0, ROPE, 2, dtype=np.float32) / np.float32(ROPE))
    angle = freq[:, None] * np.arange(T, dtype=np.float32)[None, :]
    rotary = np.concatenate([np.cos(angle), np.cos(angle), -np.sin(angle), np.sin(angle)]).astype(np.float32)

    arrays = dict(xT=a["x"][0].T.reshape(KC, P, T).transpose(1, 0, 2), wproj=wproj, whead=np.stack(heads),
                  keysT=keysT, uT=uT, vtab=vtab, vecs=vecs, tables=tables, rotary=rotary)
    arrays = {k: np.ascontiguousarray(x) for k, x in arrays.items()}
    nc = bacc.Bacc("TRN2", target_bir_lowering=False, num_devices=1)
    args = [nc.dram_tensor(k, x.shape, mybir.dt.float32, kind="ExternalInput").ap() for k, x in arrays.items()]
    args.append(nc.dram_tensor("outT", (P, KC, T), mybir.dt.float32, kind="ExternalOutput").ap())
    build(nc, *args)
    got = run_bass_kernel_spmd(nc, [arrays], core_ids=[0]).results[0]["outT"]
    return np.ascontiguousarray(got.transpose(2, 1, 0).reshape(1, T, D))
```

```python
import math

import numpy as np

P = 128
D = 1024
T = 1024
KC = D // P
HALF = 512
TAPS = 31
HEADS = 8
NOPE, ROPE, VDIM = 128, 64, 128
LORA = 256
LC = LORA // P
QT = T // P
CHUNK = 64
KEYS = 128
TOPK = 16
EXPERT_TILES = 128
EPS = 1e-6
SCALE = 1.0 / math.sqrt(NOPE + ROPE)
THETA = 10000.0

W_LATENT = 0
W_GLU = 5
W_GATE = W_GLU + 16
W_MLAOUT = W_GATE + 16
W_CONVOUT = W_MLAOUT + 8
W_OUT = W_CONVOUT + 8
W_ROUTER = W_OUT + 8

J_NORM_X = 0
J_LATENT = 1
J_NORM_Q = 6
J_NORM_KV = 7
J_GLU = 8
J_GATE = J_GLU + 16
J_LN_MEAN = J_GATE + 16
J_MLAOUT = J_LN_MEAN + 1
J_LN_VAR = J_MLAOUT + 4
J_CONVOUT = J_LN_VAR + 5
J_OUT = J_CONVOUT + 8
J_NORM_H = J_OUT + 8
J_ROUTER = J_NORM_H + 1
R_JOBS = 8
R_QUERY, R_SCORE, R_HIDDEN = 0, 3, (2, 5, 6, 7)
ROUTER_AHEAD = 34
J_SEL = J_ROUTER + 8 * R_JOBS + 2
J_G = J_SEL + 3
G_TOK = 8
G_BATCH = 64
G_BLOCKS = T // G_BATCH
G_JOBS = 20
GROUP = 2
GROUPS = EXPERT_TILES // GROUP
AHEAD = ROUTER_AHEAD + 2 * G_BLOCKS + 2
GROUPS_AHEAD = AHEAD // GROUP
J_BEHIND_G = J_G + G_BLOCKS // 2 * G_JOBS
J_AHEAD = J_BEHIND_G + 2
STEP_JOBS = GROUP + KC
J_EXP = J_AHEAD + GROUPS_AHEAD * KC
J_STEP = J_EXP + GROUP - STEP_JOBS * GROUPS_AHEAD
J_NORM_OUT = J_EXP + (GROUPS - GROUPS_AHEAD) * STEP_JOBS

FIRST_HEAD = (2, 3, 4, 5, 0, 1, 6, 7)
W_SHIFT = 2.0 ** 15

V_GMIX, V_BM, V_BC, V_DWB, V_LNG, V_LNB, V_QG, V_KG, V_GFFN, V_GFIN = 0, 8, 16, 24, 32, 40, 48, 50, 52, 60
V_DW = 68
V_COLS = V_DW + KC * TAPS


def build(nc, xT, wproj, whead, keysT, uT, vtab, vecs, tables, rotary, outT):
    import concourse.bass as bass
    from concourse import mybir

    f32, f32r, f16, u32 = mybir.dt.float32, mybir.dt.float32r, mybir.dt.float16, mybir.dt.uint32
    ALU, ACT, AX = mybir.AluOpType, mybir.ActivationFunctionType, mybir.AxisListType
    mm = nc.tensor.matmul

    base = (nc.sbuf_base + 31) // 32 * 32

    def at(name, shape, kib, dt=f32):
        return nc.alloc_sbuf_tensor_at(name, shape, dt, offset=base + int(kib * 1024))

    in_hi = at("in_hi", [P, KC, T], 0, f32r)
    in_lo = at("in_lo", [P, KC, T], 32, f32r)
    act = at("act", [P, KC, T], 0)
    raw = at("raw", [P, KC, T], 64)
    PAD = TAPS - 1
    conv = at("conv", [P, KC, PAD + T], 64)
    merged = at("merged", [P, KC, T], 97)
    m_hi = at("m_hi", [P, KC, T], 64, f32r)
    m_lo = at("m_lo", [P, KC, T], 97, f32r)
    q_nope = at("q_nope", [P, 2, T], 97)
    k_nope = at("k_nope", [P, 2, T], 105)
    probs = at("probs", [P, 2, T], 113)
    probsT = at("probsT", [P, 2, QT, P], 121)
    turned = at("turned", [ROPE, 2, HALF], 169)
    q_rope = at("q_rope", [ROPE, 2, T], 173)
    v_head = at("v_head", [P, 2, QT, VDIM], 189)
    hw_q = at("hw_q", [P, LC, 2 * P], 197.5)
    hw_kv = at("hw_kv", [P, LC, 2 * P], 199.5)
    w1_hi = at("w1_hi", [P, 2, KC, P], 113, f32r)
    w1_lo = at("w1_lo", [P, 2, KC, P], 121, f32r)
    w2_hi = at("w2_hi", [P, 2, KC, P], 145, f32r)
    w2_lo = at("w2_lo", [P, 2, KC, P], 153, f32r)
    wring = at("wring", [P, 4, KC, P], 129)
    latent = at("latent", [P, 4, T], 145)
    k_rope = at("k_rope", [ROPE, T], 161)
    rot = at("rot", [P, T], 165)
    total = at("total", [P, T], 161)
    rstd = at("rstd", [P, T], 169)
    squares = at("squares", [P, 2, T], 173)
    gate = at("gate", [P, 2, T], 181)
    normed = at("normed", [P, 4, T], 181)
    conv_sum = at("conv_sum", [P, 2, T], 189)
    tabs = at("tabs", [P, 3, P], 201.5)
    vec = at("vec", [P, V_COLS], 203)
    negmax = at("negmax", [P, 2], 204.5)
    expsum = at("expsum", [P, 2], 204.625)
    spare = at("spare", [P, 32], 204.75)
    ones, ident, iota = tabs[:, 0, :], tabs[:, 1, :], tabs[:, 2, :]
    x_hi = at("x_hi", [P, KC, T], 32, f32r)
    x_lo = at("x_lo", [P, KC, T], 64, f32r)
    wq_hi = at("wq_hi", [P, 2, KC, P], 97, f32r)
    wq_lo = at("wq_lo", [P, 2, KC, P], 105, f32r)
    query = at("query", [P, 2, T], 113)
    keys = at("keys", [P, 16, KEYS], 121)
    best = at("best", [P, 2, QT, TOPK], 145)
    best_key = at("best_key", [P, 2, QT, TOPK], 146, u32)
    best_keyf = at("best_keyf", [P, 2, QT, TOPK], 147)
    rest = at("rest", [P, QT, KEYS], 149)
    cand = at("cand", [P, QT, TOPK, TOPK], 153)
    cand_rest = at("cand_rest", [P, QT, TOPK, TOPK], 161)
    pick = at("pick", [P, QT, TOPK, TOPK], 173)
    top = at("top", [P, QT, TOPK], 181)
    top_pos = at("top_pos", [P, QT, TOPK], 181.5, u32)
    pos_a = at("pos_a", [P, QT, TOPK], 182, u32)
    pos_b = at("pos_b", [P, QT, TOPK], 182.5, u32)
    pos_af = at("pos_af", [P, QT, TOPK], 183)
    pos_bf = at("pos_bf", [P, QT, TOPK], 183.5)
    shifted = at("shifted", [P, QT, TOPK], 184)
    weight = at("weight", [P, QT, TOPK], 184.5)
    wsum = at("wsum", [P, 2, QT], 185)
    sel = at("sel", [P, 3, QT, P], 189)
    selT = at("selT", [P, 2, T], 97)
    w16 = at("w16", [P, 2, T], 105, f16)
    hot2 = at("hot2", [P, 2, G_TOK, P], 109, f16)
    hot1 = at("hot1", [P, 2, G_TOK, P], 113, f16)
    hot1_hi = at("hot1_hi", [P, 2, G_TOK, P], 117, f16)
    hot1_lo = at("hot1_lo", [P, 2, G_TOK, P], 121, f16)
    gblock = at("gblock", [P, 2, P, G_BATCH], 125)
    a_hi = at("a_hi", [P, 2, GROUP, T], 97, f32r)
    a_lo = at("a_lo", [P, 2, GROUP, T], 113, f32r)
    v_hi = at("v_hi", [P, GROUP, D], 129, f32r)
    v_lo = at("v_lo", [P, GROUP, D], 137, f32r)
    v_raw = at("v_raw", [P, 2, D], 145)
    u_raw = at("u_raw", [P, 2, KC, P], 153)
    u_hi = at("u_hi", [P, 2, KC, P], 161, f32r)
    u_lo = at("u_lo", [P, 2, KC, P], 169, f32r)
    g_raw = at("g_raw", [P, 2, G_BLOCKS, GROUP * G_BATCH], 177)
    hidden = at("hidden", [P, 2, T], 193)
    v_hi_odd = at("v_hi_odd", [P, GROUP, D], 161, f32r)
    v_lo_odd = at("v_lo_odd", [P, GROUP, D], 169, f32r)
    ahead_raw = at("ahead_raw", [P, 2, KC, P], 0)
    ahead_hi = at("ahead_hi", [P, 2, KC, P], 8, f32r)
    ahead_lo = at("ahead_lo", [P, 2, KC, P], 16, f32r)
    ahead_out = at("ahead_out", [P, 2, T], 24)

    g_dram = nc.dram_tensor("g_dram", [G_BLOCKS, P, P * G_BATCH], f32).ap()
    h_dram = nc.dram_tensor("h_dram", [P, KC, T], f32).ap()
    gate_dram = nc.dram_tensor("gate_dram", [16, P, T], f32).ap()
    ahead_dram = nc.dram_tensor("ahead_dram", [AHEAD, P, T], f32).ap()
    ps = nc.alloc_psum_tensor("ps", [P, 4, T], f32)

    names = dict(
        tabs_in=1, vec_in=1, rot_in=1, x_in=4, x_again=4, w_in=4, hw_q_in=1, hw_kv_in=1, unit_done=1, unit_read=1, q_rope_ready=1, keys_in=1, u_in=2, v_in=2, g_in=2, g_out=2, y_out=1, h_out=1, h_in=4, ahead_out=2, hid_in=2,
        job_done=1, slot_free=4,
        sq_ready=1, sq_used=1, add_done=1, var_ready=1, rstd_ready=1,
        lat_normed=1, krope_ready=1,
        w_hi_ready=1, w_split=1, gate_out=2, gate_in=2, gate_used=1, u_ready=1, conv_ready=1,
        s_ready=1, max_ready=1, exp_ready=1, p_ready=1, pt_ready=1, pt_copied=1, pv_done=1, o_copied=1, o_split=1,
        centred=1, ln_ready=1, silu_ready=1, y_hi_ready=1, y_split=1, merged_ready=1, m_hi_ready=1, m_split=1, h_ready=1,
        xn_ready=1, xhi_ready=1, xlo_even=1, xlo_odd=1, wq_hi_ready=1, wq_split=1,
        shifted_ready=1, weight_exp=1, sel_ready=1, selT_ready=1, w_hi16_ready=1, w_lo16_ready=1, hot1_ready=1, hot_ready=1, hot_lo_ready=1,
        a_ready=1, a_hi_ready=1, a_split=1, u_hi_ready=1, u_split=1, v_hi_ready=1, v_split=1,
        final_ready=1, dve_step=1)
    S = {}
    for name, n in names.items():
        made = [nc.alloc_semaphore(f"{name}{k}" if n > 1 else name) for k in range(n)]
        S[name] = made if n > 1 else made[0]
    job_done, slot_free = S["job_done"], S["slot_free"]

    def wait_job(eng, j):
        eng.wait_ge(job_done, j + 1)

    def wait_slot(eng, j, rounds=0):
        eng.wait_ge(slot_free[j % 4], rounds + j // 4)

    def wait_read(eng, j, rounds=0):
        eng.wait_ge(slot_free[j % 4], rounds + (j // 4 + 1))

    def flat(ap):
        return ap.rearrange("p a b -> p (a b)")

    def w_split_place(w):
        hi, lo = (w1_hi, w1_lo) if w < W_MLAOUT else (w2_hi, w2_lo)
        return hi[:, w % 2], lo[:, w % 2]

    def token_weights(part, i, n):
        tok = bass.ds(i * (2 * G_BATCH) + n * G_TOK, G_TOK)
        return w16[:, part, tok].unsqueeze(2).to_broadcast([P, G_TOK, P])

    block_cm = nc.Block()
    block = block_cm.__enter__()

    @block.sync
    def _(sp):
        sp.dma_start(tabs[:], tables).then_inc(S["tabs_in"], 16)
        for k in range(4):
            sp.dma_start(raw[:, 2 * k:2 * k + 2, :], xT[:, 2 * k:2 * k + 2, :]).then_inc(S["x_in"][k], 16)
        sp.dma_start(vec[:], vecs).then_inc(S["vec_in"], 16)
        for k in range(4):
            if k == 2:
                sp.dma_start(rot[:], rotary).then_inc(S["rot_in"], 16)
            sp.dma_start(flat(wring[:, k]), wproj[k]).then_inc(S["w_in"][k], 16)

        def load_w(w, i=0):
            sp.dma_start(flat(wring[:, w % 4]), wproj[i * 4 + w]).then_inc(S["w_in"][w % 4], 16)

        def next_w(w, i=0):
            sp.wait_ge(S["w_split"], i * 4 + (w - 3))
            load_w(w, i)

        sp.dma_start(flat(hw_q[:]), whead[0, 0]).then_inc(S["hw_q_in"], 16)
        sp.dma_start(flat(hw_kv[:]), whead[0, 1]).then_inc(S["hw_kv_in"], 16)
        with sp.Fori(0, 5) as i:
            for w in range(4, 8):
                next_w(w, i)
        for w in range(24, W_GATE + 6):
            next_w(w)

        def gate_store(k, i=0, more=True):
            wait_read(sp, J_GATE + k, i)
            sp.dma_start(gate_dram[i * 4 + k], gate[:, k % 2]).then_inc(S["gate_out"][k % 2], 16)
            if more:
                next_w(W_GATE + k + 6, i)

        with sp.Fori(0, 3) as i:
            for k in range(4):
                gate_store(k, i)
        for k in range(12, 16):
            gate_store(k, more=k < 14)

        def load_gate(n, i=0):
            sp.dma_start(gate[:, n % 2], gate_dram[i * 4 + n]).then_inc(S["gate_in"][n % 2], 16)

        sp.wait_ge(S["gate_out"][0], 16 * 8)
        load_gate(0)
        with sp.Fori(1, HEADS) as h:
            sp.wait_ge(S["unit_done"], h * 8 - 2)
            sp.dma_start(flat(hw_q[:]), whead[h, 0]).then_inc(S["hw_q_in"], 16)
            sp.wait_ge(S["unit_done"], h * 8)
            sp.dma_start(flat(hw_kv[:]), whead[h, 1]).then_inc(S["hw_kv_in"], 16)
        wait_job(sp, J_LN_MEAN)
        load_gate(1)

        def branch_loads(m, i=0):
            next_w(W_MLAOUT + 4 + m, i)
            if m >= 2:
                sp.wait_ge(S["gate_used"], i * 4 + m - 1)
                load_gate(m, i)

        for m in range(4):
            branch_loads(m)
        with sp.Fori(0, 3) as i:
            for m in range(4, 8):
                branch_loads(m, i)
        next_w(W_OUT + 4)
        next_w(W_OUT + 5)
        wait_job(sp, J_OUT - 1)
        for k in range(4):
            sp.dma_start(act[:, 2 * k:2 * k + 2, :], xT[:, 2 * k:2 * k + 2, :]).then_inc(S["x_again"][k], 16)
        for w in range(W_OUT + 6, W_OUT + 12):
            next_w(w)
        wait_job(sp, J_NORM_H - 1)
        sp.dma_start(keys[:], keysT).then_inc(S["keys_in"], 16)
        sp.wait_ge(S["xn_ready"], 2 * KC)
        sp.dma_start(h_dram, act[:]).then_inc(S["h_out"], 16)
        sp.wait_ge(S["h_out"], 16)

        def load_ahead(n, i=0, step=0):
            sp.dma_start(flat(ahead_raw[:, n % 2]), uT[i * step + n]).then_inc(S["u_in"][n % 2], 16)

        def tile_ahead(n, j, i=0, step=0, jstep=0, more=True, between=None):
            if more:
                sp.wait_ge(S["u_split"], i * step + (n + 1))
                load_ahead(n + 2, i, step)
            if between:
                between()
            wait_read(sp, j, i * (jstep // 4))
            sp.dma_start(ahead_dram[i * step + n], ahead_out[:, n % 2]).then_inc(S["ahead_out"][n % 2], 16)

        load_ahead(0)
        load_ahead(1)

        def router_loads(i, h, more_w=True):
            if more_w:
                for k in range(2):
                    sp.wait_ge(S["wq_split"], i * 4 + (2 * h + k + 1))
                    load_w(W_ROUTER + 4 + 2 * h + k, i)
            for m in range(4):
                tile_ahead(4 * h + m, J_ROUTER + R_JOBS * h + R_HIDDEN[m], i, 8, 2 * R_JOBS)

        with sp.Fori(0, 3) as i:
            router_loads(i, 0)
            router_loads(i, 1)
        router_loads(3, 0, more_w=False)
        router_loads(3, 1, more_w=False)

        for m in range(2):
            tile_ahead(ROUTER_AHEAD - 2 + m, J_SEL - 2 + m)

        def g_loads(i):
            for q in range(4):
                def g_store():
                    wait_read(sp, J_G + 5 * q + 3, i * (G_JOBS // 4))
                    sp.dma_start(g_dram[i * 2 + q // 2],
                                 gblock[:, q // 2].rearrange("p a t -> p (a t)")).then_inc(S["g_out"][q // 2], 16)
                tile_ahead(ROUTER_AHEAD + q, J_G + 5 * q + 4, i, 4, G_JOBS, between=g_store if q % 2 else None)

        with sp.Fori(0, G_BLOCKS // 2) as i:
            g_loads(i)
        for k in range(2):
            sp.wait_ge(S["g_out"][k], 16 * G_BLOCKS // 2)
            sp.wait_ge(S["ahead_out"][k], 16 * (AHEAD // 2 - 1))

        def load_u(e, k):
            sp.dma_start(flat(u_raw[:, k]), uT[e]).then_inc(S["u_in"][k], 16)

        def load_v(e, k):
            sp.dma_start(v_raw[:, k], vtab[e]).then_inc(S["v_in"][k], 16)

        def load_g(g, k):
            cols = g_dram.rearrange("b p (g c) -> g p b c", c=GROUP * G_BATCH)
            sp.dma_start(g_raw[:, k], cols[g]).then_inc(S["g_in"][k], 16)

        def ahead_v_g_loads(s, k, first=False):
            for n in range(GROUP):
                if not first:
                    sp.wait_ge(S["v_split"], s * 4 + 2 * k - 1 + n)
                load_v(s * 4 + (2 * k + n), n)
            if not isinstance(s, int):
                sp.wait_ge(S["a_ready"], s * 4 + 2 * k - 2)
            load_g(s * 2 + k, k)

        def hidden_loads(s, k, first=False):
            for n in range(GROUP):
                if not first:
                    sp.wait_ge(S["a_split"], s * 4 + 2 * k - 1 + n)
                sp.dma_start(hidden[:, n], ahead_dram[s * 4 + (2 * k + n)]).then_inc(S["hid_in"][n], 16)

        ahead_v_g_loads(0, 0, first=True)
        hidden_loads(0, 0, first=True)
        ahead_v_g_loads(0, 1)
        for m in range(2):
            tile_ahead(AHEAD - 2 + m, J_BEHIND_G + m, more=False)
        for k in range(2):
            sp.wait_ge(S["ahead_out"][k], 16 * AHEAD // 2)
        hidden_loads(0, 1)
        for k in range(4):
            sp.dma_start(act[:, 2 * k:2 * k + 2, :], h_dram[:, 2 * k:2 * k + 2, :]).then_inc(S["h_in"][k], 16)
        with sp.Fori(1, GROUPS_AHEAD // 2) as s:
            for k in range(2):
                ahead_v_g_loads(s, k)
                hidden_loads(s, k)

        def expert_loads(s, k, more_u=True, more_g=True):
            for n in range(GROUP):
                sp.wait_ge(S["v_split"], s * 4 + 2 * k - 1 + n)
                load_v(s * 4 + (2 * k + n), n)
            if more_g:
                sp.wait_ge(S["a_ready"], s * 4 + 2 * k)
                load_g(s * 2 + (k + 1), (k + 1) % 2)
            if more_u:
                for n in range(GROUP):
                    sp.wait_ge(S["u_split"], s * 4 + 2 * k + 3 + n)
                    load_u(s * 4 + (2 * k + 4 + n), n)

        load_u(AHEAD, 0)
        load_u(AHEAD + 1, 1)
        sp.wait_ge(S["a_ready"], AHEAD - GROUP)
        load_g(GROUPS_AHEAD, 0)
        for n in range(GROUP):
            sp.wait_ge(S["u_split"], AHEAD + n + 1)
            load_u(AHEAD + 2 + n, n)
        with sp.Fori(GROUPS_AHEAD // 2, GROUPS // 2 - 1) as s:
            expert_loads(s, 0)
            expert_loads(s, 1)
        expert_loads(GROUPS // 2 - 1, 0, more_u=False)
        expert_loads(GROUPS // 2 - 1, 1, more_u=False, more_g=False)

        for c in range(KC):
            sp.wait_ge(S["final_ready"], c + 1)
            sp.dma_start(outT[:, c, :], act[:, c, :]).then_inc(S["y_out"], 16)
        sp.wait_ge(S["y_out"], 16 * KC)

    @block.tensor
    def _(pe):
        used = {"sq": 0}

        def three_passes(out, hi, lo, m_hi, m_lo, first, last_one):
            mm(out, hi, m_hi, start=first, stop=False)
            mm(out, hi, m_lo, start=False, stop=False)
            return mm(out, lo, m_hi, start=False, stop=last_one)

        def project(j, w, in_hi, in_lo, i=0, by_chunk=None):
            wait_slot(pe, j, i)
            pe.wait_ge(S["w_split"], i * 4 + (w + 1))
            hi, lo = w_split_place(w)
            for half in range(2):
                cols = slice(half * HALF, (half + 1) * HALF)
                for c in range(KC):
                    if by_chunk and half == 0:
                        pe.wait_ge(by_chunk, c + 1)
                    last = three_passes(ps[:, j % 4, cols], hi[:, c, :], lo[:, c, :], in_hi[:, c, cols],
                                        in_lo[:, c, cols], c == 0, c == KC - 1)
            last.then_inc(job_done, 1)

        def ones_sum(j, tiles):
            if j >= 4:
                wait_slot(pe, j)
            for n, (ready, tile) in enumerate(tiles):
                pe.wait_ge(S["sq_ready"], ready)
                for half in range(2):
                    cols = slice(half * HALF, (half + 1) * HALF)
                    last = mm(ps[:, j % 4, cols], ones, tile[:, cols], start=n == 0, stop=n == len(tiles) - 1,
                              skip_group_check=True)
                last.then_inc(S["sq_used"], 1)
            pe.wait_ge(S["sq_used"], used["sq"])
            pe.nop().then_inc(job_done, 1)

        def total_sum(j, adds, tile):
            wait_slot(pe, j)
            pe.wait_ge(S["add_done"], adds)
            for half in range(2):
                cols = slice(half * HALF, (half + 1) * HALF)
                last = mm(ps[:, j % 4, cols], ones, tile[:, cols], start=True, stop=True)
            last.then_inc(job_done, 1)

        def square_tiles(n):
            first = used["sq"]
            used["sq"] += n
            return [(k + 1, squares[:, k % 2, :]) for k in range(first, first + n)]

        def wait_chunk(c, first=0):
            pe.wait_ge(S["xlo_odd" if c % 2 else "xlo_even"], first // 2 + c // 2 + 1)

        pe.wait_ge(S["tabs_in"], 16)
        ones_sum(J_NORM_X, square_tiles(KC))
        for k in range(5):
            j, w = J_LATENT + k, W_LATENT + k
            if j >= 4:
                wait_slot(pe, j)
            pe.wait_ge(S["w_split"], w + 1)
            hi, lo = w_split_place(w)
            for half in range(2):
                cols = slice(half * HALF, (half + 1) * HALF)
                for c in range(KC):
                    if k == 0 and half == 0:
                        wait_chunk(c)
                    last = three_passes(ps[:, j % 4, cols], hi[:, c, :], lo[:, c, :], in_hi[:, c, cols],
                                        in_lo[:, c, cols], c == 0, c == KC - 1)
            last.then_inc(job_done, 1)
        ones_sum(J_NORM_Q, square_tiles(LC))
        ones_sum(J_NORM_KV, square_tiles(LC))

        with pe.Fori(0, 8) as i:
            for k in range(4):
                project(J_GLU + k, W_GLU + k, in_hi, in_lo, i)

        unit_bank, out_bank = ps[:, 3, 0:HALF], ps[:, 3, HALF:T]

        def unit(s, par, u, place=None):
            if place != 0:
                pe.wait_ge(S["unit_read"], s * 16 + (par * 8 + (u if place is None else place)))
            if u == 0 or place == 0:
                pe.wait_ge(S["hw_q_in"], s * 32 + (par + 1) * 16)
            if u == 4:
                pe.wait_ge(S["hw_kv_in"], s * 32 + (par + 1) * 16)
            half = u % 2
            if u < 6:
                w, first, tile = ((hw_q, P, 0), (hw_q, 0, 0), (hw_kv, 0, 2))[u // 2]
                for c in range(LC):
                    last = mm(unit_bank, w[:, c, first:first + P], latent[:, tile + c, half * HALF:(half + 1) * HALF],
                              start=c == 0, stop=c == LC - 1)
            else:
                for t in range(QT // 2):
                    tok = slice(half * HALF + t * P, half * HALF + (t + 1) * P)
                    for c in range(LC):
                        last = mm(unit_bank[:, t * P:(t + 1) * P], latent[:, 2 + c, tok], hw_kv[:, c, P:2 * P],
                                  start=c == 0, stop=c == LC - 1)
            last.then_inc(S["unit_done"], 1)

        def scores(s, par, i):
            if i == 0:
                pe.wait_ge(S["unit_read"], s * 16 + (par * 8 + 6))
                pe.wait_ge(S["q_rope_ready"], s * 4 + (par * 2 + 2))
            rows = slice(i * P, (i + 1) * P)
            width = (i + 1) * P
            for c0 in range(0, width, HALF):
                cols = slice(c0, min(width, c0 + HALF))
                mm(ps[:, i % 2, cols], q_nope[:, par, rows], k_nope[:, par, cols], start=True, stop=False)
                last = mm(ps[:, i % 2, cols], q_rope[:, par, rows], k_rope[:, cols], start=False, stop=True)
            last.then_inc(S["s_ready"], 1)

        def attention_step(s, par, i, has_next=True):
            n = s * 16 + (par * 8 + i)
            pe.wait_ge(S["p_ready"], n + 1)
            pe.wait_ge(S["pt_copied"], n + 1)
            for b in range(i + 1):
                last = nc.tensor.transpose(ps[:, 2, b * P:(b + 1) * P], probs[:, i % 2, b * P:(b + 1) * P], ident)
            last.then_inc(S["pt_ready"], 1)
            following = (s, 1) if par == 0 else (s + 1, 0)
            if i + 2 < QT:
                scores(s, par, i + 2)
            elif has_next:
                scores(*following, i + 2 - QT)
            if has_next:
                unit(*following, i)
            if i == 0:
                pe.wait_ge(S["unit_read"], s * 16 + (par * 8 + 8))
            if i % 4 == 0:
                pe.wait_ge(S["o_split"], s * 4 + (par * 2 + i // 4 + 1))
            pe.wait_ge(S["pt_copied"], n + 2)
            for b in range(i + 1):
                last = mm(out_bank[:, (i % 4) * P:(i % 4 + 1) * P], v_head[:, par, b, :], probsT[:, i % 2, b, :],
                          start=b == 0, stop=b == i)
            last.then_inc(S["pv_done"], 1)

        pe.wait_ge(S["lat_normed"], 4)
        pe.wait_ge(S["krope_ready"], 1)
        for j in range(J_LN_MEAN - 4, J_LN_MEAN):
            wait_read(pe, j)
        for place, u in enumerate(FIRST_HEAD):
            unit(0, 0, u, place)
        scores(0, 0, 0)
        scores(0, 0, 1)
        with pe.Fori(0, HEADS // 2 - 1) as s:
            for par in range(2):
                for i in range(QT):
                    attention_step(s, par, i)
        for par in range(2):
            for i in range(QT):
                attention_step(HEADS // 2 - 1, par, i, has_next=par == 0)

        total_sum(J_LN_MEAN, KC - 1, gate[:, 1, :])
        pe.wait_ge(S["o_split"], 2 * HEADS + 1)
        for c in range(4):
            project(J_MLAOUT + c, W_MLAOUT + c, in_hi, in_lo)
        total_sum(J_LN_VAR, 2 * (KC - 1), total)
        for c in range(4, KC):
            project(J_MLAOUT + c + 1, W_MLAOUT + c, in_hi, in_lo)
        with pe.Fori(0, 2) as i:
            for k in range(4):
                project(J_CONVOUT + k, W_CONVOUT + k, in_hi, in_lo, i, S["y_split"] if k == 0 else None)
        with pe.Fori(0, 2) as i:
            for k in range(4):
                project(J_OUT + k, W_OUT + k, m_hi, m_lo, i, S["m_split"] if k == 0 else None)
        total_sum(J_NORM_H, 3 * (KC - 1), total)

        def hidden_half(j, hi, lo, half, by_chunk=False):
            cols = slice(half * HALF, (half + 1) * HALF)
            for c in range(KC):
                if by_chunk:
                    wait_chunk(c, KC)
                last = three_passes(ps[:, j % 4, cols], hi[:, c, :], lo[:, c, :],
                                    x_hi[:, c, cols], x_lo[:, c, cols], c == 0, c == KC - 1)
            return last

        pe.wait_ge(S["keys_in"], 16)
        with pe.Fori(0, HEADS) as h:
            def queries(k):
                j = J_ROUTER + R_QUERY + k
                wait_slot(pe, j, h * 2)
                pe.wait_ge(S["wq_split"], h * 2 + k + 1)
                for half in range(2):
                    last = hidden_half(j, wq_hi[:, k], wq_lo[:, k], half, by_chunk=k + half == 0)
                last.then_inc(job_done, 1)

            def key_scores(k):
                j = J_ROUTER + R_SCORE + k
                wait_slot(pe, j, h * 2)
                wait_read(pe, J_ROUTER + R_QUERY + k, h * 2)
                for t in range(QT):
                    last = mm(ps[:, j % 4, t * P:(t + 1) * P], query[:, k, t * P:(t + 1) * P],
                              keys[:, bass.ds(h * 2 + k, 1), :].rearrange("p a k -> p (a k)"), start=True, stop=True)
                last.then_inc(job_done, 1)

            def hidden_ahead(m):
                j = J_ROUTER + R_HIDDEN[m]
                wait_slot(pe, j, h * 2)
                pe.wait_ge(S["u_split"], h * 4 + m + 1)
                for half in range(2):
                    last = hidden_half(j, ahead_hi[:, m % 2], ahead_lo[:, m % 2], half)
                last.then_inc(job_done, 1)

            queries(0)
            queries(1)
            hidden_ahead(0)
            key_scores(0)
            key_scores(1)
            hidden_ahead(1)
            hidden_ahead(2)
            hidden_ahead(3)

        def hidden_single(j, n):
            wait_slot(pe, j)
            pe.wait_ge(S["u_split"], n + 1)
            for half in range(2):
                last = hidden_half(j, ahead_hi[:, n % 2], ahead_lo[:, n % 2], half)
            last.then_inc(job_done, 1)

        for m in range(2):
            hidden_single(J_SEL - 2 + m, ROUTER_AHEAD - 2 + m)
        pe.wait_ge(S["sel_ready"], HEADS)
        for n in range(3):
            j = J_SEL + n
            wait_slot(pe, j)
            for t in range(QT):
                last = nc.tensor.transpose(ps[:, j % 4, t * P:(t + 1) * P], sel[:, n, t, :], ident)
            last.then_inc(job_done, 1)

        with pe.Fori(0, G_BLOCKS // 2) as i:
            for q in range(4):
                def g_job(r):
                    j = J_G + 5 * q + r
                    wait_slot(pe, j, i * (G_JOBS // 4))
                    pe.wait_ge(S["hot_ready"], i * 16 + (4 * q + r + 1))
                    pe.wait_ge(S["hot_lo_ready"], i * 16 + (4 * q + r + 1))
                    for t in range(G_TOK):
                        out = ps[:, j % 4, t * P:(t + 1) * P]
                        mm(out, hot2[:, r % 2, t, :], hot1_hi[:, r % 2, t, :], start=True, stop=False)
                        last = mm(out, hot2[:, r % 2, t, :], hot1_lo[:, r % 2, t, :], start=False, stop=True)
                    last.then_inc(job_done, 1)

                j = J_G + 5 * q + 4
                g_job(0)
                g_job(1)
                wait_slot(pe, j, i * (G_JOBS // 4))
                pe.wait_ge(S["u_split"], i * 4 + (ROUTER_AHEAD + q + 1))
                hidden_half(j, ahead_hi[:, q % 2], ahead_lo[:, q % 2], 0)
                g_job(2)
                g_job(3)
                hidden_half(j, ahead_hi[:, q % 2], ahead_lo[:, q % 2], 1).then_inc(job_done, 1)

        for m in range(2):
            hidden_single(J_BEHIND_G + m, AHEAD - 2 + m)

        def hidden_job(j, s, e):
            wait_slot(pe, j, s * 5)
            hidden_half(j, u_hi[:, e], u_lo[:, e], 0)
            hidden_half(j, u_hi[:, e], u_lo[:, e], 1).then_inc(job_done, 1)

        def value_job(j, rounds, hi, lo, place, c):
            wait_slot(pe, j, rounds)
            for half in range(2):
                cols = slice(half * HALF, (half + 1) * HALF)
                for n in range(GROUP):
                    feats = slice(c * P, (c + 1) * P)
                    last = three_passes(ps[:, j % 4, cols], hi[:, n, feats], lo[:, n, feats],
                                        a_hi[:, place, n, cols], a_lo[:, place, n, cols], n == 0, n == GROUP - 1)
            last.then_inc(job_done, 1)

        def expert_step(s, k, has_next=True):
            j = J_STEP + STEP_JOBS * k
            if has_next:
                for n in range(GROUP):
                    pe.wait_ge(S["u_split"], s * 4 + 2 * k + 3 + n)
                    hidden_job(j + n, s, n)
                j += GROUP
            pe.wait_ge(S["v_split"], s * 4 + 2 * k + 2)
            pe.wait_ge(S["a_split"], s * 4 + 2 * k + 2)
            for c in range(KC):
                value_job(j + c, s * 5, v_hi, v_lo, k, c)

        with pe.Fori(0, GROUPS_AHEAD // 2) as s:
            for k, (hi, lo) in enumerate(((v_hi, v_lo), (v_hi_odd, v_lo_odd))):
                pe.wait_ge(S["v_split"], s * 4 + 2 * k + 2)
                pe.wait_ge(S["a_split"], s * 4 + 2 * k + 2)
                for c in range(KC):
                    value_job(J_AHEAD + KC * k + c, s * 4, hi, lo, k, c)
        for n in range(GROUP):
            pe.wait_ge(S["u_split"], AHEAD + n + 1)
            hidden_job(J_EXP + n, 0, n)
        with pe.Fori(GROUPS_AHEAD // 2, GROUPS // 2 - 1) as s:
            expert_step(s, 0)
            expert_step(s, 1)
        expert_step(GROUPS // 2 - 1, 0)
        expert_step(GROUPS // 2 - 1, 1, has_next=False)
        total_sum(J_NORM_OUT, 4 * (KC - 1), total)

    @block.scalar
    def _(sc):
        fn = nc.scalar.activation
        count = {"sq": 0, "rstd": 0}

        def square(tile):
            n = count["sq"]
            count["sq"] += 1
            if n >= 2:
                sc.wait_ge(S["sq_used"], n - 1)
            fn(squares[:, n % 2, :], tile, ACT.Square).then_inc(S["sq_ready"], 1)

        def root():
            count["rstd"] += 1
            sc.wait_ge(S["var_ready"], count["rstd"])
            fn(rstd[:], rstd[:], ACT.Sqrt).then_inc(S["rstd_ready"], 1)

        def w_hi_copy(w, i=0):
            sc.wait_ge(S["w_in"][w % 4], i * 16 + (w // 4 + 1) * 16)
            fn(flat(w_split_place(w)[0]), flat(wring[:, w % 4]), ACT.Copy).then_inc(S["w_hi_ready"], 1)

        def normed_hi(hi, first):
            for c in range(KC):
                sc.wait_ge(S["xn_ready"], first + c + 1)
                fn(hi[:, c, :], normed[:, c % 4, :], ACT.Copy).then_inc(S["xhi_ready"], 1)

        for c in range(KC):
            if c % 2 == 0:
                sc.wait_ge(S["x_in"][c // 2], 16)
            square(raw[:, c, :])
        root()
        w_hi_copy(0)
        normed_hi(in_hi, 0)
        w_hi_copy(1)
        sc.wait_ge(S["vec_in"], 16)
        for k in range(5):
            j = J_LATENT + k
            wait_job(sc, j)
            w_hi_copy(k + 2)
            if k < 4:
                square(ps[:, j % 4, :])
                fn(latent[:, k, :], ps[:, j % 4, :], ACT.Copy).then_inc(slot_free[j % 4], 1)
        root()
        root()
        with sc.Fori(0, 4) as i:
            for n in range(2):
                j = J_GLU + 2 * n
                wait_job(sc, i * 4 + j)
                sc.wait_ge(S["u_ready"], i * 2 + n + 1)
                fn(gate[:, n, :], ps[:, j % 4, :], ACT.Sigmoid).then_inc(slot_free[j % 4], 1)
                w_hi_copy(W_GLU + 2 * n + 2, i)
                wait_job(sc, i * 4 + (j + 1))
                fn(conv[:, bass.ds(i * 2 + n, 1), PAD:].rearrange("p a t -> p (a t)"), ps[:, (j + 1) % 4, :],
                   ACT.Copy).then_inc(slot_free[(j + 1) % 4], 1)
                w_hi_copy(W_GLU + 2 * n + 3, i)

        def gate_job(k, i=0, more=True):
            wait_job(sc, i * 4 + (J_GATE + k))
            if k >= 2:
                sc.wait_ge(S["gate_out"][k % 2], i * 32 + 16 * (k // 2))
            else:
                sc.wait_ge(S["u_ready"], 2 + KC - 1 + k)
            fn(gate[:, k % 2, :], ps[:, (J_GATE + k) % 4, :], ACT.Sigmoid,
               bias=vec[:, bass.ds(i * 4 + (V_BM + k), 1)]).then_inc(slot_free[(J_GATE + k) % 4], 1)
            if more:
                w_hi_copy(W_GATE + k + 2, i)

        for k in range(4):
            gate_job(k)
        with sc.Fori(0, 2) as i:
            for k in range(4, 8):
                gate_job(k, i)
        for k in range(12, 16):
            gate_job(k, more=k < 14)

        def unit_copy(s, par, u, place=None):
            if u < 2:
                return
            sc.wait_ge(S["unit_done"], s * 16 + (par * 8 + (u if place is None else place) + 1))
            half = slice((u % 2) * HALF, (u % 2 + 1) * HALF)
            out = (q_nope[:, par, half], k_nope[:, par, half],
                   v_head[:, par, (u % 2) * 4:(u % 2 + 1) * 4, :].rearrange("p t v -> p (t v)"))[u // 2 - 1]
            fn(out, ps[:, 3, 0:HALF], ACT.Copy, scale=SCALE if u < 4 else 1.0).then_inc(S["unit_read"], 1)

        def exps(s, par, i):
            n = s * 16 + (par * 8 + i)
            sc.wait_ge(S["max_ready"], n + 1)
            if i >= 2 or par or not isinstance(s, int):
                sc.wait_ge(S["pt_ready"], n - 1)
            width = (i + 1) * P
            fn(probs[:, i % 2, 0:width], ps[:, i % 2, 0:width], ACT.Exp, bias=negmax[:, i % 2:i % 2 + 1],
               accum_out=expsum[:, i % 2:i % 2 + 1]).then_inc(S["exp_ready"], 1)

        def copy_out(s, par, part):
            sc.wait_ge(S["pv_done"], s * 16 + (par * 8 + 4 * part + 4))
            cols = slice(part * HALF, (part + 1) * HALF)
            fn(in_hi[:, bass.ds(s * 2 + par, 1), cols].rearrange("p a t -> p (a t)"), ps[:, 3, HALF:T],
               ACT.Copy).then_inc(S["o_copied"], 1)

        def attention_step(s, par, i, has_next=True, first=False):
            n = s * 16 + (par * 8 + i)
            following = (s, 1) if par == 0 else (s + 1, 0)
            if i + 1 < QT:
                exps(s, par, i + 1)
            elif has_next:
                exps(*following, 0)
            if i == 4:
                copy_out(s, par, 0)
            if i == 0 and not first:
                copy_out(*((s, 0) if par else (s - 1, 1)), 1)
            sc.wait_ge(S["pt_ready"], n + 1)
            width = (i + 1) * P
            fn(probsT[:, i % 2, 0:i + 1, :].rearrange("p b k -> p (b k)"), ps[:, 2, 0:width],
               ACT.Copy).then_inc(S["pt_copied"], 1)
            if has_next:
                unit_copy(*following, i)

        sc.nop().then_inc(S["pt_copied"], 1)
        for place, u in enumerate(FIRST_HEAD):
            if u == 6:
                sc.wait_ge(S["conv_ready"], KC)
            unit_copy(0, 0, u, place)
        exps(0, 0, 0)
        for par in range(2):
            for i in range(QT):
                attention_step(0, par, i, first=par + i == 0)
        with sc.Fori(1, HEADS // 2 - 1) as s:
            for par in range(2):
                for i in range(QT):
                    attention_step(s, par, i)
        for par in range(2):
            for i in range(QT):
                attention_step(HEADS // 2 - 1, par, i, has_next=par == 0)
        copy_out(HEADS // 2 - 1, 1, 1)

        w_hi_copy(W_MLAOUT)
        w_hi_copy(W_MLAOUT + 1)
        def centred_square(c):
            sc.wait_ge(S["centred"], c + 1)
            square(conv[:, c, PAD:])

        for c in range(4):
            centred_square(c)
        wait_job(sc, J_MLAOUT)
        w_hi_copy(W_MLAOUT + 2)
        for c in range(4, KC):
            centred_square(c)
        for c in range(1, 4):
            wait_job(sc, J_MLAOUT + c)
            w_hi_copy(W_MLAOUT + c + 2)
        root()
        for c in range(4, 6):
            wait_job(sc, J_MLAOUT + 1 + c)
            w_hi_copy(W_MLAOUT + c + 2)
        for c in range(KC):
            sc.wait_ge(S["ln_ready"], c + 1)
            fn(conv[:, c, PAD:], conv[:, c, PAD:], ACT.Silu, scale=vec[:, V_LNG + c:V_LNG + c + 1],
               bias=vec[:, V_LNB + c:V_LNB + c + 1]).then_inc(S["silu_ready"], 1)
        wait_job(sc, J_MLAOUT + 7)
        w_hi_copy(W_CONVOUT)
        wait_job(sc, J_MLAOUT + 8)
        sc.wait_ge(S["silu_ready"], KC)
        for c in range(KC):
            fn(in_hi[:, c, :], conv[:, c, PAD:], ACT.Copy).then_inc(S["y_hi_ready"], 1)
            if c == 0:
                w_hi_copy(W_CONVOUT + 1)
        for c in range(KC):
            wait_job(sc, J_CONVOUT + c)
            w_hi_copy(W_CONVOUT + c + 2)
            sc.wait_ge(S["merged_ready"], c + 1)
            fn(m_hi[:, c, :], merged[:, c, :], ACT.Copy).then_inc(S["m_hi_ready"], 1)
        for c in range(KC):
            if c < KC - 2:
                wait_job(sc, J_OUT + c)
                w_hi_copy(W_OUT + c + 2)
            sc.wait_ge(S["h_ready"], c + 1)
            square(act[:, c, :])

        def split_wq(n, i=0):
            w = W_ROUTER + n
            sc.wait_ge(S["w_in"][w % 4], i * 16 + (w // 4 + 1) * 16)
            fn(flat(wq_hi[:, n % 2]), flat(wring[:, w % 4]), ACT.Copy).then_inc(S["wq_hi_ready"], 1)

        wait_job(sc, J_NORM_H - 1)
        split_wq(0)
        split_wq(1)
        root()
        normed_hi(x_hi, KC)

        def ahead_hi_copy(e, i=0, step=0):
            sc.wait_ge(S["u_in"][e % 2], i * (8 * step) + (e // 2 + 1) * 16)
            fn(flat(ahead_hi[:, e % 2]), flat(ahead_raw[:, e % 2]), ACT.Copy).then_inc(S["u_hi_ready"], 1)

        def ahead_gelu(e, j, i=0, step=0, jstep=0, more=True):
            wait_job(sc, i * jstep + j)
            if e >= 2 or not isinstance(i, int):
                sc.wait_ge(S["ahead_out"][e % 2], i * (8 * step) + e // 2 * 16)
            fn(ahead_out[:, e % 2, :], ps[:, j % 4, :], ACT.Gelu_apprx_tanh).then_inc(slot_free[j % 4], 1)
            if more:
                ahead_hi_copy(e + 2, i, step)

        def router_head(i, h, more_w=True):
            for k in range(2):
                j = J_ROUTER + R_JOBS * h + R_QUERY + k
                wait_job(sc, i * (2 * R_JOBS) + j)
                fn(query[:, k, :], ps[:, j % 4, :], ACT.Copy).then_inc(slot_free[j % 4], 1)
                if more_w:
                    split_wq(2 * h + k + 2, i)
            for m in range(4):
                ahead_gelu(4 * h + m, J_ROUTER + R_JOBS * h + R_HIDDEN[m], i, 8, 2 * R_JOBS)
            sc.wait_ge(S["shifted_ready"], i * 2 + h + 1)
            fn(weight[:], shifted[:], ACT.Exp).then_inc(S["weight_exp"], 1)

        ahead_hi_copy(0)
        ahead_hi_copy(1)
        router_head(0, 0)
        router_head(0, 1)
        with sc.Fori(1, 3) as i:
            router_head(i, 0)
            router_head(i, 1)
        router_head(3, 0)
        router_head(3, 1, more_w=False)
        for m in range(2):
            ahead_gelu(ROUTER_AHEAD - 2 + m, J_SEL - 2 + m)
        for n in range(3):
            j = J_SEL + n
            wait_job(sc, j)
            if n < 2:
                fn(selT[:, n, :], ps[:, j % 4, :], ACT.Copy).then_inc(slot_free[j % 4], 1)
            else:
                fn(w16[:, 0, :], ps[:, j % 4, :], ACT.Copy, scale=W_SHIFT).then_inc(S["w_hi16_ready"], 1)
        def g_blocks(i, first=False):
            for q in range(4):
                b = q // 2
                if q % 2 == 0 and not first:
                    sc.wait_ge(S["g_out"][b], i * 16)
                for r in range(4):
                    j = J_G + 5 * q + r
                    wait_job(sc, i * G_JOBS + j)
                    tok = slice(G_TOK * (4 * (q % 2) + r), G_TOK * (4 * (q % 2) + r + 1))
                    fn(gblock[:, b, :, tok].rearrange("p a t -> p t a"),
                       ps[:, j % 4, :].rearrange("p (t a) -> p t a", a=P), ACT.Copy,
                       scale=1.0 / W_SHIFT).then_inc(slot_free[j % 4], 1)
                ahead_gelu(ROUTER_AHEAD + q, J_G + 5 * q + 4, i, 4, G_JOBS)

        g_blocks(0, first=True)
        with sc.Fori(1, G_BLOCKS // 2) as i:
            g_blocks(i)

        def u_hi_copy(e, k, s=0):
            sc.wait_ge(S["u_in"][k], s * 32 + (e // 2 + 1) * 16)
            fn(flat(u_hi[:, k]), flat(u_raw[:, k]), ACT.Copy).then_inc(S["u_hi_ready"], 1)

        def gelu(j, s, e):
            wait_job(sc, s * 20 + j)
            sc.wait_ge(S["a_split"], s * 4 + e - 1)
            fn(hidden[:, e % 2, :], ps[:, j % 4, :], ACT.Gelu_apprx_tanh).then_inc(slot_free[j % 4], 1)

        def a_hi_copy(s, e, place):
            sc.wait_ge(S["a_ready"], s * 4 + e + 1)
            fn(a_hi[:, place, e % 2, :], hidden[:, e % 2, :], ACT.Copy).then_inc(S["a_hi_ready"], 1)

        def v_hi_copy(s, e, place=v_hi):
            sc.wait_ge(S["v_in"][e % 2], s * 32 + (e // 2 + 1) * 16)
            fn(place[:, e % 2, :], v_raw[:, e % 2, :], ACT.Copy).then_inc(S["v_hi_ready"], 1)

        def ahead_group(s, k):
            for n in range(GROUP):
                v_hi_copy(s, 2 * k + n, v_hi_odd if k else v_hi)
            for n in range(GROUP):
                a_hi_copy(s, 2 * k + n, k)

        v_hi_copy(0, 0)
        v_hi_copy(0, 1)
        ahead_gelu(AHEAD - 2, J_BEHIND_G, more=False)
        a_hi_copy(0, 0, 0)
        a_hi_copy(0, 1, 0)
        ahead_gelu(AHEAD - 1, J_BEHIND_G + 1, more=False)
        ahead_group(0, 1)
        with sc.Fori(1, GROUPS_AHEAD // 2) as s:
            for k in range(2):
                wait_job(sc, s * (2 * KC) + (J_AHEAD + KC * k - KC - 1))
                ahead_group(s, k)

        def expert_step(s, k, has_next=True, more_u=True):
            wait_job(sc, s * 20 + (J_STEP + STEP_JOBS * k - 1))
            for n in range(GROUP):
                v_hi_copy(s, 2 * k + n)
            if has_next:
                j = J_STEP + STEP_JOBS * k
                for n in range(GROUP):
                    gelu(j + n, s, 2 * k + 2 + n)
                    if more_u:
                        u_hi_copy(2 * k + 4 + n, n, s)
                for n in range(GROUP):
                    a_hi_copy(s, 2 * k + 2 + n, (k + 1) % 2)

        wait_job(sc, J_EXP - 1)
        u_hi_copy(AHEAD, 0)
        u_hi_copy(AHEAD + 1, 1)
        for n in range(GROUP):
            gelu(J_EXP + n, 0, AHEAD + n)
            u_hi_copy(AHEAD + 2 + n, n)
        for n in range(GROUP):
            a_hi_copy(0, AHEAD + n, 0)
        with sc.Fori(GROUPS_AHEAD // 2, GROUPS // 2 - 1) as s:
            expert_step(s, 0)
            expert_step(s, 1)
        expert_step(GROUPS // 2 - 1, 0, more_u=False)
        expert_step(GROUPS // 2 - 1, 1, has_next=False)
        for c in range(KC):
            wait_read(sc, J_NORM_OUT - KC + c)
            square(act[:, c, :])
        root()

    @block.gpsimd
    def _(pool):
        def wq_lo_sub(n, i=0):
            pool.wait_ge(S["wq_hi_ready"], i * 4 + n + 1)
            nc.gpsimd.tensor_tensor(flat(wq_lo[:, n % 2]), flat(wring[:, (W_ROUTER + n) % 4]), flat(wq_hi[:, n % 2]),
                                    ALU.subtract).then_inc(S["wq_split"], 1)

        def ahead_lo_sub(e, i=0, step=0):
            pool.wait_ge(S["u_hi_ready"], i * step + e + 1)
            nc.gpsimd.tensor_tensor(flat(ahead_lo[:, e % 2]), flat(ahead_raw[:, e % 2]), flat(ahead_hi[:, e % 2]),
                                    ALU.subtract).then_inc(S["u_split"], 1)

        def router_head(i, h, more_w=True):
            if more_w:
                wq_lo_sub(2 * h + 2, i)
                wq_lo_sub(2 * h + 3, i)
            for m in range(4):
                ahead_lo_sub(4 * h + m + 2, i, 8)

        def w_lo_sub(w, i=0, step=4):
            pool.wait_ge(S["w_hi_ready"], i * step + (w + 1))
            hi, lo = w_split_place(w)
            nc.gpsimd.tensor_tensor(flat(lo), flat(wring[:, w % 4]), flat(hi), ALU.subtract).then_inc(S["w_split"], 1)

        def lo_odd(lo, hi, first):
            for c in range(1, KC, 2):
                pool.wait_ge(S["xhi_ready"], first + c + 1)
                nc.gpsimd.tensor_tensor(lo[:, c, :], normed[:, c % 4, :], hi[:, c, :],
                                        ALU.subtract).then_inc(S["xlo_odd"], 1)

        w_lo_sub(0)
        lo_odd(in_lo, in_hi, 0)
        for w in range(1, W_GLU + 2):
            w_lo_sub(w)
        with pool.Fori(0, 4) as i:
            for n in range(2):
                w_lo_sub(W_GLU + 2 * n + 2, i)
                j = J_GLU + 2 * n
                wait_read(pool, j, i)
                wait_read(pool, j + 1, i)
                out = conv[:, bass.ds(i * 2 + n, 1), PAD:].rearrange("p a t -> p (a t)")
                nc.gpsimd.tensor_tensor(out, out, gate[:, n, :], ALU.mult).then_inc(S["u_ready"], 1)
                w_lo_sub(W_GLU + 2 * n + 3, i)
        for w in range(W_GATE + 2, W_MLAOUT):
            w_lo_sub(w)
        added = {"tiles": 0, "squares": 8 + 2 * LC}

        def add(out, first, second):
            if added["tiles"]:
                pool.wait_ge(S["add_done"], added["tiles"])
            added["tiles"] += 1
            nc.gpsimd.tensor_tensor(out, first, second, ALU.add).then_inc(S["add_done"], 1)

        def add_square(c):
            added["squares"] += 1
            n = added["squares"]
            pool.wait_ge(S["sq_ready"], n)
            if c:
                first = squares[:, (n - 2) % 2, :] if c == 1 else total[:]
                add(total[:], first, squares[:, (n - 1) % 2, :])
                pool.wait_ge(S["add_done"], added["tiles"])
                pool.nop().then_inc(S["sq_used"], 2 if c == 1 else 1)

        pool.wait_ge(S["gate_out"][1], 16 * 8)
        for c in range(1, KC):
            pool.wait_ge(S["conv_ready"], (c // 2 + 1) * 2)
            add(gate[:, 1, :], gate[:, 1, :] if c > 1 else conv[:, 0, PAD:], conv[:, c, PAD:])
        w_lo_sub(W_MLAOUT)
        w_lo_sub(W_MLAOUT + 1)
        for c in range(KC):
            if c == 4:
                w_lo_sub(W_MLAOUT + 2)
            add_square(c)
        for w in range(W_MLAOUT + 3, W_OUT + 2):
            w_lo_sub(w)
        for c in range(KC):
            if c < KC - 2:
                w_lo_sub(W_OUT + 2 + c)
            add_square(c)

        wq_lo_sub(0)
        lo_odd(x_lo, x_hi, KC)
        wq_lo_sub(1)
        ahead_lo_sub(0)
        ahead_lo_sub(1)
        with pool.Fori(0, 3) as i:
            router_head(i, 0)
            router_head(i, 1)
        router_head(3, 0)
        router_head(3, 1, more_w=False)
        ahead_lo_sub(ROUTER_AHEAD)
        pool.wait_ge(S["w_lo16_ready"], 1)
        with pool.Fori(0, G_BLOCKS // 2) as i:
            for q in range(4):
                for r in range(4):
                    pool.wait_ge(S["hot1_ready"], i * 16 + (4 * q + r + 1))
                    nc.gpsimd.tensor_tensor(hot1_lo[:, r % 2], hot1[:, r % 2], token_weights(1, i, 4 * q + r),
                                            ALU.mult).then_inc(S["hot_lo_ready"], 1)
                    if r == 1:
                        ahead_lo_sub(ROUTER_AHEAD + 1 + q, i, 4)
        ahead_lo_sub(AHEAD - 1)
        for c in range(KC):
            add_square(c)

    @block.vector
    def _(v):
        dv = nc.vector
        step = S["dve_step"]
        chain = {"base": 0, "n": 0}

        def link(ins, back=0):
            ins.then_inc(step, 1)
            chain["n"] += 1
            v.wait_ge(step, chain["base"] + (chain["n"] - back))

        def enter_loop(i, per):
            chain["base"] = i * per
            return chain["n"] + per

        def leave_loop(end, per, rounds):
            assert chain["n"] == end, (chain["n"], end)
            chain["base"] = 0
            chain["n"] += per * (rounds - 1)

        count = {"norm": 0}

        def rstd_of(j, width):
            wait_job(v, j)
            dv.tensor_scalar(rstd[:], ps[:, j % 4, :], 1.0 / width, EPS, ALU.mult, ALU.add).then_inc(slot_free[j % 4], 1)
            wait_read(v, j)
            dv.reciprocal(rstd[:], rstd[:]).then_inc(S["var_ready"], 1)
            count["norm"] += 1
            v.wait_ge(S["rstd_ready"], count["norm"])

        def normed_split(src, gain, lo, hi, first):
            even, odd = (lambda n: v.wait_ge(S["xlo_even"], first // 2 + n),
                         lambda n: v.wait_ge(S["xlo_odd"], first // 2 + n))
            for c in range(KC):
                if c >= 4:
                    (odd if c % 2 else even)(c // 2 - 1)
                dv.scalar_tensor_tensor(normed[:, c % 4, :], src[:, c, :], vec[:, gain + c:gain + c + 1], rstd[:],
                                        ALU.mult, ALU.mult).then_inc(S["xn_ready"], 1)
                if c % 2:
                    v.wait_ge(S["xhi_ready"], first + c)
                    dv.tensor_tensor(lo[:, c - 1, :], normed[:, (c - 1) % 4, :], hi[:, c - 1, :],
                                     ALU.subtract).then_inc(S["xlo_even"], 1)
            even(KC // 2)
            odd(KC // 2)

        for k in range(4):
            v.wait_ge(S["x_in"][k], 16)
        rstd_of(J_NORM_X, D)
        v.wait_ge(S["vec_in"], 16)
        normed_split(raw, V_GMIX, in_lo, in_hi, 0)
        v.nop().then_inc(S["u_ready"], 2)
        link(dv.memset(conv[:, :, 0:PAD], 0.0))
        j = J_LATENT + 4
        wait_job(v, j)
        v.wait_ge(S["rot_in"], 16)
        dv.tensor_tensor(conv_sum[0:ROPE, 0, :], ps[0:ROPE, j % 4, :], rot[0:ROPE, :], ALU.mult)
        dv.tensor_tensor(conv_sum[0:ROPE, 1, :], ps[ROPE:P, j % 4, :], rot[ROPE:P, :],
                         ALU.mult).then_inc(slot_free[j % 4], 1)
        wait_read(v, j)
        dv.tensor_tensor(k_rope[:], conv_sum[0:ROPE, 0, :], conv_sum[0:ROPE, 1, :],
                         ALU.add).then_inc(S["krope_ready"], 1)
        for lat, (j, g) in enumerate(((J_NORM_Q, V_QG), (J_NORM_KV, V_KG))):
            rstd_of(j, LORA)
            for c in range(LC):
                dv.scalar_tensor_tensor(latent[:, 2 * lat + c, :], latent[:, 2 * lat + c, :], vec[:, g + c:g + c + 1],
                                        rstd[:], ALU.mult, ALU.mult).then_inc(S["lat_normed"], 1)
            v.wait_ge(S["lat_normed"], 2 * lat + 2)

        with v.Fori(0, 4) as i:
            end = enter_loop(i, 2 * TAPS)
            v.wait_ge(S["u_ready"], i * 2 + 4)

            def tile(n, k):
                return conv[:, bass.ds(i * 2 + n, 1), k:k + T].rearrange("p a t -> p (a t)")

            def tap(n, k):
                return vec[:, bass.ds(i * (2 * TAPS) + (V_DW + n * TAPS + k), 1)]

            for k in range(TAPS):
                for n in range(2):
                    if k == 0:
                        ins = dv.tensor_scalar(conv_sum[:, n, :], tile(n, 0), tap(n, 0),
                                               vec[:, bass.ds(i * 2 + (V_DWB + n), 1)], ALU.mult, ALU.add)
                    else:
                        out = tile(n, PAD) if k == PAD else conv_sum[:, n, :]
                        ins = dv.scalar_tensor_tensor(out, tile(n, k), tap(n, k), conv_sum[:, n, :],
                                                      ALU.mult, ALU.add)
                    link(ins, back=1)
            v.wait_ge(step, chain["base"] + chain["n"])
            v.nop().then_inc(S["conv_ready"], 2)

        leave_loop(end, 2 * TAPS, 4)

        def turn(s, par, u, place=None):
            v.wait_ge(S["unit_done"], s * 16 + (par * 8 + (u if place is None else place) + 1))
            half = slice(u * HALF, (u + 1) * HALF)
            for n in range(2):
                part = slice(n * ROPE, (n + 1) * ROPE)
                ins = dv.scalar_tensor_tensor(turned[:, n, :], ps[part, 3, 0:HALF], SCALE, rot[part, half],
                                              ALU.mult, ALU.mult)
            link(ins)
            v.nop().then_inc(S["unit_read"], 1)
            dv.tensor_tensor(q_rope[:, par, half], turned[:, 0, :], turned[:, 1, :],
                             ALU.add).then_inc(S["q_rope_ready"], 1)
            v.wait_ge(S["q_rope_ready"], s * 4 + (par * 2 + u + 1))

        def row_max(s, par, i):
            width = (i + 1) * P
            v.wait_ge(S["s_ready"], s * 16 + (par * 8 + i + 1))
            link(dv.memset(ps[0:CHUNK, i % 2, width - CHUNK:width], -1e30))
            dv.tensor_reduce(negmax[:, i % 2:i % 2 + 1], ps[:, i % 2, 0:width], AX.X, ALU.max,
                             negate=True).then_inc(S["max_ready"], 1)

        def split_out(s, par, part):
            v.wait_ge(S["o_copied"], s * 4 + (par * 2 + part + 1))
            cols = slice(part * HALF, (part + 1) * HALF)
            out = [x[:, bass.ds(s * 2 + par, 1), cols].rearrange("p a t -> p (a t)") for x in (in_lo, in_hi)]
            dv.tensor_tensor(out[0], ps[:, 3, HALF:T], out[1], ALU.subtract).then_inc(S["o_split"], 1)

        def attention_step(s, par, i, has_next=True, first=False):
            following = (s, 1) if par == 0 else (s + 1, 0)
            if i + 1 < QT:
                row_max(s, par, i + 1)
            elif has_next:
                row_max(*following, 0)
            width = (i + 1) * P
            v.wait_ge(S["exp_ready"], s * 16 + (par * 8 + i + 1))
            link(dv.reciprocal(expsum[:, i % 2:i % 2 + 1], expsum[:, i % 2:i % 2 + 1]))
            dv.tensor_scalar(probs[:, i % 2, 0:width], probs[:, i % 2, 0:width], expsum[:, i % 2:i % 2 + 1],
                             None, ALU.mult).then_inc(S["p_ready"], 1)
            if has_next and i in (1, 2):
                turn(*following, i - 1)
            if i == 4:
                split_out(s, par, 0)
            if i == 0 and not first:
                split_out(*((s, 0) if par else (s - 1, 1)), 1)

        v.nop().then_inc(S["o_split"], 1)
        turn(0, 0, 0, FIRST_HEAD.index(0))
        turn(0, 0, 1, FIRST_HEAD.index(1))
        row_max(0, 0, 0)
        per = 4 * QT + 4
        for par in range(2):
            for i in range(QT):
                attention_step(0, par, i, first=par + i == 0)
        with v.Fori(1, HEADS // 2 - 1) as s:
            end = enter_loop(s - 1, per)
            for par in range(2):
                for i in range(QT):
                    attention_step(s, par, i)
        leave_loop(end, per, HEADS // 2 - 2)
        for par in range(2):
            for i in range(QT):
                attention_step(HEADS // 2 - 1, par, i, has_next=par == 0)
        split_out(HEADS // 2 - 1, 1, 1)

        def wait_gate(n):
            v.wait_ge(S["gate_in"][n % 2], (n // 2 + 1) * 16)

        def mla_branch(c):
            j = J_MLAOUT + c + (c >= 4)
            wait_gate(c)
            wait_job(v, j)
            dv.tensor_tensor(merged[:, c, :], ps[:, j % 4, :], gate[:, c % 2, :],
                             ALU.mult).then_inc(slot_free[j % 4], 1)
            wait_read(v, j)
            v.nop().then_inc(S["gate_used"], 1)

        wait_job(v, J_LN_MEAN)
        dv.tensor_scalar(rstd[:], ps[:, J_LN_MEAN % 4, :], 1.0 / D, None,
                         ALU.mult).then_inc(slot_free[J_LN_MEAN % 4], 1)
        wait_read(v, J_LN_MEAN)
        for c in range(KC):
            dv.tensor_tensor(conv[:, c, PAD:], conv[:, c, PAD:], rstd[:], ALU.subtract).then_inc(S["centred"], 1)
        for c in range(4):
            mla_branch(c)
        rstd_of(J_LN_VAR, D)
        for c in range(KC):
            dv.tensor_tensor(conv[:, c, PAD:], conv[:, c, PAD:], rstd[:], ALU.mult).then_inc(S["ln_ready"], 1)
        for c in range(4, KC):
            mla_branch(c)
        for c in range(KC):
            v.wait_ge(S["y_hi_ready"], c + 1)
            dv.tensor_tensor(in_lo[:, c, :], conv[:, c, PAD:], in_hi[:, c, :], ALU.subtract).then_inc(S["y_split"], 1)
        v.wait_ge(S["y_split"], KC)
        for c in range(KC):
            j = J_CONVOUT + c
            wait_gate(KC + c)
            wait_job(v, j)
            dv.tensor_tensor(gate[:, c % 2, :], ps[:, j % 4, :], gate[:, c % 2, :],
                             ALU.mult).then_inc(slot_free[j % 4], 1)
            wait_read(v, j)
            dv.tensor_tensor(merged[:, c, :], merged[:, c, :], gate[:, c % 2, :],
                             ALU.add).then_inc(S["merged_ready"], 1)
            v.wait_ge(S["merged_ready"], c + 1)
            v.nop().then_inc(S["gate_used"], 1)
            v.wait_ge(S["m_hi_ready"], c + 1)
            dv.tensor_tensor(m_lo[:, c, :], merged[:, c, :], m_hi[:, c, :], ALU.subtract).then_inc(S["m_split"], 1)
        for c in range(KC):
            j = J_OUT + c
            v.wait_ge(S["x_again"][c // 2], 16)
            wait_job(v, j)
            dv.tensor_tensor(act[:, c, :], ps[:, j % 4, :], act[:, c, :], ALU.add).then_inc(slot_free[j % 4], 1)
            wait_read(v, j)
            v.nop().then_inc(S["h_ready"], 1)
        rstd_of(J_NORM_H, D)
        normed_split(act, V_GFFN, x_lo, x_hi, KC)

        def carry_wait():
            carried[0] += 1
            dv.memset(spare[:, carried[0] - 1:carried[0]], 0.0)

        carried = [0]

        def wide(ap, n):
            return ap.unsqueeze(3).to_broadcast([P, QT, TOPK, n])

        def tall(ap, n):
            return ap.unsqueeze(2).to_broadcast([P, QT, n, TOPK])

        iota16 = iota[:, 0:TOPK].unsqueeze(1).unsqueeze(1).to_broadcast([P, QT, TOPK, TOPK])
        with v.Fori(0, HEADS) as h:
            end = enter_loop(h, 25)
            for k in range(2):
                j = J_ROUTER + R_SCORE + k
                wait_job(v, h * R_JOBS + j)
                scores = [ps[:, j % 4, t * P:(t + 1) * P] for t in range(QT)]
                carry_wait()
                for t in range(QT):
                    last = dv.max(best[:, k, t, 0:8], scores[t])
                link(last)
                carry_wait()
                for t in range(QT):
                    dv.max_index(best_key[:, k, t, 0:8], best[:, k, t, 0:8], scores[t])
                for t in range(QT):
                    last = dv.match_replace(rest[:, t, :], best[:, k, t, 0:8], scores[t], -3e38)
                link(last)
                v.nop().then_inc(slot_free[j % 4], 1)
                carry_wait()
                for t in range(QT):
                    last = dv.max(best[:, k, t, 8:16], rest[:, t, :])
                link(last)
                carry_wait()
                for t in range(QT):
                    last = dv.max_index(best_key[:, k, t, 8:16], best[:, k, t, 8:16], rest[:, t, :])
                link(last)
                link(dv.tensor_copy(best_keyf[:, k], best_key[:, k]))
            link(dv.tensor_tensor(cand[:], wide(best[:, 0], TOPK), tall(best[:, 1], TOPK), ALU.add))
            sums = [cand[:, t].rearrange("p a b -> p (a b)") for t in range(QT)]
            sums_rest = [cand_rest[:, t].rearrange("p a b -> p (a b)") for t in range(QT)]
            carry_wait()
            for t in range(QT):
                last = dv.max(top[:, t, 0:8], sums[t])
            link(last)
            carry_wait()
            for t in range(QT):
                dv.max_index(top_pos[:, t, 0:8], top[:, t, 0:8], sums[t])
            for t in range(QT):
                last = dv.match_replace(sums_rest[t], top[:, t, 0:8], sums[t], -3e38)
            link(last)
            carry_wait()
            for t in range(QT):
                last = dv.max(top[:, t, 8:16], sums_rest[t])
            link(last)
            dv.tensor_tensor(shifted[:], top[:], top[:, :, 0:1].to_broadcast([P, QT, TOPK]),
                             ALU.subtract).then_inc(S["shifted_ready"], 1)
            carry_wait()
            for t in range(QT):
                last = dv.max_index(top_pos[:, t, 8:16], top[:, t, 8:16], sums_rest[t])
            link(last)
            dv.tensor_scalar(pos_a[:], top_pos[:], 4, None, ALU.logical_shift_right)
            link(dv.tensor_scalar(pos_b[:], top_pos[:], 15, None, ALU.bitwise_and))
            dv.tensor_copy(pos_af[:], pos_a[:])
            link(dv.tensor_copy(pos_bf[:], pos_b[:]))
            for n, pos in enumerate((pos_af, pos_bf)):
                link(dv.tensor_tensor(pick[:], iota16, wide(pos[:], TOPK), ALU.is_equal))
                link(dv.tensor_tensor(pick[:], pick[:], tall(best_keyf[:, n], TOPK), ALU.mult))
                link(dv.tensor_reduce(sel[:, n, :, bass.ds(h * TOPK, TOPK)], pick[:], AX.X, ALU.add))
            v.wait_ge(S["weight_exp"], h + 1)
            link(dv.tensor_reduce(wsum[:, 0, :], weight[:], AX.X, ALU.add))
            link(dv.reciprocal(wsum[:, 1, :], wsum[:, 0, :]))
            dv.tensor_tensor(sel[:, 2, :, bass.ds(h * TOPK, TOPK)], weight[:],
                             wsum[:, 1, :].unsqueeze(2).to_broadcast([P, QT, TOPK]),
                             ALU.mult).then_inc(S["sel_ready"], 1)
            v.wait_ge(S["sel_ready"], h + 1)

        leave_loop(end, 25, HEADS)

        v.wait_ge(S["w_hi16_ready"], 1)
        j = J_SEL + 2
        dv.scalar_tensor_tensor(w16[:, 1, :], ps[:, j % 4, :], W_SHIFT, w16[:, 0, :], ALU.mult,
                                ALU.subtract).then_inc(S["w_lo16_ready"], 1)
        v.wait_ge(S["w_lo16_ready"], 1)
        v.nop().then_inc(slot_free[j % 4], 1)
        for n in range(2):
            wait_read(v, J_SEL + n)
        iota8 = iota.unsqueeze(1).to_broadcast([P, G_TOK, P])
        with v.Fori(0, G_BLOCKS // 2) as i:
            for q in range(4):
                for r in range(4):
                    wait_job(v, i * G_JOBS + (J_G + 5 * q + r - (2 if r >= 2 else 3)))

                    def index(n):
                        tok = bass.ds(i * (2 * G_BATCH) + (4 * q + r) * G_TOK, G_TOK)
                        return selT[:, n, tok].unsqueeze(2).to_broadcast([P, G_TOK, P])

                    dv.tensor_tensor(hot1[:, r % 2], iota8, index(0), ALU.is_equal).then_inc(S["hot1_ready"], 1)
                    dv.tensor_tensor(hot2[:, r % 2], iota8, index(1), ALU.is_equal)
                    v.wait_ge(S["hot1_ready"], i * 16 + (4 * q + r + 1))
                    dv.tensor_tensor(hot1_hi[:, r % 2], hot1[:, r % 2], token_weights(0, i, 4 * q + r),
                                     ALU.mult).then_inc(S["hot_ready"], 1)

        def u_lo_sub(s, e):
            v.wait_ge(S["u_hi_ready"], s * 4 + e + 1)
            k = e % 2
            dv.tensor_tensor(flat(u_lo[:, k]), flat(u_raw[:, k]), flat(u_hi[:, k]), ALU.subtract).then_inc(S["u_split"], 1)

        def v_lo_sub(s, e, hi=v_hi, lo=v_lo):
            v.wait_ge(S["v_hi_ready"], s * 4 + e + 1)
            dv.tensor_tensor(lo[:, e % 2, :], v_raw[:, e % 2, :], hi[:, e % 2, :],
                             ALU.subtract).then_inc(S["v_split"], 1)

        def weigh(j, s, e):
            if e % 2 == 0:
                v.wait_ge(S["g_in"][(e // 2) % 2], s * 16 + (e // 4 + 1) * 16)
            if j is None:
                v.wait_ge(S["hid_in"][e % 2], s * 32 + (e // 2 + 1) * 16)
            else:
                wait_read(v, j, s * 5)
            h3 = hidden[:, e % 2, :].rearrange("p (b t) -> p b t", t=G_BATCH)
            g3 = g_raw[:, (e // 2) % 2, :, (e % 2) * G_BATCH:(e % 2 + 1) * G_BATCH]
            dv.tensor_tensor(h3, h3, g3, ALU.mult).then_inc(S["a_ready"], 1)

        def a_lo_sub(s, e, slot):
            v.wait_ge(S["a_hi_ready"], s * 4 + e + 1)
            dv.tensor_tensor(a_lo[:, slot, e % 2, :], hidden[:, e % 2, :], a_hi[:, slot, e % 2, :],
                             ALU.subtract).then_inc(S["a_split"], 1)

        def expert_step(s, k, has_next=True, more_u=True, before=STEP_JOBS):
            for n in range(GROUP):
                v_lo_sub(s, 2 * k + n)
            j = J_STEP + STEP_JOBS * k
            if has_next:
                for n in range(GROUP):
                    weigh(j + n, s, 2 * k + 2 + n)
                    if more_u:
                        u_lo_sub(s, 2 * k + 4 + n)
                for n in range(GROUP):
                    a_lo_sub(s, 2 * k + 2 + n, (k + 1) % 2)
                j += GROUP
            accumulate(s, j, STEP_JOBS // 2, before)

        def accumulate(s, j, rounds, before):
            for c in range(KC):
                wait_job(v, s * (rounds * 4) + (j + c))
                if not before:
                    v.wait_ge(S["h_in"][c // 2], 16)
                else:
                    wait_read(v, j + c - before, s * rounds)
                dv.tensor_tensor(act[:, c, :], ps[:, (j + c) % 4, :], act[:, c, :],
                                 ALU.add).then_inc(slot_free[(j + c) % 4], 1)

        def ahead_group(s, k):
            for n in range(GROUP):
                v_lo_sub(s, 2 * k + n, v_hi_odd if k else v_hi, v_lo_odd if k else v_lo)
            for n in range(GROUP):
                weigh(None, s, 2 * k + n)
            for n in range(GROUP):
                a_lo_sub(s, 2 * k + n, k)

        ahead_group(0, 0)
        ahead_group(0, 1)
        accumulate(0, J_AHEAD, 4, 0)
        with v.Fori(1, GROUPS_AHEAD // 2) as s:
            ahead_group(s, 0)
            accumulate(s, J_AHEAD - KC, 4, KC)
            ahead_group(s, 1)
            accumulate(s, J_AHEAD, 4, KC)
        accumulate(0, J_EXP - KC, 4, KC)
        u_lo_sub(0, AHEAD)
        u_lo_sub(0, AHEAD + 1)
        for n in range(GROUP):
            weigh(J_EXP + n, 0, AHEAD + n)
            u_lo_sub(0, AHEAD + 2 + n)
        for n in range(GROUP):
            a_lo_sub(0, AHEAD + n, 0)
        expert_step(GROUPS_AHEAD // 2, 0, before=STEP_JOBS + GROUP)
        expert_step(GROUPS_AHEAD // 2, 1)
        with v.Fori(GROUPS_AHEAD // 2 + 1, GROUPS // 2 - 1) as s:
            expert_step(s, 0)
            expert_step(s, 1)
        expert_step(GROUPS // 2 - 1, 0, more_u=False)
        expert_step(GROUPS // 2 - 1, 1, has_next=False, before=KC)
        rstd_of(J_NORM_OUT, D)
        for c in range(KC):
            dv.scalar_tensor_tensor(act[:, c, :], act[:, c, :], vec[:, V_GFIN + c:V_GFIN + c + 1], rstd[:],
                                    ALU.mult, ALU.mult).then_inc(S["final_ready"], 1)

    block_cm.__exit__(None, None, None)


def kernel(**inputs):
    import concourse.bacc as bacc
    from concourse import mybir
    from concourse.bass_utils import run_bass_kernel_spmd

    a = {k: np.asarray(x) for k, x in inputs.items()}

    def column_tiles(w):
        k, n = w.shape
        return w.reshape(k // P, P, n // P, P).transpose(2, 1, 0, 3).reshape(n // P, P, k)

    w_in = a["w_in"][0]
    glu_a, glu_b = w_in[:, 0:D], w_in[:, D:2 * D]
    at = 2 * D
    q_lat, kv_lat = w_in[:, at:at + LORA], w_in[:, at + LORA:at + 2 * LORA]
    at += 2 * LORA
    rope = w_in[:, at:at + ROPE]
    at += ROPE
    gate_c, gate_m = w_in[:, at:at + D], w_in[:, at + D:at + 2 * D]

    def swapped(w):
        return np.concatenate([w[:, ROPE // 2:], w[:, :ROPE // 2]], axis=1)

    def in_pairs(first, second):
        return np.stack([column_tiles(first), column_tiles(second)], axis=1).reshape(16, P, D)

    wproj = np.concatenate([
        column_tiles(q_lat), column_tiles(kv_lat), column_tiles(np.concatenate([rope, swapped(rope)], axis=1)),
        in_pairs(glu_b, glu_a), column_tiles(gate_m), column_tiles(gate_c), column_tiles(a["mla_w_o"][0]),
        column_tiles(a["conv_w_pw"][0]),
        column_tiles(a["w_out"][0]), column_tiles(a["peer_w_q"][0])])
    heads = []
    for h in range(HEADS):
        q = a["w_q_up"][0][:, h * (NOPE + ROPE):(h + 1) * (NOPE + ROPE)]
        kv = a["w_kv_up"][0][:, h * (NOPE + VDIM):(h + 1) * (NOPE + VDIM)]
        w = np.concatenate([q[:, :NOPE], q[:, NOPE:], swapped(q[:, NOPE:]), kv], axis=1)
        heads.append(w.reshape(LC, P, 2, 2 * P).transpose(2, 1, 0, 3).reshape(2, P, LC * 2 * P))
    keysT = a["peer_sub_keys"][0].transpose(3, 0, 1, 2).reshape(P, 16, KEYS)
    uT = a["peer_u"][0].reshape(EXPERT_TILES, P, KC, P).transpose(0, 3, 2, 1).reshape(EXPERT_TILES, P, D)
    vtab = a["peer_v"][0].reshape(EXPERT_TILES, P, D)

    def cols(x):
        return x.reshape(-1, P).T

    dw = a["conv_dw"][0].reshape(TAPS, KC, P).transpose(2, 1, 0).reshape(P, KC * TAPS)
    vecs = np.concatenate([cols(a["norm_mix_g"][0]), cols(a["b_gate"][0, 1]), cols(a["b_gate"][0, 0]),
                           cols(a["conv_dw_b"][0]), cols(a["conv_ln_g"][0]), cols(a["conv_ln_b"][0]),
                           cols(a["q_norm_g"][0]), cols(a["kv_norm_g"][0]), cols(a["norm_ffn_g"][0]),
                           cols(a["norm_final_g"]), dw], axis=1)
    tables = np.stack([np.ones((P, P)), np.eye(P), np.broadcast_to(np.arange(P), (P, P))], axis=1).astype(np.float32)
    freq = np.float32(THETA) ** (-np.arange(0, ROPE, 2, dtype=np.float32) / np.float32(ROPE))
    angle = freq[:, None] * np.arange(T, dtype=np.float32)[None, :]
    rotary = np.concatenate([np.cos(angle), np.cos(angle), -np.sin(angle), np.sin(angle)]).astype(np.float32)

    arrays = dict(xT=a["x"][0].T.reshape(KC, P, T).transpose(1, 0, 2), wproj=wproj, whead=np.stack(heads),
                  keysT=keysT, uT=uT, vtab=vtab, vecs=vecs, tables=tables, rotary=rotary)
    arrays = {k: np.ascontiguousarray(x) for k, x in arrays.items()}
    nc = bacc.Bacc("TRN2", target_bir_lowering=False, num_devices=1)
    args = [nc.dram_tensor(k, x.shape, mybir.dt.float32, kind="ExternalInput").ap() for k, x in arrays.items()]
    args.append(nc.dram_tensor("outT", (P, KC, T), mybir.dt.float32, kind="ExternalOutput").ap())
    build(nc, *args)
    got = run_bass_kernel_spmd(nc, [arrays], core_ids=[0]).results[0]["outT"]
    return np.ascontiguousarray(got.transpose(2, 1, 0).reshape(1, T, D))
```
